# Optimizing a Trainium2 kernel written in Bass

```python
import jax, jax.numpy as jnp
from jax import lax
import numpy as np

D_MODEL = 1024
BATCH = 1
SEQ = 128
DEPTH = 2
DEC_BATCH = 1
DEC_SEQ = 256
PAST_LEN = 128

GRID_W = 64
D_CONV = 512
CONV_K = 31
N_HEADS = 8
QK_NOPE = 64
QK_ROPE = 32
QK_DIM = QK_NOPE + QK_ROPE
V_DIM = 64
Q_LORA = 256
KV_LORA = 128
N_GROUPS = 4
EXPERTS_PER_GROUP = 4
N_EXPERTS = N_GROUPS * EXPERTS_PER_GROUP
TOP_K_IN_GROUP = 2
D_EXPERT = 256
ROPE_BASE = 10000.0
Q_BLOCK = 128
EPS = 1e-6
IN_W = 2 * D_CONV + Q_LORA + KV_LORA + QK_ROPE + 2 * D_MODEL

kernel_name = 'hybrid_conv_mla_hmoe_diffusion_step'

def rms_norm(x, g):
    xf = x.astype(jnp.float32)
    y = xf * lax.rsqrt(jnp.mean(xf * xf, axis=-1, keepdims=True) + EPS)
    return (y * g.astype(jnp.float32)).astype(x.dtype)

def layer_norm(x, g, b):
    xf = x.astype(jnp.float32)
    mu = jnp.mean(xf, axis=-1, keepdims=True)
    var = jnp.mean(jnp.square(xf - mu), axis=-1, keepdims=True)
    y = (xf - mu) * lax.rsqrt(var + EPS)
    return (y * g.astype(jnp.float32) + b.astype(jnp.float32)).astype(x.dtype)

def axial_rope(x, rows, cols):
    half = QK_ROPE // 2
    nf = half // 2
    freqs = ROPE_BASE ** (-jnp.arange(nf, dtype=jnp.float32) / nf)

    def rot(xa, pos):
        ang = pos.astype(jnp.float32)[:, None] * freqs
        cos = jnp.cos(ang)[:, None, :]
        sin = jnp.sin(ang)[:, None, :]
        xf = xa.astype(jnp.float32)
        x1, x2 = xf[..., :nf], xf[..., nf:]
        return jnp.concatenate([x1 * cos - x2 * sin, x2 * cos + x1 * sin], axis=-1)

    out = jnp.concatenate([rot(x[..., :half], rows), rot(x[..., half:], cols)], axis=-1)
    return out.astype(x.dtype)

def rope_heads(x, rows, cols):
    return jnp.concatenate([x[..., :QK_NOPE], axial_rope(x[..., QK_NOPE:], rows, cols)], axis=-1)

def adaln(c_vec, w_ada, b_ada):
    mod = jax.nn.silu(c_vec) @ w_ada + b_ada
    return jnp.split(mod[:, None, :], 6, axis=-1)

def split_projection(proj):
    i0 = 2 * D_CONV
    i1 = i0 + Q_LORA
    i2 = i1 + KV_LORA
    i3 = i2 + QK_ROPE
    return proj[..., :i0], proj[..., i0:i1], proj[..., i1:i2], proj[..., i2:i3], proj[..., i3:]

def conv_module(conv_in, w_dw, b_dw, ln_g, ln_b, w_pw2):
    a, b = jnp.split(conv_in, 2, axis=-1)
    u = a * jax.nn.sigmoid(b)
    u = lax.conv_general_dilated(
        u, w_dw[:, None, :], window_strides=(1,), padding=[(CONV_K // 2, CONV_K // 2)],
        dimension_numbers=('NWC', 'WIO', 'NWC'), feature_group_count=D_CONV) + b_dw
    u = jax.nn.silu(layer_norm(u, ln_g, ln_b))
    return u @ w_pw2

def mla_queries(q_lat, q_lora_g, w_uq, q_norm_g):
    cq = rms_norm(q_lat, q_lora_g)
    q = (cq @ w_uq).reshape(cq.shape[0], cq.shape[1], N_HEADS, QK_DIM)
    return rms_norm(q, q_norm_g)

def mla_keys_values(ckv, krope, w_ukv, k_norm_g):
    bsz, length = ckv.shape[0], ckv.shape[1]
    kv = (ckv @ w_ukv).reshape(bsz, length, N_HEADS, QK_NOPE + V_DIM)
    k_nope, v = kv[..., :QK_NOPE], kv[..., QK_NOPE:]
    k_pe = jnp.broadcast_to(krope[:, :, None, :], (bsz, length, N_HEADS, QK_ROPE))
    k = rms_norm(jnp.concatenate([k_nope, k_pe], axis=-1), k_norm_g)
    return k, v

def attend(q, k, v):
    bsz, s = q.shape[0], q.shape[1]
    nb = s // Q_BLOCK
    qb = q.reshape(bsz, nb, Q_BLOCK, N_HEADS, QK_DIM).transpose(1, 0, 2, 3, 4)
    scale = QK_DIM ** -0.5

    def block(qi):
        sc = jnp.einsum('bqhd,bkhd->bhqk', qi, k).astype(jnp.float32) * scale
        p = jax.nn.softmax(sc, axis=-1).astype(v.dtype)
        return jnp.einsum('bhqk,bkhv->bqhv', p, v)

    o = lax.map(block, qb)
    return o.transpose(1, 0, 2, 3, 4).reshape(bsz, s, N_HEADS * V_DIM)

def hier_moe(h, w_group, b_group, w_expert, b_expert, w1, w3, w2):
    bsz, s, d = h.shape
    t = h.reshape(-1, d)
    g_logits = (t @ w_group + b_group).astype(jnp.float32)
    g_prob = jax.nn.softmax(g_logits, axis=-1)
    g_idx = jnp.argmax(g_logits, axis=-1)
    g_w = jnp.take_along_axis(g_prob, g_idx[:, None], axis=-1)
    e_logits = (t @ w_expert + b_expert).astype(jnp.float32).reshape(-1, N_GROUPS, EXPERTS_PER_GROUP)
    e_sel = jnp.take_along_axis(e_logits, g_idx[:, None, None], axis=1)[:, 0]
    e_prob = jax.nn.softmax(e_sel, axis=-1)
    top_v, top_i = lax.top_k(e_prob, TOP_K_IN_GROUP)
    top_v = top_v / jnp.sum(top_v, axis=-1, keepdims=True)
    ids = g_idx[:, None] * EXPERTS_PER_GROUP + top_i
    comb = jnp.sum(jax.nn.one_hot(ids, N_EXPERTS, dtype=jnp.float32) * (g_w * top_v)[..., None], axis=1)
    hid = jax.nn.silu(jnp.einsum('td,edf->tef', t, w1)) * jnp.einsum('td,edf->tef', t, w3)
    hid = hid * comb.astype(hid.dtype)[..., None]
    y = jnp.einsum('tef,efd->td', hid, w2)
    return y.reshape(bsz, s, d)

def trunk_layer(x, c_vec, lp, ctx_cache, pos):
    shift1, scale1, gate1, shift2, scale2, gate2 = adaln(c_vec, lp['w_ada'], lp['b_ada'])
    h = rms_norm(x, lp['norm1']) * (1 + scale1) + shift1
    conv_in, q_lat, kv_lat, k_rope, gates = split_projection(h @ lp['w_in'])
    conv_out = conv_module(conv_in, lp['conv_dw'], lp['conv_dw_b'], lp['conv_ln_g'], lp['conv_ln_b'], lp['w_pw2'])
    q = mla_queries(q_lat, lp['q_lora_norm'], lp['w_uq'], lp['q_norm'])
    ckv = rms_norm(kv_lat, lp['kv_lora_norm'])
    k, v = mla_keys_values(ckv, k_rope, lp['w_ukv'], lp['k_norm'])
    if ctx_cache is not None:
        rows, cols = pos
        q = rope_heads(q, rows, cols)
        k = rope_heads(k, rows, cols)
        k_ctx, v_ctx = mla_keys_values(ctx_cache[0], ctx_cache[1], lp['w_ukv'], lp['k_norm'])
        k = jnp.concatenate([k, k_ctx], axis=1)
        v = jnp.concatenate([v, v_ctx], axis=1)
    att = attend(q, k, v) @ lp['w_o']
    g_conv, g_att = jnp.split(jax.nn.sigmoid(gates), 2, axis=-1)
    x = x + gate1 * ((g_conv * conv_out + g_att * att) @ lp['w_out'])
    h2 = rms_norm(x, lp['norm2']) * (1 + scale2) + shift2
    x = x + gate2 * hier_moe(h2, lp['w_group'], lp['b_group'], lp['w_expert'], lp['b_expert'],
                             lp['w1'], lp['w3'], lp['w2'])
    return x, ckv, k_rope

def setup_inputs(seed: int = 0) -> dict:
    key = jax.random.key(seed)
    ks = jax.random.split(key, 32)

    def nrm(k, shape, scale=1.0):
        return jax.random.normal(k, shape, dtype=jnp.float32) * scale

    L = DEPTH
    return {
        'x_prompt': nrm(ks[0], (BATCH, SEQ, D_MODEL)),
        'x_sample': nrm(ks[1], (DEC_BATCH, DEC_SEQ, D_MODEL)),
        'cache_ckv': nrm(ks[2], (DEC_BATCH, DEPTH, PAST_LEN, KV_LORA)),
        'cache_krope': nrm(ks[3], (DEC_BATCH, DEPTH, PAST_LEN, QK_ROPE)),
        'c': nrm(ks[4], (DEC_BATCH, D_MODEL)),
        'c_ctx': nrm(ks[5], (D_MODEL,)),
        'w_ada': nrm(ks[6], (L, D_MODEL, 6 * D_MODEL), 0.5 * D_MODEL ** -0.5),
        'b_ada': nrm(ks[7], (L, 6 * D_MODEL), 0.01),
        'norm1': 1.0 + nrm(ks[8], (L, D_MODEL), 0.01),
        'w_in': nrm(ks[9], (L, D_MODEL, IN_W), D_MODEL ** -0.5),
        'q_lora_norm': 1.0 + nrm(ks[10], (L, Q_LORA), 0.01),
        'w_uq': nrm(ks[11], (L, Q_LORA, N_HEADS * QK_DIM), Q_LORA ** -0.5),
        'kv_lora_norm': 1.0 + nrm(ks[12], (L, KV_LORA), 0.01),
        'w_ukv': nrm(ks[13], (L, KV_LORA, N_HEADS * (QK_NOPE + V_DIM)), KV_LORA ** -0.5),
        'q_norm': 1.0 + nrm(ks[14], (L, QK_DIM), 0.01),
        'k_norm': 1.0 + nrm(ks[15], (L, QK_DIM), 0.01),
        'w_o': nrm(ks[16], (L, N_HEADS * V_DIM, D_MODEL), (N_HEADS * V_DIM) ** -0.5),
        'conv_dw': nrm(ks[17], (L, CONV_K, D_CONV), CONV_K ** -0.5),
        'conv_dw_b': nrm(ks[18], (L, D_CONV), 0.01),
        'conv_ln_g': 1.0 + nrm(ks[19], (L, D_CONV), 0.01),
        'conv_ln_b': nrm(ks[20], (L, D_CONV), 0.01),
        'w_pw2': nrm(ks[21], (L, D_CONV, D_MODEL), D_CONV ** -0.5),
        'w_out': nrm(ks[22], (L, D_MODEL, D_MODEL), D_MODEL ** -0.5),
        'norm2': 1.0 + nrm(ks[23], (L, D_MODEL), 0.01),
        'w_group': nrm(ks[24], (L, D_MODEL, N_GROUPS), D_MODEL ** -0.5),
        'b_group': nrm(ks[25], (L, N_GROUPS), 0.01),
        'w_expert': nrm(ks[26], (L, D_MODEL, N_EXPERTS), D_MODEL ** -0.5),
        'b_expert': nrm(ks[27], (L, N_EXPERTS), 0.01),
        'w1': nrm(ks[28], (L, N_EXPERTS, D_MODEL, D_EXPERT), D_MODEL ** -0.5),
        'w3': nrm(ks[29], (L, N_EXPERTS, D_MODEL, D_EXPERT), D_MODEL ** -0.5),
        'w2': nrm(ks[30], (L, N_EXPERTS, D_EXPERT, D_MODEL), D_EXPERT ** -0.5),
    }

def reference(x_prompt, x_sample, cache_ckv, cache_krope, c, c_ctx, w_ada, b_ada, norm1, w_in,
              q_lora_norm, w_uq, kv_lora_norm, w_ukv, q_norm, k_norm, w_o, conv_dw, conv_dw_b,
              conv_ln_g, conv_ln_b, w_pw2, w_out, norm2, w_group, b_group, w_expert, b_expert,
              w1, w3, w2):
    n_lat = x_sample.shape[1]
    n_rows = n_lat // GRID_W
    rows = jnp.repeat(jnp.arange(n_rows, dtype=jnp.int32), GRID_W)
    cols = jnp.tile(jnp.arange(GRID_W, dtype=jnp.int32), n_rows)
    c_ctx_vec = c_ctx[None, :]

    xp, xs = x_prompt, x_sample
    ckv_list, krope_list = [], []
    for l in range(DEPTH):
        lp = {
            'w_ada': w_ada[l], 'b_ada': b_ada[l], 'norm1': norm1[l], 'w_in': w_in[l],
            'q_lora_norm': q_lora_norm[l], 'w_uq': w_uq[l], 'kv_lora_norm': kv_lora_norm[l],
            'w_ukv': w_ukv[l], 'q_norm': q_norm[l], 'k_norm': k_norm[l], 'w_o': w_o[l],
            'conv_dw': conv_dw[l], 'conv_dw_b': conv_dw_b[l], 'conv_ln_g': conv_ln_g[l],
            'conv_ln_b': conv_ln_b[l], 'w_pw2': w_pw2[l], 'w_out': w_out[l], 'norm2': norm2[l],
            'w_group': w_group[l], 'b_group': b_group[l], 'w_expert': w_expert[l],
            'b_expert': b_expert[l], 'w1': w1[l], 'w3': w3[l], 'w2': w2[l],
        }
        xp, ckv_l, krope_l = trunk_layer(xp, c_ctx_vec, lp, None, None)
        ckv_list.append(ckv_l)
        krope_list.append(krope_l)
        xs, _, _ = trunk_layer(xs, c, lp, (cache_ckv[:, l], cache_krope[:, l]), (rows, cols))
    new_ckv = jnp.stack(ckv_list, axis=1)
    new_krope = jnp.stack(krope_list, axis=1)
    return (xp, xs, new_ckv, new_krope)


_drawn_inputs = setup_inputs


def setup_inputs(seed=0):
    import zlib

    import numpy as np

    out = dict(_drawn_inputs(seed))
    spreads = {}
    factors = {'cache_ckv': 4.982,
     'cache_krope': 8.0,
     'b_ada': 4.073,
     'norm1': 5.854,
     'q_lora_norm': 8.0,
     'kv_lora_norm': 5.912,
     'q_norm': 8.0,
     'k_norm': 8.0,
     'conv_dw_b': 8.0,
     'conv_ln_g': 8.0,
     'conv_ln_b': 8.0,
     'norm2': 5.724,
     'b_group': 8.0,
     'b_expert': 6.672}
    for name, (base, spread) in spreads.items():
        noise = np.random.default_rng([zlib.crc32(name.encode()), seed]).standard_normal(out[name].shape)
        drawn = base * np.exp(spread * noise) if base else spread * noise
        out[name] = __import__('jax').numpy.asarray(drawn.astype(out[name].dtype))
    for name, factor in factors.items():
        out[name] = (out[name] * factor).astype(out[name].dtype)
    return out
```

```python
from contextlib import ExitStack

import numpy as np

import concourse.bass as bass
from concourse import mybir

F32 = mybir.dt.float32
I32 = mybir.dt.int32
ALU = mybir.AluOpType
ACT = mybir.ActivationFunctionType
AX_X = mybir.AxisListType.X

P = 128
LAYERS = 2
D = 1024
KD = D // P
CTX, LAT, PAST = 128, 256, 128
TOK = CTX + LAT
TT = TOK // P
KEYS = TOK + PAST
KT = KEYS // P
GRID_W = 64
DC = 512
KC = DC // P
TAPS = 31
HALF = TAPS // 2
H, NOPE, ROPE, VD = 8, 64, 32, 64
QK = NOPE + ROPE
NF = ROPE // 4
QL, KVL = 256, 128
GROUPS, EPG = 4, 4
EXPERTS = GROUPS * EPG
FE = 256
EPS = 1e-6

U_CTX = HALF
U_LAT = HALF + CTX + HALF
U_W = U_LAT + LAT + HALF
Z_W = U_W - 2 * HALF
Z_LAT = CTX + HALF

UNIT = 2048
SLOTS = 6
ADA_UNITS = 6 * D * KD // UNIT
PRE_UNITS = 24
MOE_UNITS = 3 * EXPERTS
LAYER_UNITS = ADA_UNITS + PRE_UNITS + MOE_UNITS
ADA_TURNS = ADA_UNITS // SLOTS
PRE_TURNS = PRE_UNITS // SLOTS
GROUP_UNITS = 3 * EPG
GROUP_TURNS = GROUP_UNITS // SLOTS

_FIELDS = [("b_ada", 48), ("norm1", KD), ("norm2", KD), ("dw", KC * TAPS), ("dw_b", KC), ("ln_g", KC),
           ("ln_b", KC), ("q_lora", QL // P), ("kv_lora", 1), ("q_norm", QK), ("k_norm", QK),
           ("route_b", GROUPS + EXPERTS), ("route_w", KD * (GROUPS + EXPERTS)),
           ("cache_ckv", PAST), ("cache_kr", ROPE)]
FIELD = {}
NPAR = 0
for _n, _w in _FIELDS:
    FIELD[_n] = (NPAR, NPAR + _w)
    NPAR += _w
NR = GROUPS + EXPERTS

C_ID, C_ONE, C_TRI, C_SLOT, C_SEL, C_ROPE, C_ORD = 0, 128, 256, 384, 512, 514, 514 + 64
NCONST = C_ORD + 4


def pre_jobs():
    jobs = []

    def add(name, index, taker, bank=None):
        if bank is None:
            bank = add.next
            add.next = (add.next + 1) % add.banks
        jobs.append((name, index, bank, taker))

    add.next, add.banks = 0, 8
    add("ss", 0, "act")
    for t in range(TT):
        add("lat", t, "dve")
    for c in range(KC):
        add("glu_a", c, "dve")
        add("glu_b", c, "act")
    for c in range(3):
        add("latT", c, "dve")
    for j in range(2 * TT):
        add("q", j, "act")
    for t in range(KT):
        add("k", t, "act")
        add("v", t, "act")
    for c in range(KD):
        add("gate", c, "act")
    for h in range(H):
        add("qT", h, "act")
    for h in range(H):
        add("kT", h, "act")
    for c in range(KD, 2 * KD):
        add("gate", c, "act")
    add.next, add.banks = 0, 5
    add("mean", 0, "dve")
    for i in range(H * TT + 2):
        if i < H * TT:
            add("s", i, "act")
        if i >= 2:
            add("pT", i - 2, "dve" if i % 2 == 0 else "act")
        if i == 12:
            add("var", 0, "act")
    for t in range(TT):
        add("o", t, "dve", 5 + t)
    add.next, add.banks = 0, 8
    for c in range(4):
        add("oT", c, "act")
    for name in ("pw2", "wo", "wout"):
        for c in range(KD):
            add(name, c, "dve")
    add("ss", 1, "act")
    add("logit", 0, "dve")
    for j in range(2 * TT):
        add("hrow", j, "act")
    add("rank", 0, "dve")
    return jobs


JOBS = pre_jobs()
JOB = {(n, i): k for k, (n, i, _, _) in enumerate(JOBS)}
FULL_JOBS = [j for j in JOBS if j[0] != "o"]
FULL = {(n, i): k for k, (n, i, _, _) in enumerate(FULL_JOBS)}
TAKEN = {}
for _who in ("act", "dve"):
    for _k, (_n, _i, _, _) in enumerate([j for j in JOBS if j[3] == _who]):
        TAKEN[(_n, _i)] = (_who, _k)
N_TAKEN = {who: sum(j[3] == who for j in JOBS) for who in ("act", "dve")}


def build(nc, wstream, x0, cond, par_in, const_in, x_out, ckv_out, kr_out):
    ctx = ExitStack()
    with ctx:
        def sb(name, shape, dt=F32):
            return ctx.enter_context(nc.sbuf_tensor(name, shape, dt))

        def sem(name):
            return ctx.enter_context(nc.semaphore(name))

        ring = sb("ring", [P, SLOTS * UNIT])
        x = sb("x", [P, KD, TOK])
        h = sb("h", [P, KD, TOK])
        u = sb("u", [P, KC, U_W])
        z = sb("z", [P, KC, Z_W])
        gates = sb("gates", [P, 2 * KD, TOK])
        par_all = sb("par_all", [P, LAYERS, NPAR])
        par = sb("par", [P, NPAR])
        const = sb("const", [P, NCONST])
        cond_sb = sb("cond_sb", [P, KD, 2])
        condp = sb("condp", [P, KD, 32])
        ada_rows = sb("ada_rows", [P, 2, 256])
        mod_all = sb("mod_all", [P, LAYERS, 48, 2])
        mod = sb("mod", [P, 48, 2])
        amp = sb("amp", [P, 2, KD, 2])
        rs = sb("rs", [P, Z_W])
        cq = sb("cq", [P, TT, QL])
        ckv = sb("ckv", [P, TT, KVL])
        kr = sb("kr", [P, KT, ROPE])
        cqT = sb("cqT", [P, 2, TOK])
        ckvT = sb("ckvT", [P, KEYS])
        q = sb("q", [P, TT, H, QK])
        kv_o = sb("kv_o", [P, KT * H * QK])
        k = kv_o[:, :].rearrange("p (t h d) -> p t h d", t=KT, h=H)
        o = kv_o[:, 0:TT * DC].rearrange("p (t n) -> p t n", t=TT)
        oT = kv_o[:, TT * DC:2 * TT * DC].rearrange("p (c n) -> p c n", c=4)
        v = sb("v", [P, KT, H * VD])
        qT = sb("qT", [P, H, TOK])
        kT_h = sb("kT_h", [P, H * KEYS])
        kT = kT_h[:, :].rearrange("p (h n) -> p h n", h=H)
        hrow = kT_h[:, 0:TT * D].rearrange("p (t n) -> p t n", t=TT)
        cT = q[:, :, :, :].rearrange("p t h d -> p (t h d)")[:, 0:KC * TOK].rearrange("p (c n) -> p c n", c=KC)
        probs = sb("probs", [P, 3, TOK])
        probsT = sb("probsT", [P, 2, TOK])
        scratch = sb("scratch", [P, 2, 512])
        sig = probsT
        small = sb("small", [P, 512])
        eps = sb("eps", [P, 2])
        rounds = sb("rounds", [1, LAYERS], I32)
        before = sb("before", [1, LAYERS + 1], I32)

        at = [0]

        def sm(n):
            at[0] += n
            return small[:, at[0] - n:at[0]]

        lat_ss = sm(6)
        kr_ss = sm(KT)
        lat_r = sm(6)
        head_ss = sm(32)
        head_r = sm(32)
        row_max = sm(H * TT)
        row_sum = sm(H * TT)
        lg = sm(TT * NR).rearrange("p (t n) -> p t n", t=TT)
        best = sm(TT)
        tie = sm(TT * 4).rearrange("p (t n) -> p t n", t=TT)
        low = sm(TT)
        oh_g = sm(TT * 4).rearrange("p (t n) -> p t n", t=TT)
        oh_1 = sm(TT * 4).rearrange("p (t n) -> p t n", t=TT)
        oh_2 = sm(TT * 4).rearrange("p (t n) -> p t n", t=TT)
        ex = sm(TT * 5).rearrange("p (t n) -> p t n", t=TT)
        e_own = sm(TT * 4).rearrange("p (t n) -> p t n", t=TT)
        e_rest = sm(TT * 4).rearrange("p (t n) -> p t n", t=TT)
        m1 = sm(TT)
        m2 = sm(TT)
        gw = sm(TT)
        dn = sm(TT)
        v1 = sm(TT)
        v2 = sm(TT)
        cw = sm(TT * 4).rearrange("p (t n) -> p t n", t=TT)
        cw2 = sm(TT * 4).rearrange("p (t n) -> p t n", t=TT)
        pos = sm(TT)
        most = sm(4)
        tmp16 = scratch[:, 0, 0:TT * 16]
        gflat = gates[:, :, :].rearrange("p c n -> p (c n)")
        gat = [0]

        def gm(n):
            gat[0] += n
            return gflat[:, gat[0] - n:gat[0]]

        pick = gm(TT * P).rearrange("p (t n) -> p t n", t=TT)
        pickT = gm(TOK)
        hg = gm(KD * P).rearrange("p (c n) -> p c n", c=KD)
        cwg = gm(4)
        gm(4)
        hs = gm(2 * FE).rearrange("p (s n) -> p s n", s=2)
        hm = gm(2 * FE).rearrange("p (s n) -> p s n", s=2)
        hT = gm(2 * FE).rearrange("p (s c n) -> p s c n", s=2, c=2)
        y_sb = gm(D)
        unused = gflat[:, 0:4 * 416].rearrange("p (t n) -> p t n", t=4)

        ps = ctx.enter_context(nc.psum_tensor("ps", [P, 8, 512], F32))

        ident = const[:, C_ID:C_ID + P]
        ones = const[:, C_ONE:C_ONE + P]
        tri = const[:, C_TRI:C_TRI + P]
        slot_no = const[:, C_SLOT:C_SLOT + P]
        sel = const[:, C_SEL:C_SEL + 2]
        rope = const[:, C_ROPE:C_ROPE + 64].rearrange("p (t s a f) -> p t s a f", t=2, s=2, a=2)
        order4 = const[:, C_ORD:C_ORD + 4]

        def pf(name):
            a, b = FIELD[name]
            return par[:, a:b]

        route_w = pf("route_w").rearrange("p (c n) -> p c n", c=KD)
        dw = pf("dw").rearrange("p (c n) -> p c n", c=KC)

        def slot(s, n=1):
            return ring[:, s * UNIT:(s + n) * UNIT]

        loaded = sem("loaded")
        w_landed = [sem(f"w_landed{s}") for s in range(SLOTS)]
        w_free = [sem(f"w_free{s}") for s in range(SLOTS)]
        set_up = sem("set_up")
        settled = sem("settled")
        cond_ready = sem("cond_ready")
        condp_ready = sem("condp_ready")
        ada_full = sem("ada_full")
        ada_taken = sem("ada_taken")
        adaT_full = sem("adaT_full")
        adaT_taken = sem("adaT_taken")
        layer_set = sem("layer_set")
        psum_full = sem("psum_full")
        taken = {"act": sem("psum_taken_by_act"), "dve": sem("psum_taken_by_dve")}
        sq_ready = sem("sq_ready")
        xn_ready = sem("xn_ready")
        h_ready = sem("h_ready")
        lat_rms = sem("lat_rms")
        squared = sem("squared")
        sq_summed = sem("sq_summed")
        head_summed = sem("head_summed")
        head_rooted = sem("head_rooted")
        qk_ready = sem("qk_ready")
        conv_done = sem("conv_done")
        z_squared = sem("z_squared")
        z_normed = sem("z_normed")
        conv_act = sem("conv_act")
        max_ready = sem("max_ready")
        pv_done = sem("pv_done")
        merged = sem("merged")
        ex_in = sem("ex_in")
        ex_out = sem("ex_out")
        onehot_ready = sem("onehot_ready")
        routed = sem("routed")
        ckv_ready = sem("ckv_ready")
        ckv_stored = sem("ckv_stored")
        pick_ready = sem("pick_ready")
        pickT_full = sem("pickT_full")
        pickT_taken = sem("pickT_taken")
        hg_full = sem("hg_full")
        hg_act = sem("hg_act")
        hg_dve = sem("hg_dve")
        hid_full = sem("hid_full")
        silu_done = sem("silu_done")
        hm_ready = sem("hm_ready")
        hT_full = sem("hT_full")
        hT_taken = sem("hT_taken")
        w2_done = sem("w2_done")
        y_act = sem("y_act")
        y_dve = sem("y_dve")
        back_full = sem("back_full")
        x_moe = sem("x_moe")
        x_stored = sem("x_stored")
        act_order = sem("act_order")
        dve_order = sem("dve_order")

        def pre_use(l, done, turn):
            return l * PRE_TURNS + done * GROUP_TURNS + (LAYERS * ADA_TURNS + turn)

        def moe_use(l, rounds_done, turn):
            return l * PRE_TURNS + rounds_done * GROUP_TURNS + (LAYERS * ADA_TURNS + PRE_TURNS + turn)

        def settle(eng):
            eng.sem_inc(settled, 1)

        def rounds_before(eng, l):
            settle(eng)
            return eng.value_load(before[0:1, bass.ts(l, 1)], min_val=0, max_val=3 * GROUPS * LAYERS)

        def passes(eng, l):
            settle(eng)
            return eng.value_load(rounds[0:1, bass.ts(l, 1)], min_val=1, max_val=3)

        def wait_full(eng, l, name, index=0):
            eng.wait_ge(psum_full, l * len(FULL_JOBS) + (FULL[(name, index)] + 1))

        def wait_taken(eng, l, name, index=0):
            who, n = TAKEN[(name, index)]
            eng.wait_ge(taken[who], l * N_TAKEN[who] + (n + 1))

        def ps_of(name, index=0):
            return ps[:, JOBS[JOB[(name, index)]][2], :]

        block = ctx.enter_context(nc.Block())

        @block.sync
        def _(sp):
            sp.dma_start(cond_sb[:, :, :], cond).then_inc(loaded, 16)
            sp.dma_start(const[:, :], const_in).then_inc(loaded, 16)
            sp.dma_start(par_all[:, :, :], par_in).then_inc(loaded, 16)
            sp.dma_start(x[:, :, :], x0).then_inc(loaded, 16)
            with sp.Fori(0, LAYERS) as l:
                with sp.Fori(0, ADA_TURNS) as r:
                    use = sp.snap(l * ADA_TURNS + r)
                    for s in range(SLOTS):
                        sp.wait_ge(w_free[s], use + 1)
                        sp.dma_start(slot(s), wstream[l, r, s]).then_inc(w_landed[s], 16)
            sp.wait_ge(set_up, 1)
            with sp.Fori(0, LAYERS) as l:
                done = rounds_before(sp, l)
                with sp.Fori(0, PRE_TURNS) as r:
                    use = sp.snap(pre_use(l, done, r))
                    for s in range(SLOTS):
                        sp.wait_ge(w_free[s], use + 1)
                        sp.dma_start(slot(s), wstream[l, r + ADA_TURNS, s]).then_inc(w_landed[s], 16)

                def experts(first):
                    with sp.Fori(0, GROUPS) as g:
                        for turn in range(GROUP_TURNS):
                            use = sp.snap(moe_use(l, first + g, turn))
                            for s in range(SLOTS):
                                sp.wait_ge(w_free[s], use + 1)
                                sp.dma_start(slot(s), wstream[l, g * GROUP_TURNS + (ADA_TURNS + PRE_TURNS + turn), s]
                                             ).then_inc(w_landed[s], 16)

                experts(done)
                sp.wait_ge(routed, l + 1)
                n = passes(sp, l)
                with sp.If(n > 1):
                    with sp.Fori(1, n) as p:
                        experts(done + p * GROUPS)
                with sp.Else():
                    pass
            total = rounds_before(sp, LAYERS)
            sp.wait_ge(x_moe, total * KD + 1)
            sp.dma_start(x_out, x[:, :, :]).then_inc(x_stored, 16)
            sp.wait_ge(x_stored, 16)
            sp.wait_ge(ckv_stored, 32 * LAYERS)

        @block.gpsimd
        def _(pool):
            with pool.Fori(0, LAYERS) as l:
                pool.wait_ge(ckv_ready, l + 1)
                pool.dma_start(ckv_out[l], ckvT[:, 0:CTX]).then_inc(ckv_stored, 16)
                pool.dma_start(kr_out[l], kr[:, 0, :]).then_inc(ckv_stored, 16)

        @block.tensor
        def _(pe):
            mm = nc.tensor.matmul
            held = []

            def first(ins):
                if held:
                    ins.then_inc(held.pop(0), 1)
                return ins

            pe.wait_ge(loaded, 64)
            for s in range(SLOTS):
                pe.sem_inc(w_free[s], 1)
            pe.wait_ge(condp_ready, 1)
            with pe.Fori(0, LAYERS) as l:
                with pe.Fori(0, ADA_TURNS) as r:
                    use = pe.snap(l * ADA_TURNS + r)

                    def rows(s):
                        w = slot(s).rearrange("p (c n) -> p c n", c=KD)
                        pe.wait_ge(w_landed[s], use * 16 + 16)
                        if s >= 2:
                            pe.wait_ge(ada_taken, use * SLOTS + (s - 1))
                        for c in range(2):
                            for j in range(4):
                                m = mm(ps[32 * j:32 * j + 32, s % 2, 0:256], condp[:, 2 * j + c, :],
                                       w[:, 2 * j + c, :], start=(c == 0), stop=(c == 1))
                        m.then_inc(ada_full, 1)

                    def columns(s):
                        pe.wait_ge(ada_taken, use * SLOTS + (s + 1))
                        if s >= 2:
                            pe.wait_ge(adaT_taken, use * SLOTS + (s - 1))
                        m = mm(ps[:, 2 + s % 2, 0:2], ada_rows[:, s % 2, 0:P], sel, start=True, stop=True)
                        m.then_inc(w_free[s], 1)
                        m = mm(ps[:, 2 + s % 2, 2:4], ada_rows[:, s % 2, P:256], sel, start=True, stop=True)
                        m.then_inc(adaT_full, 1)

                    for s in range(SLOTS):
                        rows(s)
                        if s:
                            columns(s - 1)
                    columns(SLOTS - 1)

            with pe.Fori(0, LAYERS) as l:
                done = rounds_before(pe, l)
                base16 = pe.snap(pre_use(l, done, 0) * 16)
                unit = [0]

                def next_unit():
                    n = unit[0]
                    unit[0] += 1
                    pe.wait_ge(w_landed[n % SLOTS], base16 + 16 * (n // SLOTS + 1))
                    return slot(n % SLOTS), w_free[n % SLOTS]

                def begin(name, index=0):
                    j = JOB[(name, index)]
                    bank = JOBS[j][2]
                    for n, i, b, _ in reversed(JOBS[:j]):
                        if b == bank:
                            wait_taken(pe, l, n, i)
                            break
                    return ps[:, bank, :]

                def product(out, lhs, rhs):
                    n = len(lhs)
                    for i in range(n):
                        m = mm(out, lhs[i], rhs[i], start=(i == 0), stop=(i == n - 1))
                        if i == 0 and n > 1:
                            first(m)
                    return m

                def square_sum(which):
                    out = begin("ss", which)
                    for c in range(KD):
                        pe.wait_ge(sq_ready, l * 2 * KD + (which * KD + c + 1))
                        m = mm(out[:, 0:TOK], ones, h[:, c, :], start=(c == 0), stop=(c == KD - 1))
                        if c == 0:
                            first(m)
                    m.then_inc(psum_full, 1)

                square_sum(0)
                wq, free_q = next_unit()
                wk, free_k = next_unit()
                wq = wq.rearrange("p (c n) -> p c n", c=KD)
                wk = wk.rearrange("p (c n) -> p c n", c=KD)
                for t in range(TT):
                    out = begin("lat", t)
                    if t == 0:
                        pe.wait_ge(h_ready, l * 2 * KD + KD)
                    hs_t = [h[:, c, t * P:(t + 1) * P] for c in range(KD)]
                    product(out[:, 0:QL], hs_t, [wq[:, c, :] for c in range(KD)])
                    product(out[:, QL:QL + KVL + ROPE], hs_t, [wk[:, c, 0:KVL + ROPE] for c in range(KD)]
                            ).then_inc(psum_full, 1)
                held.extend([free_q])
                held2 = free_k
                for c in range(KC):
                    w, free = next_unit()
                    w = w.rearrange("p (c n) -> p c n", c=KD)
                    for half, name in enumerate(("glu_a", "glu_b")):
                        out = begin(name, c)
                        product(out[:, 0:TOK], [w[:, d, half * P:(half + 1) * P] for d in range(KD)],
                                [h[:, d, :] for d in range(KD)]).then_inc(psum_full, 1)
                        if held2 is not None:
                            held.append(held2)
                            held2 = None
                    held.append(free)
                for c in range(3):
                    out = begin("latT", c)
                    for t in range(TT):
                        if c == 0:
                            wait_taken(pe, l, "lat", t)
                        src = cq[:, t, c * P:(c + 1) * P] if c < 2 else ckv[:, t, :]
                        m = nc.tensor.transpose(out[:, t * P:(t + 1) * P], src, ident)
                        if t == 0:
                            first(m)
                    m.then_inc(psum_full, 1)
                w, free = next_unit()
                for j in range(2 * TT):
                    t, half = divmod(j, 2)
                    out = begin("q", j)
                    if j == 0:
                        wait_taken(pe, l, "latT", 1)
                    n = H * QK // 2
                    product(out[:, 0:n], [cqT[:, c, t * P:(t + 1) * P] for c in range(2)],
                            [w[:, c * H * QK + half * n:c * H * QK + (half + 1) * n] for c in range(2)]
                            ).then_inc(psum_full, 1)
                held.append(free)
                w, free = next_unit()
                for t in range(KT):
                    for half, name in enumerate(("k", "v")):
                        out = begin(name, t)
                        if t == 0 and half == 0:
                            wait_taken(pe, l, "latT", 2)
                        product(out[:, 0:512], [ckvT[:, t * P:(t + 1) * P]], [w[:, half * 512:(half + 1) * 512]]
                                ).then_inc(psum_full, 1)
                held.append(free)

                def gate(c0):
                    for c in range(c0, c0 + KD, 2):
                        w, free = next_unit()
                        w = w.rearrange("p (c n) -> p c n", c=KD)
                        for half in range(2):
                            out = begin("gate", c + half)
                            product(out[:, 0:TOK], [w[:, d, half * P:(half + 1) * P] for d in range(KD)],
                                    [h[:, d, :] for d in range(KD)]).then_inc(psum_full, 1)
                        held.append(free)

                gate(0)
                for n, (name, tiles) in enumerate((("qT", TT), ("kT", KT))):
                    pe.wait_ge(qk_ready, l * 2 + (n + 1))
                    for hd in range(H):
                        out = begin(name, hd)
                        for t in range(tiles):
                            src = q[:, t, hd, :] if n == 0 else k[:, t, hd, :]
                            m = nc.tensor.transpose(out[0:QK, t * P:(t + 1) * P], src, ident)
                            if t == 0:
                                first(m)
                        m.then_inc(psum_full, 1)
                gate(KD)

                out = begin("mean")
                pe.wait_ge(conv_done, l + 1)
                product(out[:, 0:Z_W], [ones] * KC, [z[:, c, :] for c in range(KC)]).then_inc(psum_full, 1)

                def scores(i):
                    hd, t = divmod(i, TT)
                    out = begin("s", i)
                    if i == 0:
                        wait_taken(pe, l, "kT", H - 1)
                    keys = kT[0:QK, hd, 0:CTX] if t == 0 else kT[0:QK, hd, CTX:KEYS]
                    n = CTX if t == 0 else LAT + PAST
                    product(out[:, 0:n], [qT[0:QK, hd, t * P:(t + 1) * P]], [keys]).then_inc(psum_full, 1)

                def weigh(i):
                    hd, t = divmod(i, TT)
                    n = 1 if t == 0 else KT - 1
                    out = begin("pT", i)
                    wait_taken(pe, l, "s", i)
                    for b in range(n):
                        m = nc.tensor.transpose(out[:, b * P:(b + 1) * P], probs[:, i % 3, b * P:(b + 1) * P], ident)
                    m.then_inc(psum_full, 1)
                    return hd, t, n

                def attend(i, hd, t, n):
                    wait_taken(pe, l, "pT", i)
                    k0 = 0 if t == 0 else 1
                    o_ps = ps[:, 5 + t, hd * VD:(hd + 1) * VD]
                    for b in range(n):
                        m = mm(o_ps, probsT[:, i % 2, b * P:(b + 1) * P], v[:, k0 + b, hd * VD:(hd + 1) * VD],
                               start=(b == 0), stop=(b == n - 1))
                    m.then_inc(pv_done, 1)

                for t in range(TT):
                    begin("o", t)
                last = None
                for i in range(H * TT + 2):
                    if i < H * TT:
                        scores(i)
                    if i >= 2:
                        turned = weigh(i - 2)
                        if last is not None:
                            attend(i - 3, *last)
                        last = turned
                    if i == 12:
                        out = begin("var")
                        pe.wait_ge(z_squared, l + 1)
                        product(out[:, 0:Z_W], [ones] * KC, [u[:, c, HALF:HALF + Z_W] for c in range(KC)]
                                ).then_inc(psum_full, 1)
                attend(H * TT - 1, *last)

                def widen(name, lhs_chunks, rhs, wait):
                    for unit_no in range(2):
                        w, free = next_unit()
                        w = w.rearrange("p (c n) -> p c n", c=4)
                        for c4 in range(4):
                            c = unit_no * 4 + c4
                            out = begin(name, c)
                            if c == 0:
                                wait()
                            product(out[:, 0:TOK], [w[:, d, c4 * P:(c4 + 1) * P] for d in range(4)],
                                    [rhs[:, d, :] for d in range(4)]).then_inc(psum_full, 1)
                        held.append(free)

                def turn_o():
                    for c in range(4):
                        out = begin("oT", c)
                        for t in range(TT):
                            if c == 0:
                                wait_taken(pe, l, "o", t)
                            m = nc.tensor.transpose(out[:, t * P:(t + 1) * P], o[:, t, c * P:(c + 1) * P], ident)
                            if t == 0:
                                first(m)
                        m.then_inc(psum_full, 1)

                turn_o()
                widen("pw2", 4, cT, lambda: pe.wait_ge(conv_act, l + 1))
                widen("wo", 4, oT, lambda: wait_taken(pe, l, "oT", 3))
                for c in range(0, KD, 2):
                    w, free = next_unit()
                    w = w.rearrange("p (c n) -> p c n", c=KD)
                    for half in range(2):
                        out = begin("wout", c + half)
                        if c + half == 0:
                            pe.wait_ge(merged, l * KD + KD)
                        product(out[:, 0:TOK], [w[:, d, half * P:(half + 1) * P] for d in range(KD)],
                                [gates[:, d, :] for d in range(KD)]).then_inc(psum_full, 1)
                    held.append(free)
                square_sum(1)
                out = begin("logit")
                pe.wait_ge(h_ready, l * 2 * KD + 2 * KD)
                for t in range(TT):
                    m = product(out[:, t * NR:(t + 1) * NR], [h[:, c, t * P:(t + 1) * P] for c in range(KD)],
                                [route_w[:, c, :] for c in range(KD)])
                m.then_inc(psum_full, 1)
                for j in range(2 * TT):
                    t, half = divmod(j, 2)
                    out = begin("hrow", j)
                    for b in range(4):
                        m = nc.tensor.transpose(out[:, b * P:(b + 1) * P],
                                                h[:, half * 4 + b, t * P:(t + 1) * P], ident)
                        if b == 0:
                            first(m)
                    m.then_inc(psum_full, 1)
                out = begin("rank")
                pe.wait_ge(onehot_ready, l + 1)
                for t in range(TT + 1):
                    n = min(t + 1, TT)
                    m = product(out[:, t * 4:t * 4 + 4], [tri if j == t else ones for j in range(n)],
                                [oh_g[:, j, :] for j in range(n)])
                m.then_inc(psum_full, 1)

                pe.wait_ge(routed, l + 1)
                n = passes(pe, l)
                wait_taken(pe, l, "hrow", 2 * TT - 1)
                settle(pe)
                with pe.Fori(0, n) as p:
                    with pe.Fori(0, GROUPS) as g:
                        i = pe.snap(done + p * GROUPS + g)
                        land = pe.snap(moe_use(l, i, 0) * 16)
                        pe.wait_ge(x_moe, i * KD + 1)
                        pe.wait_ge(pick_ready, i + 1)
                        for t in range(TT):
                            m = nc.tensor.transpose(ps[:, 6, t * P:(t + 1) * P], pick[:, t, :], ident)
                        m.then_inc(pickT_full, 1)
                        for c in range(KD):
                            m = product(ps[:, 4 + c // 4, (c % 4) * P:(c % 4 + 1) * P],
                                        [hrow[:, t, c * P:(c + 1) * P] for t in range(TT)],
                                        [pick[:, t, :] for t in range(TT)])
                            if c % 4 == 3:
                                m.then_inc(hg_full, 1)
                        product(ps[:, 7, 0:4], [pick[:, t, :] for t in range(TT)],
                                [cw[:, t, :] for t in range(TT)]).then_inc(hg_full, 1)

                        def up(e):
                            a = 3 * (e % 2)
                            w = slot(a, 2).rearrange("p (c n) -> p c n", c=KD)
                            pe.wait_ge(w_landed[a], land + 16 * (e // 2 + 1))
                            if e == 0:
                                pe.wait_ge(hg_dve, i * 2 + 2)
                                pe.wait_ge(hg_act, i + 1)
                            if e >= 2:
                                pe.wait_ge(hm_ready, i * EPG + (e - 1))
                            for c in range(KD):
                                if c == KD // 2:
                                    pe.wait_ge(w_landed[a + 1], land + 16 * (e // 2 + 1))
                                m = mm(ps[:, 2 + e % 2, :], hg[:, c, :], w[:, c, :], start=(c == 0), stop=(c == KD - 1))
                                if c == 0:
                                    first(m)
                                if c == KD // 2:
                                    m.then_inc(w_free[a], 1)
                            m.then_inc(hid_full, 1)
                            held.append(w_free[a + 1])

                        def turn(e):
                            pe.wait_ge(hm_ready, i * EPG + (e + 1))
                            if e < 2:
                                pe.wait_ge(pickT_taken, i + 1)
                            else:
                                pe.wait_ge(hT_taken, i * EPG + (e - 1))
                            for b in range(2):
                                m = nc.tensor.transpose(ps[:, 6 + e % 2, b * P:(b + 1) * P],
                                                        hm[:, e % 2, b * P:(b + 1) * P], ident)
                                if b == 0:
                                    first(m)
                            m.then_inc(hT_full, 1)

                        def down(e):
                            a = 3 * (e % 2) + 2
                            w = slot(a).rearrange("p (c n) -> p c n", c=2)
                            pe.wait_ge(w_landed[a], land + 16 * (e // 2 + 1))
                            pe.wait_ge(hT_taken, i * EPG + (e + 1))
                            for half in range(2):
                                for b in range(2):
                                    m = mm(ps[:, half, :], hT[:, e % 2, b, :], w[:, b, half * 512:(half + 1) * 512],
                                           start=(e == 0 and b == 0), stop=(e == EPG - 1 and b == 1))
                            m.then_inc(w2_done, 1)
                            held.append(w_free[a])

                        up(0)
                        for e in range(EPG):
                            if e + 1 < EPG:
                                up(e + 1)
                            turn(e)
                            down(e)
                        pe.wait_ge(y_dve, i + 1)
                        pe.wait_ge(y_act, i + 1)
                        for c in range(KD):
                            bank = (4, 5, 6, 7, 2, 3, 4, 5)[c]
                            if c == 2:
                                pe.wait_ge(hT_taken, i * EPG + EPG)
                            if c >= 6:
                                pe.wait_ge(x_moe, i * KD + (c - 4))
                            m = mm(ps[:, bank, 0:TOK], y_sb[:, c * P:(c + 1) * P], pickT, start=True, stop=True)
                            m.then_inc(back_full, 1)
                        tail = mm(ps[:, 0, 0:4], ident, ident[:, 0:4], start=True, stop=True)
                        first(tail)

        @block.scalar
        def _(act):
            af = nc.scalar.activation
            count = [0]

            def chain(ins):
                count[0] += 1
                ins.then_inc(act_order, 1)
                act.wait_ge(act_order, count[0])

            def rewind():
                if count[0]:
                    act.sem_clear(act_order)
                    count[0] = 0

            act.wait_ge(loaded, 64)
            af(cond_sb[:, :, :], cond_sb[:, :, :], ACT.Silu).then_inc(cond_ready, 1)
            act.wait_ge(set_up, 1)

            with act.Fori(0, LAYERS) as l:
                done = rounds_before(act, l)
                act.wait_ge(layer_set, l + 1)

                def norm(which):
                    for c in range(KD):
                        if which == 0:
                            if c == 0:
                                act.wait_ge(x_moe, done * KD + 1)
                        else:
                            wait_taken(act, l, "wout", c)
                        af(h[:, c, :], x[:, c, :], ACT.Square).then_inc(sq_ready, 1)
                    wait_full(act, l, "ss", which)
                    af(rs[:, 0:TOK], ps_of("ss", which)[:, 0:TOK], ACT.Sqrt, bias=eps[:, 0:1],
                       scale=1.0 / D).then_inc(taken["act"], 1)
                    for c in range(KD):
                        act.wait_ge(xn_ready, l * 2 * KD + (which * KD + c + 1))
                        for st, (a, b) in enumerate(((0, CTX), (CTX, TOK))):
                            m = af(h[:, c, a:b], h[:, c, a:b], ACT.Identity, scale=amp[:, which, c, st:st + 1],
                                   bias=mod[:, 24 * which + c, st:st + 1])
                        m.then_inc(h_ready, 1)

                norm(0)
                for t in range(TT):
                    wait_full(act, l, "lat", t)
                    src = ps_of("lat", t)
                    for n, (a, b) in enumerate(((0, QL), (QL, QL + KVL), (QL + KVL, QL + KVL + ROPE))):
                        dst = lat_ss[:, n * 3 + t:n * 3 + t + 1] if n < 2 else kr_ss[:, t:t + 1]
                        af(unused[:, t, a:b], src[:, a:b], ACT.Square, accum_out=dst)
                chain(af(unused[:, TT, 0:ROPE], pf("cache_kr"), ACT.Square, accum_out=kr_ss[:, TT:TT + 1]))
                af(lat_r[:, 0:3], lat_ss[:, 0:3], ACT.Sqrt, bias=eps[:, 0:1], scale=1.0 / QL)
                af(lat_r[:, 3:6], lat_ss[:, 3:6], ACT.Sqrt, bias=eps[:, 0:1], scale=1.0 / KVL).then_inc(lat_rms, 1)
                for c in range(KC):
                    wait_full(act, l, "glu_b", c)
                    if c >= 2:
                        wait_taken(act, l, "glu_a", c - 2)
                    af(sig[:, c % 2, :], ps_of("glu_b", c)[:, 0:TOK], ACT.Sigmoid).then_inc(taken["act"], 1)
                n_sq = 0
                for j in range(2 * TT):
                    t, half = divmod(j, 2)
                    wait_full(act, l, "q", j)
                    if n_sq >= 2:
                        act.wait_ge(sq_summed, l * 10 + (n_sq - 1))
                    src = ps_of("q", j)[:, 0:H * QK // 2]
                    af(scratch[:, n_sq % 2, 0:H * QK // 2], src, ACT.Square).then_inc(squared, 1)
                    af(q[:, t, half * 4:half * 4 + 4, :], src.rearrange("p (h d) -> p h d", h=4), ACT.Copy
                       ).then_inc(taken["act"], 1)
                    n_sq += 1
                act.wait_ge(head_summed, l * 2 + 1)
                af(head_r[:, 0:24], head_ss[:, 0:24], ACT.Sqrt, bias=eps[:, 1:2], scale=1.0).then_inc(head_rooted, 1)
                for t in range(KT):
                    wait_full(act, l, "k", t)
                    act.wait_ge(sq_summed, l * 10 + (n_sq - 1))
                    src = ps_of("k", t)
                    af(scratch[:, n_sq % 2, :], src, ACT.Square).then_inc(squared, 1)
                    af(k[:, t, :, 0:NOPE], src.rearrange("p (h d) -> p h d", h=H), ACT.Copy).then_inc(taken["act"], 1)
                    n_sq += 1
                    wait_full(act, l, "v", t)
                    af(v[:, t, :], ps_of("v", t), ACT.Copy).then_inc(taken["act"], 1)
                act.wait_ge(head_summed, l * 2 + 2)
                af(head_r[:, 0:32], head_ss[:, 0:32], ACT.Sqrt, bias=eps[:, 0:1], scale=1.0 / QK).then_inc(head_rooted, 1)

                def gate(c0):
                    for c in range(c0, c0 + KD):
                        wait_full(act, l, "gate", c)
                        af(gates[:, c, :], ps_of("gate", c)[:, 0:TOK], ACT.Sigmoid).then_inc(taken["act"], 1)

                gate(0)
                for hd in range(H):
                    wait_full(act, l, "qT", hd)
                    af(qT[0:QK, hd, :], ps_of("qT", hd)[0:QK, 0:TOK], ACT.Copy).then_inc(taken["act"], 1)
                for hd in range(H):
                    wait_full(act, l, "kT", hd)
                    af(kT[0:QK, hd, :], ps_of("kT", hd)[0:QK, :], ACT.Copy).then_inc(taken["act"], 1)
                gate(KD)

                wait_taken(act, l, "mean")
                m = af(u[:, :, HALF:HALF + Z_W], z[:, :, :], ACT.Square)
                m.then_inc(z_squared, 1)

                def soft(i):
                    hd, t = divmod(i, TT)
                    n = CTX if t == 0 else LAT + PAST
                    if i >= 3:
                        wait_full(act, l, "pT", i - 3)
                    act.wait_ge(max_ready, l * H * TT + (i + 1))
                    af(probs[:, i % 3, 0:n], ps_of("s", i)[:, 0:n], ACT.Exp, bias=row_max[:, i:i + 1],
                       accum_out=row_sum[:, t * H + hd:t * H + hd + 1]).then_inc(taken["act"], 1)

                def copy_pT(i):
                    n = CTX if i % TT == 0 else LAT + PAST
                    wait_full(act, l, "pT", i)
                    act.wait_ge(pv_done, l * H * TT + (i - 1))
                    af(probsT[:, i % 2, 0:n], ps_of("pT", i)[:, 0:n], ACT.Copy).then_inc(taken["act"], 1)

                for i in range(H * TT + 2):
                    if i < H * TT:
                        soft(i)
                    if i >= 2 and i % 2:
                        copy_pT(i - 2)
                    if i == 12:
                        wait_full(act, l, "var")
                        af(rs[:, :], ps_of("var")[:, 0:Z_W], ACT.Sqrt, bias=eps[:, 0:1], scale=1.0 / DC
                           ).then_inc(taken["act"], 1)
                act.wait_ge(z_normed, l + 1)
                wait_full(act, l, "oT", 0)
                for c in range(KC):
                    for a, b, n in ((0, 0, CTX), (CTX, Z_LAT, LAT)):
                        m = af(cT[:, c, a:a + n], z[:, c, b:b + n], ACT.Silu, scale=pf("ln_g")[:, c:c + 1],
                               bias=pf("ln_b")[:, c:c + 1])
                m.then_inc(conv_act, 1)
                for c in range(4):
                    wait_full(act, l, "oT", c)
                    af(oT[:, c, :], ps_of("oT", c)[:, 0:TOK], ACT.Copy).then_inc(taken["act"], 1)
                norm(1)
                for j in range(2 * TT):
                    t, half = divmod(j, 2)
                    if j == 3:
                        act.wait_ge(ex_in, l + 1)
                        af(ex, ex, ACT.Exp).then_inc(ex_out, 1)
                    wait_full(act, l, "hrow", j)
                    af(hrow[:, t, half * 512:(half + 1) * 512], ps_of("hrow", j), ACT.Copy).then_inc(taken["act"], 1)

                act.wait_ge(routed, l + 1)
                n = passes(act, l)
                rewind()
                with act.Fori(0, n) as p:
                    with act.Fori(0, GROUPS) as g:
                        i = act.snap(done + p * GROUPS + g)
                        act.wait_ge(pickT_full, i + 1)
                        af(pickT, ps[:, 6, 0:TOK], ACT.Copy).then_inc(pickT_taken, 1)
                        act.wait_ge(hg_full, i * 3 + 2)
                        af(hg[:, 4:8, :], ps[:, 5, :].rearrange("p (c n) -> p c n", c=4), ACT.Copy).then_inc(hg_act, 1)

                        def silu(e):
                            act.wait_ge(hid_full, i * EPG + (e + 1))
                            if e >= 2:
                                act.wait_ge(hm_ready, i * EPG + (e - 1))
                            af(hs[:, e % 2, :], ps[:, 2 + e % 2, 0:FE], ACT.Silu).then_inc(silu_done, 1)

                        def copy_hT(e):
                            act.wait_ge(hT_full, i * EPG + (e + 1))
                            if e >= 2:
                                act.wait_ge(w2_done, i * EPG + (e - 1))
                            af(hT[:, e % 2, :, :], ps[:, 6 + e % 2, 0:FE].rearrange("p (c n) -> p c n", c=2), ACT.Copy
                               ).then_inc(hT_taken, 1)

                        silu(0)
                        for e in range(EPG):
                            if e + 1 < EPG:
                                silu(e + 1)
                            copy_hT(e)
                        act.wait_ge(w2_done, i * EPG + EPG)
                        af(y_sb[:, 512:D], ps[:, 1, :], ACT.Copy).then_inc(y_act, 1)

        @block.vector
        def _(dve):
            vt = nc.vector.tensor_tensor
            vs = nc.vector.tensor_scalar
            stt = nc.vector.scalar_tensor_tensor
            copy = nc.vector.tensor_copy
            count = [0]

            def mark(ins):
                count[0] += 1
                ins.then_inc(dve_order, 1)
                return count[0]

            def chain(ins):
                mark(ins)
                dve.wait_ge(dve_order, count[0])

            def rewind():
                dve.wait_ge(dve_order, count[0])
                dve.sem_clear(dve_order)
                count[0] = 0

            mark(nc.vector.memset(u[:, :, :], 0.0))
            mark(nc.vector.memset(eps[:, 0:1], EPS))
            mark(nc.vector.memset(eps[:, 1:2], EPS * QK))
            chain(nc.vector.memset(condp[:, :, :], 0.0))
            nc.vector.memset(before[0:1, :], 0).then_inc(set_up, 1)
            dve.wait_ge(loaded, 64)
            dve.wait_ge(cond_ready, 1)
            copy(condp[:, :, 0:2], cond_sb[:, :, :]).then_inc(condp_ready, 1)
            rewind()
            with dve.Fori(0, LAYERS) as l:
                with dve.Fori(0, ADA_TURNS) as r:
                    first = dve.snap((l * ADA_TURNS + r) * SLOTS)

                    def rows(s):
                        dve.wait_ge(ada_full, first + (s + 1))
                        if s >= 2:
                            dve.wait_ge(adaT_full, first + (s - 1))
                        copy(ada_rows[:, s % 2, :], ps[:, s % 2, 0:256]).then_inc(ada_taken, 1)

                    def columns(s):
                        dve.wait_ge(adaT_full, first + (s + 1))
                        ch = r * (2 * SLOTS) + 2 * s
                        bias = par_all[:, bass.ds(l, 1), bass.ds(ch, 2)].rearrange("p a c -> p (a c)")
                        vt(mod_all[:, bass.ds(l, 1), bass.ds(ch, 2), :].rearrange("p a c s -> p (a c) s"),
                           ps[:, 2 + s % 2, 0:4].rearrange("p (c s) -> p c s", c=2),
                           bias.unsqueeze(2).broadcast_to([P, 2, 2]), ALU.add).then_inc(adaT_taken, 1)

                    for s in range(SLOTS):
                        rows(s)
                        if s:
                            columns(s - 1)
                    columns(SLOTS - 1)
            nc.vector.memset(best, 0.0).then_inc(x_moe, 1)
            dve.wait_ge(adaT_taken, LAYERS * ADA_UNITS)

            with dve.Fori(0, LAYERS) as l:
                done = rounds_before(dve, l)
                mark(copy(par[:, :], par_all[:, bass.ds(l, 1), :].rearrange("p a n -> p (a n)")))
                mark(nc.vector.memset(u[:, :, U_CTX + CTX:U_LAT], 0.0))
                chain(copy(mod[:, :, :], mod_all[:, bass.ds(l, 1), :, :].rearrange("p a c s -> p (a c) s")))
                for which, name in enumerate(("norm1", "norm2")):
                    m = stt(amp[:, which, :, :], mod[:, 24 * which + 8:24 * which + 16, :], 1.0,
                            pf(name).unsqueeze(2).broadcast_to([P, KD, 2]), ALU.add, ALU.mult)
                m.then_inc(layer_set, 1)

                def norm(which):
                    wait_taken(dve, l, "ss", which)
                    chain(nc.vector.reciprocal(rs[:, 0:TOK], rs[:, 0:TOK]))
                    for c in range(KD):
                        vt(h[:, c, :], x[:, c, :], rs[:, 0:TOK], ALU.mult).then_inc(xn_ready, 1)

                norm(0)
                dve.wait_ge(lat_rms, l + 1)
                chain(nc.vector.reciprocal(lat_r, lat_r))
                for t in range(TT):
                    src = ps_of("lat", t)
                    vs(cq[:, t, :], src[:, 0:QL], lat_r[:, t:t + 1], None, ALU.mult)
                    vs(ckv[:, t, :], src[:, QL:QL + KVL], lat_r[:, 3 + t:4 + t], None, ALU.mult)
                    copy(kr[:, t, :], src[:, QL + KVL:QL + KVL + ROPE]).then_inc(taken["dve"], 1)
                mark(copy(kr[:, TT, :], pf("cache_kr")))
                for c in range(KC):
                    wait_full(dve, l, "glu_a", c)
                    wait_taken(dve, l, "glu_b", c)
                    src = ps_of("glu_a", c)
                    vt(u[:, c, U_CTX:U_CTX + CTX], src[:, 0:CTX], sig[:, c % 2, 0:CTX], ALU.mult)
                    vt(u[:, c, U_LAT:U_LAT + LAT], src[:, CTX:TOK], sig[:, c % 2, CTX:TOK], ALU.mult
                       ).then_inc(taken["dve"], 1)
                copy(ckvT[:, TOK:KEYS], pf("cache_ckv"))
                for c in range(3):
                    wait_full(dve, l, "latT", c)
                    gain = pf("q_lora")[:, c:c + 1] if c < 2 else pf("kv_lora")
                    dst = cqT[:, c, :] if c < 2 else ckvT[:, 0:TOK]
                    vs(dst, ps_of("latT", c)[:, 0:TOK], gain, None, ALU.mult).then_inc(taken["dve"], 1)
                mark(nc.vector.memset(low, 0.0))
                dve.wait_ge(taken["dve"], l * N_TAKEN["dve"] + (TAKEN[("latT", 2)][1] + 1))
                nc.vector.memset(most, 0.0).then_inc(ckv_ready, 1)

                def bc_head(a, n):
                    return a.unsqueeze(2).broadcast_to([P, a.shape[1], n])

                def bc_row(a, heads):
                    return a.unsqueeze(1).broadcast_to([P, heads, a.shape[1]])

                def rotate(rows, tile):
                    part = rows[:, :, NOPE:QK].rearrange("p h (a s f) -> p h a s f", a=2, s=2)
                    x1, x2 = part[:, :, :, 0, :], part[:, :, :, 1, :]
                    tmp = [scratch[:, 0, n * 128:(n + 1) * 128].rearrange("p (h a f) -> p h a f", h=H, a=2)
                           for n in range(4)]
                    cos, sin = (rope[:, tile, s, :, :].unsqueeze(1).broadcast_to([P, H, 2, NF]) for s in range(2))
                    vt(tmp[0], x1, cos, ALU.mult)
                    vt(tmp[1], x2, sin, ALU.mult)
                    vt(tmp[2], x2, cos, ALU.mult)
                    chain(vt(tmp[3], x1, sin, ALU.mult))
                    chain(vt(x1, tmp[0], tmp[1], ALU.subtract))
                    return vt(x2, tmp[2], tmp[3], ALU.add)

                for j in range(2 * TT):
                    dve.wait_ge(squared, l * 10 + (j + 1))
                    m = nc.vector.tensor_reduce(head_ss[:, j * 4:j * 4 + 4],
                                                scratch[:, j % 2, 0:H * QK // 2].rearrange("p (h d) -> p h d", h=4),
                                                AX_X, ALU.add)
                    m.then_inc(sq_summed, 1)
                mark(nc.vector.memset(low, 0.0))
                dve.wait_ge(sq_summed, l * 10 + 6)
                nc.vector.memset(most, 0.0).then_inc(head_summed, 1)
                dve.wait_ge(head_rooted, l * 2 + 1)
                chain(nc.vector.reciprocal(head_r[:, 0:24], head_r[:, 0:24]))
                wait_taken(dve, l, "q", 2 * TT - 1)
                for t in range(TT):
                    mark(vt(q[:, t, :, :], q[:, t, :, :], bc_head(head_r[:, t * 8:t * 8 + 8], QK), ALU.mult))
                last = count[0]
                for t in range(KT):
                    n = 2 * TT + t
                    dve.wait_ge(squared, l * 10 + (n + 1))
                    m = nc.vector.tensor_reduce(head_ss[:, t * 8:t * 8 + 8],
                                                scratch[:, n % 2, :].rearrange("p (h d) -> p h d", h=H), AX_X, ALU.add)
                    m.then_inc(sq_summed, 1)
                dve.wait_ge(sq_summed, l * 10 + 10)
                hs4 = head_ss.rearrange("p (t h) -> p t h", t=KT)
                vt(hs4, hs4, kr_ss.unsqueeze(2).broadcast_to([P, KT, H]), ALU.add).then_inc(head_summed, 1)
                dve.wait_ge(dve_order, last)
                for t in range(TT):
                    mark(vt(q[:, t, :, :], q[:, t, :, :], bc_row(pf("q_norm"), H), ALU.mult))
                dve.wait_ge(dve_order, count[0])
                dve.wait_ge(head_rooted, l * 2 + 2)
                chain(rotate(q[:, 1, :, :], 0))
                rotate(q[:, 2, :, :], 1).then_inc(qk_ready, 1)
                chain(nc.vector.reciprocal(head_r, head_r))
                wait_taken(dve, l, "k", KT - 1)
                for t in range(KT):
                    r8 = head_r[:, t * 8:t * 8 + 8]
                    mark(vt(k[:, t, :, 0:NOPE], k[:, t, :, 0:NOPE], bc_head(r8, NOPE), ALU.mult))
                    mark(vt(k[:, t, :, NOPE:QK], bc_row(kr[:, t, :], H), bc_head(r8, ROPE), ALU.mult))
                dve.wait_ge(dve_order, count[0])
                for t in range(KT):
                    mark(vt(k[:, t, :, :], k[:, t, :, :], bc_row(pf("k_norm"), H), ALU.mult))
                dve.wait_ge(dve_order, count[0])
                chain(rotate(k[:, 1, :, :], 0))
                rotate(k[:, 2, :, :], 1).then_inc(qk_ready, 1)

                dve.wait_ge(taken["dve"], l * N_TAKEN["dve"] + (TAKEN[("glu_a", KC - 1)][1] + 1))
                for tap in range(TAPS):
                    for c in range(KC):
                        src = u[:, c, tap:tap + Z_W]
                        if tap == 0:
                            mark(vs(z[:, c, :], src, dw[:, c, 0:1], pf("dw_b")[:, c:c + 1], ALU.mult, ALU.add))
                            continue
                        dve.wait_ge(dve_order, count[0] - (KC - 1))
                        m = stt(z[:, c, :], src, dw[:, c, tap:tap + 1], z[:, c, :], ALU.mult, ALU.add)
                        if tap == TAPS - 1 and c == KC - 1:
                            m.then_inc(conv_done, 1)
                        else:
                            mark(m)
                dve.wait_ge(conv_done, l + 1)
                wait_full(dve, l, "mean")
                for c in range(KC):
                    m = stt(z[:, c, :], ps_of("mean")[:, 0:Z_W], -1.0 / DC, z[:, c, :], ALU.mult, ALU.add)
                m.then_inc(taken["dve"], 1)

                def peak(i):
                    n = CTX if i % TT == 0 else LAT + PAST
                    wait_full(dve, l, "s", i)
                    nc.vector.tensor_reduce(row_max[:, i:i + 1], ps_of("s", i)[:, 0:n], AX_X, ALU.max, negate=True
                                            ).then_inc(max_ready, 1)

                def copy_pT(i):
                    n = CTX if i % TT == 0 else LAT + PAST
                    wait_full(dve, l, "pT", i)
                    if i >= 2:
                        dve.wait_ge(pv_done, l * H * TT + (i - 1))
                    copy(probsT[:, i % 2, 0:n], ps_of("pT", i)[:, 0:n]).then_inc(taken["dve"], 1)

                for i in range(H * TT + 2):
                    if i < H * TT:
                        peak(i)
                    if i >= 2 and i % 2 == 0:
                        copy_pT(i - 2)
                    if i == 14:
                        wait_taken(dve, l, "var")
                        chain(nc.vector.reciprocal(rs[:, :], rs[:, :]))
                        for c in range(KC):
                            m = vt(z[:, c, :], z[:, c, :], rs[:, :], ALU.mult)
                        m.then_inc(z_normed, 1)
                dve.wait_ge(pv_done, l * H * TT + H * TT)
                chain(nc.vector.reciprocal(row_sum, row_sum))
                for t in range(TT):
                    vt(o[:, t, :].rearrange("p (h d) -> p h d", h=H), ps[:, 5 + t, :].rearrange("p (h d) -> p h d", h=H),
                       bc_head(row_sum[:, t * H:(t + 1) * H], VD), ALU.mult).then_inc(taken["dve"], 1)
                for c in range(KD):
                    wait_full(dve, l, "pw2", c)
                    vt(gates[:, c, :], gates[:, c, :], ps_of("pw2", c)[:, 0:TOK], ALU.mult).then_inc(taken["dve"], 1)
                for c in range(KD):
                    wait_full(dve, l, "wo", c)
                    vt(gates[:, KD + c, :], gates[:, KD + c, :], ps_of("wo", c)[:, 0:TOK], ALU.mult
                       ).then_inc(taken["dve"], 1)
                    wait_taken(dve, l, "wo", c)
                    vt(gates[:, c, :], gates[:, c, :], gates[:, KD + c, :], ALU.add).then_inc(merged, 1)
                for c in range(KD):
                    wait_full(dve, l, "wout", c)
                    for st, (a, b) in enumerate(((0, CTX), (CTX, TOK))):
                        m = stt(x[:, c, a:b], ps_of("wout", c)[:, a:b], mod[:, 16 + c, st:st + 1], x[:, c, a:b],
                                ALU.mult, ALU.add)
                    m.then_inc(taken["dve"], 1)
                wait_taken(dve, l, "wout", KD - 1)
                norm(1)

                def b4(a):
                    return a.unsqueeze(2).broadcast_to([P, TT, 4])

                def one_hot(dst, src, m):
                    chain(vt(tie, src, b4(m), ALU.is_ge))
                    chain(stt(tie, tie, -8.0, order4.unsqueeze(1).broadcast_to([P, TT, 4]), ALU.mult, ALU.add))
                    chain(nc.vector.tensor_reduce(low, tie, AX_X, ALU.min))
                    return vt(dst, tie, b4(low), ALU.is_equal)

                wait_full(dve, l, "logit")
                vt(lg, ps_of("logit")[:, 0:TT * NR].rearrange("p (t n) -> p t n", t=TT),
                   pf("route_b").unsqueeze(1).broadcast_to([P, TT, NR]), ALU.add).then_inc(taken["dve"], 1)
                wait_taken(dve, l, "logit")
                g_lg = lg[:, :, 0:GROUPS]
                chain(nc.vector.tensor_reduce(best, g_lg, AX_X, ALU.max))
                one_hot(oh_g, g_lg, best).then_inc(onehot_ready, 1)
                vt(ex[:, :, 0:4], g_lg, b4(best), ALU.subtract)
                dve.wait_ge(onehot_ready, l + 1)
                for t in range(TT):
                    own = tmp16[:, t * 16:(t + 1) * 16].rearrange("p (e g) -> p e g", e=EPG)
                    mark(vt(own, lg[:, t, GROUPS:NR].rearrange("p (g e) -> p e g", g=GROUPS),
                            oh_g[:, t, :].unsqueeze(1).broadcast_to([P, EPG, GROUPS]), ALU.mult))
                dve.wait_ge(dve_order, count[0])
                chain(nc.vector.tensor_reduce(e_own.rearrange("p t e -> p (t e)"),
                                              tmp16.rearrange("p (n g) -> p n g", g=GROUPS), AX_X, ALU.add))
                chain(nc.vector.tensor_reduce(m1, e_own, AX_X, ALU.max))
                chain(one_hot(oh_1, e_own, m1))
                chain(stt(e_rest, oh_1, -3.0e38, e_own, ALU.mult, ALU.add))
                chain(nc.vector.tensor_reduce(m2, e_rest, AX_X, ALU.max))
                vt(ex[:, :, 4], m2, m1, ALU.subtract).then_inc(ex_in, 1)
                chain(one_hot(oh_2, e_rest, m2))
                dve.wait_ge(ex_out, l + 1)
                mark(nc.vector.tensor_reduce(gw, ex[:, :, 0:4], AX_X, ALU.add))
                chain(vs(dn, ex[:, :, 4], 1.0, None, ALU.add))
                chain(vt(dn, dn, gw, ALU.mult))
                chain(nc.vector.reciprocal(v1, dn))
                chain(vt(v2, v1, ex[:, :, 4], ALU.mult))
                mark(vt(cw, oh_1, b4(v1), ALU.mult))
                chain(vt(cw2, oh_2, b4(v2), ALU.mult))
                chain(vt(cw, cw, cw2, ALU.add))
                wait_full(dve, l, "rank")
                rank = ps_of("rank")[:, 0:(TT + 1) * 4].rearrange("p (t n) -> p t n", n=4)
                chain(vt(tie, rank[:, 0:TT, :], oh_g, ALU.mult))
                chain(nc.vector.tensor_reduce(pos, tie, AX_X, ALU.add))
                nc.vector.tensor_reduce(most[:, 0:1], rank[:, TT, :], AX_X, ALU.max).then_inc(taken["dve"], 1)
                wait_taken(dve, l, "rank")
                chain(vs(most[:, 1:2], most[:, 0:1], float(P), 1.0, ALU.is_gt, ALU.add))
                chain(vs(most[:, 2:3], most[:, 0:1], float(2 * P), None, ALU.is_gt))
                chain(vt(most[:, 1:2], most[:, 1:2], most[:, 2:3], ALU.add))
                mark(copy(rounds[0:1, bass.ts(l, 1)], most[0:1, 1:2]))
                chain(copy(low[0:1, 0:1], before[0:1, bass.ts(l, 1)]))
                chain(stt(low[0:1, 1:2], most[0:1, 1:2], float(GROUPS), low[0:1, 0:1], ALU.mult, ALU.add))
                copy(before[0:1, bass.ds(l + 1, 1)], low[0:1, 1:2]).then_inc(routed, 1)

                dve.wait_ge(routed, l + 1)
                dve.wait_ge(ckv_stored, l * 32 + 32)
                n = passes(dve, l)
                rewind()
                with dve.Fori(0, n) as p:
                    with dve.Fori(0, GROUPS) as g:
                        i = dve.snap(done + p * GROUPS + g)
                        for t in range(TT):
                            m = vs(pick[:, t, :], slot_no, pos[:, t:t + 1], oh_g[:, t, bass.ts(g, 1)], ALU.is_equal, ALU.mult)
                        m.then_inc(pick_ready, 1)
                        dve.wait_ge(hg_full, i * 3 + 1)
                        copy(hg[:, 0:4, :], ps[:, 4, :].rearrange("p (c n) -> p c n", c=4)).then_inc(hg_dve, 1)
                        dve.wait_ge(hg_full, i * 3 + 3)
                        copy(cwg, ps[:, 7, 0:4]).then_inc(hg_dve, 1)
                        dve.wait_ge(hg_dve, i * 2 + 2)
                        for e in range(EPG):
                            dve.wait_ge(silu_done, i * EPG + (e + 1))
                            if e >= 2:
                                dve.wait_ge(hT_full, i * EPG + (e - 1))
                            stt(hm[:, e % 2, :], hs[:, e % 2, :], cwg[:, e:e + 1], ps[:, 2 + e % 2, FE:2 * FE],
                                ALU.mult, ALU.mult).then_inc(hm_ready, 1)
                        dve.wait_ge(w2_done, i * EPG + EPG)
                        copy(y_sb[:, 0:512], ps[:, 0, :]).then_inc(y_dve, 1)
                        for c in range(KD):
                            bank = (4, 5, 6, 7, 2, 3, 4, 5)[c]
                            dve.wait_ge(back_full, i * KD + (c + 1))
                            for st, (a, b) in enumerate(((0, CTX), (CTX, TOK))):
                                m = stt(x[:, c, a:b], ps[:, bank, a:b], mod[:, 40 + c, st:st + 1], x[:, c, a:b],
                                        ALU.mult, ALU.add)
                            m.then_inc(x_moe, 1)
                        dve.wait_ge(x_moe, i * KD + (KD + 1))
                    chain(vs(pos, pos, -float(P), None, ALU.add))
                    rewind()


def _fold(w, cols):
    kk, n = w.shape
    return w.reshape(kk // P, P, n // cols, cols).transpose(2, 1, 0, 3).reshape(n // cols, P, kk // P * cols)


def _unit(a):
    out = np.zeros((P, UNIT), np.float32)
    out[:, :a.shape[1]] = a
    return out[None]


def _stream(w, l):
    w_in = w["w_in"][l]
    i0, i1, i2, i3 = 2 * DC, 2 * DC + QL, 2 * DC + QL + KVL, 2 * DC + QL + KVL + ROPE
    glu = w_in[:, :i0].reshape(D, 2, KC, P).transpose(0, 2, 1, 3).reshape(D, i0)
    latent = np.zeros((D, 256), np.float32)
    latent[:, :i3 - i1] = w_in[:, i1:i3]
    ukv = w["w_ukv"][l].reshape(KVL, H, NOPE + VD)
    ukv = np.concatenate([ukv[:, :, :NOPE].reshape(KVL, -1), ukv[:, :, NOPE:].reshape(KVL, -1)], axis=1)
    parts = [_fold(w["w_ada"][l], 256), _fold(w_in[:, i0:i1], 256), _fold(latent, 256), _fold(glu, 256),
             _unit(_fold(w["w_uq"][l], H * QK)[0]), _unit(ukv), _fold(w_in[:, i3:], 256),
             _fold(w["w_pw2"][l], 512), _fold(w["w_o"][l], 512), _fold(w["w_out"][l], 256)]
    w13 = np.concatenate([w["w1"][l], w["w3"][l]], axis=2)
    for e in range(EXPERTS):
        parts.append(w13[e].reshape(2, 4, P, 2 * FE).transpose(0, 2, 1, 3).reshape(2, P, UNIT))
        parts.append(w["w2"][l][e].reshape(2, P, D).transpose(1, 0, 2).reshape(1, P, UNIT))
    return np.concatenate(parts, axis=0)


def _columns(a):
    return a.reshape(-1, P).T


def _params(w, l):
    row = lambda a: np.broadcast_to(a.reshape(1, -1), (P, a.size))
    route = np.concatenate([w["w_group"][l], w["w_expert"][l]], axis=1)
    parts = {
        "b_ada": _columns(w["b_ada"][l]), "norm1": _columns(w["norm1"][l]), "norm2": _columns(w["norm2"][l]),
        "dw": w["conv_dw"][l].reshape(TAPS, KC, P).transpose(2, 1, 0).reshape(P, -1),
        "dw_b": _columns(w["conv_dw_b"][l]), "ln_g": _columns(w["conv_ln_g"][l]), "ln_b": _columns(w["conv_ln_b"][l]),
        "q_lora": _columns(w["q_lora_norm"][l]), "kv_lora": _columns(w["kv_lora_norm"][l]),
        "q_norm": row(w["q_norm"][l]), "k_norm": row(w["k_norm"][l]),
        "route_b": row(np.concatenate([w["b_group"][l], w["b_expert"][l]])),
        "route_w": route.reshape(KD, P, NR).transpose(1, 0, 2).reshape(P, -1),
        "cache_ckv": w["cache_ckv"][0, l].T, "cache_kr": w["cache_krope"][0, l],
    }
    return np.concatenate([parts[n] for n, _ in _FIELDS], axis=1)


def _constants():
    c = np.zeros((P, NCONST), np.float32)
    c[:, C_ID:C_ID + P] = np.eye(P)
    c[:, C_ONE:C_ONE + P] = 1.0
    c[:, C_TRI:C_TRI + P] = np.triu(np.ones((P, P)), 1)
    c[:, C_SLOT:C_SLOT + P] = np.arange(P)
    for s in range(2):
        c[s::32, C_SEL + s] = 1.0
    freqs = (np.float32(10000.0) ** (-np.arange(NF, dtype=np.float32) / np.float32(NF))).astype(np.float32)
    n = np.arange(LAT)
    ang = np.stack([(n // GRID_W).astype(np.float32)[:, None] * freqs, (n % GRID_W).astype(np.float32)[:, None] * freqs], 1)
    table = np.stack([np.cos(ang), np.sin(ang)], 1).reshape(2, P, 2 * 2 * NF)
    c[:, C_ROPE:C_ROPE + 64] = table.transpose(1, 0, 2).reshape(P, 64)
    c[:, C_ORD:C_ORD + 4] = np.arange(4)
    return c


def kernel(**inputs):
    import concourse.bacc as bacc
    from concourse.bass_utils import run_bass_kernel_spmd

    w = {n: np.asarray(a) for n, a in inputs.items()}
    tokens = np.concatenate([w["x_prompt"][0], w["x_sample"][0]], axis=0)
    arrays = {
        "wstream": np.stack([_stream(w, l) for l in range(LAYERS)]).reshape(LAYERS, LAYER_UNITS // SLOTS, SLOTS, P, UNIT),
        "x0": np.ascontiguousarray(tokens.reshape(TOK, KD, P).transpose(2, 1, 0)),
        "cond": np.ascontiguousarray(np.stack([_columns(w["c_ctx"]), _columns(w["c"][0])], axis=2)),
        "par_in": np.ascontiguousarray(np.stack([_params(w, l) for l in range(LAYERS)], axis=1)),
        "const_in": _constants(),
    }
    nc = bacc.Bacc("TRN2", target_bir_lowering=False, num_devices=1)
    args = [nc.dram_tensor(n, a.shape, F32, kind="ExternalInput").ap() for n, a in arrays.items()]
    outs = [("x_out", (P, KD, TOK)), ("ckv_out", (LAYERS, P, CTX)), ("kr_out", (LAYERS, CTX, ROPE))]
    args += [nc.dram_tensor(n, s, F32, kind="ExternalOutput").ap() for n, s in outs]
    build(nc, *args)
    r = run_bass_kernel_spmd(nc, [arrays], core_ids=[0]).results[0]
    y = r["x_out"].transpose(2, 1, 0).reshape(TOK, D)
    return (y[None, :CTX], y[None, CTX:], r["ckv_out"].transpose(0, 2, 1)[None], r["kr_out"][None])
```

```python
from contextlib import ExitStack

import numpy as np

import concourse.bass as bass
from concourse import mybir

F32 = mybir.dt.float32
I32 = mybir.dt.int32
F32R = mybir.dt.float32r
ALU = mybir.AluOpType
ACT = mybir.ActivationFunctionType
AX_X = mybir.AxisListType.X

P = 128
LAYERS = 2
D = 1024
KD = D // P
CTX, LAT, PAST = 128, 256, 128
TOK = CTX + LAT
TT = TOK // P
KEYS = TOK + PAST
KT = KEYS // P
GRID_W = 64
DC = 512
KC = DC // P
TAPS = 31
HALF = TAPS // 2
H, NOPE, ROPE, VD = 8, 64, 32, 64
QK = NOPE + ROPE
NF = ROPE // 4
QL, KVL = 256, 128
LAT_W = QL + KVL + ROPE
GROUPS, EPG = 4, 4
EXPERTS = GROUPS * EPG
FE = 256
EPS = 1e-6

U_CTX = HALF
U_LAT = HALF + CTX + HALF
U_W = U_LAT + LAT + HALF
Z_W = U_W - 2 * HALF
Z_LAT = CTX + HALF

UNIT = 2048
SLOTS = 6
ADA_UNITS = 6 * D * KD // UNIT
ADA_FIRST = 2 * D * KD // UNIT
ADA_COLS = UNIT // KD
ADA_HEAD = 4


def pre_stream():
    ada = iter(range(ADA_FIRST, ADA_UNITS))
    out = [("lat", 0), ("lat", 1)] + [("ada", next(ada)) for _ in range(ADA_HEAD)]
    for c in range(KC):
        out += [("glu", c), ("ada", next(ada))]
    for c in range(KD):
        out += [("gate", c), ("ada", next(ada))]
    out += [("uq", 0), ("ukv", 0)]
    nxt = iter(range(ADA_FIRST))
    for name, n in (("wo", 2), ("pw2", 2), ("wout", 4)):
        for c in range(n):
            out += [(name, c), ("next", next(nxt))]
    return out


PRE = pre_stream()
PRE_AT = {e: n for n, e in enumerate(PRE)}
PRE_UNITS = len(PRE)
GROUP_UNITS = 3 * EPG
SPLIT = [e for e in PRE if e[0] in ("lat", "glu", "gate", "wo", "pw2", "wout")]
SPLIT_AT = {e: n for n, e in enumerate(SPLIT)}
PRE_SPLITS = len(SPLIT)
EARLY_SPLITS = SPLIT_AT[("wo", 0)]
PRE_PLACES, MOE_PLACES = 3, 4
GROUP = [("up", 0, 0), ("up", 0, 1), ("up", 1, 0), ("up", 1, 1), ("down", 0, 0), ("up", 2, 0), ("up", 2, 1),
         ("down", 1, 0), ("up", 3, 0), ("up", 3, 1), ("down", 2, 0), ("down", 3, 0)]
GROUP_AT = {e: n for n, e in enumerate(GROUP)}

_FIELDS = [("b_ada", 48), ("norm1", KD), ("norm2", KD), ("dw", KC * TAPS), ("dw_b", KC), ("ln_g", KC),
           ("ln_b", KC), ("q_lora", QL // P), ("kv_lora", 1), ("q_norm", QK), ("k_norm", QK),
           ("route_b", GROUPS + EXPERTS), ("route_w", KD * (GROUPS + EXPERTS)),
           ("cache_ckv", PAST), ("cache_kr", ROPE)]
FIELD = {}
NPAR = 0
for _n, _w in _FIELDS:
    FIELD[_n] = (NPAR, NPAR + _w)
    NPAR += _w
NR = GROUPS + EXPERTS

C_ID, C_ONE, C_TRI, C_SLOT, C_SEL, C_ROPE, C_ORD, C_ADA = 0, 128, 256, 384, 512, 514, 514 + 64, 514 + 68
NCONST = C_ADA + 16

CONV_GLU = [6, 9, 10, 10]
CONV_EARLY = sum(CONV_GLU)
AHEAD = 3
EXPERT_STEPS = [("split", 3), ("split", 4), ("places", 0), ("gate", 0), ("split", 5), ("turn", 0), ("split", 6),
                ("gate", 1), ("split", 7), ("split", 8), ("turn", 1), ("split", 9), ("gate", 2), ("split", 10),
                ("turn", 2), ("split", 11), ("gate", 3), ("split", 12), ("turn", 3), ("split", 13), ("gather", 0),
                ("split", 14), ("sum", 0), ("sum", 1), ("gather", 1)]
BACK_BANKS = (6, 4, 0, 1, 7, 5, 6, 4)


def group_steps(last):
    return [(kind, n) for kind, n in EXPERT_STEPS
            if not (last and (kind == "gather" or kind == "split" and n >= GROUP_UNITS))]


def adas_after(kind, c):
    n = PRE_AT[(kind, c)] + 1
    out = []
    while n < PRE_UNITS and PRE[n][0] in ("ada", "next"):
        out.append(PRE[n])
        n += 1
    return out


RANK_AFTER = 2


def pre_jobs():
    jobs = []

    def add(name, index, taker, bank=None):
        if bank is None:
            bank = add.next
            add.next = (add.next + 1) % add.banks
        jobs.append((name, index, bank, taker))

    turning = []

    def add_ada(entry):
        if turning:
            add("adaT", turning.pop(), "dve")
        if entry is not None:
            add("ada", entry, "dve")
            turning.append(entry)

    add.next, add.banks = 0, 8
    add("ss", 0, "act")
    for e in adas_after("lat", 1):
        add_ada(e)
    for t in range(TT):
        add("lat", t, "dve")
    for c in range(KC):
        add("glu_a", c, "dve")
        add("glu_b", c, "act")
        for e in adas_after("glu", c):
            add_ada(e)
    for c in range(3):
        add("latT", c, "dve")
    for c in range(KD):
        add("gate", 2 * c, "act")
        add("gate", 2 * c + 1, "act")
        for e in adas_after("gate", c):
            add_ada(e)
    add_ada(None)
    for j in range(2 * TT):
        add("q", j, "act")
    for t in range(KT):
        add("k", t, "act")
        add("v", t, "act")
    add("mean", 0, "dve")
    for h in range(H):
        add("qT", h, "act")
    for h in range(H):
        add("kT", h, "act")
    add.next, add.banks = 0, 5
    for i in range(H * TT + 2):
        if i < H * TT:
            add("s", i, "act")
        if i >= 2:
            add("pT", i - 2, "dve" if i % 2 == 0 else "act")
        if i == 12:
            add("var", 0, "act")
    for t in range(TT):
        add("o", t, "dve", 5 + t)
    add.next, add.banks = 0, 8
    for c in range(4):
        add("oT", c, "dve")
    for name, units, per in (("wo", 2, 4), ("pw2", 2, 4), ("wout", 4, 2)):
        for n in range(units):
            for c in range(per):
                add(name, n * per + c, "dve")
            for e in adas_after(name, n):
                add_ada(e)
    add_ada(None)
    add("ss", 1, "act")
    add("logit", 0, "dve")
    for j in range(2 * TT):
        add("hrow", j, "dve")
        if j == RANK_AFTER:
            add("rank", 0, "dve")
    return jobs


JOBS = pre_jobs()
JOB = {(n, i): k for k, (n, i, _, _) in enumerate(JOBS)}
FULL_JOBS = [j for j in JOBS if j[0] != "o"]
FULL = {(n, i): k for k, (n, i, _, _) in enumerate(FULL_JOBS)}
TAKEN = {}
for _who in ("act", "dve"):
    for _k, (_n, _i, _, _) in enumerate([j for j in JOBS if j[3] == _who]):
        TAKEN[(_n, _i)] = (_who, _k)
JOB_ADA = {e: n for n, e in enumerate(i for name, i, _, _ in JOBS if name == "ada")}
ADA_ORDER = list(JOB_ADA)
N_TAKEN = {who: sum(j[3] == who for j in JOBS) for who in ("act", "dve")}


def build(nc, wfirst, wpre, wmoe, x0, cond, par_in, const_in, x_out, ckv_out, kr_out):
    ctx = ExitStack()
    with ctx:
        def sem(name):
            return ctx.enter_context(nc.semaphore(name))

        def up32(n):
            return (n + 31) // 32 * 32

        where = [up32(nc.sbuf_base)]
        names = set()

        def place(name, n, dt=F32, at=None):
            assert name not in names
            names.add(name)
            if at is None:
                at = region(n)
            return nc.alloc_sbuf_tensor_at(name, [P, n], dt, offset=at)[:, :]

        def region(n):
            at = where[0]
            where[0] = up32(at + 4 * n)
            return at

        def v3(a, c):
            return a.rearrange("p (c n) -> p c n", c=c)

        ring = place("ring", SLOTS * UNIT)
        x = v3(place("x", KD * TOK), KD)
        par = place("par", NPAR)
        const = place("const", NCONST)
        cond_sb = v3(place("cond_sb", KD * 2), KD)
        condp = v3(place("condp", KD * 32), KD)
        ada_rows = v3(place("ada_rows", 2 * ADA_COLS), 2)
        mod_next = v3(place("mod_next", 16 * 2), 16)
        mod = v3(place("mod", 48 * 2), 48)
        amp = place("amp", 2 * KD * 2).rearrange("p (w c s) -> p w c s", w=2, c=KD)
        rs = place("rs", Z_W)
        kr = v3(place("kr", KT * ROPE), KT)
        small = place("small", 384)
        eps = place("eps", 2)
        counts = place("counts", 2 * LAYERS + 1, I32)
        rounds, before = counts[0:1, 0:LAYERS], counts[0:1, LAYERS:2 * LAYERS + 1]

        h_hi = v3(place("h_hi", KD * TOK, F32R), KD)
        h_lo = v3(place("h_lo", KD * TOK, F32R), KD)
        hrow_hi = h_hi.rearrange("p c n -> p (c n)").rearrange("p (t n) -> p t n", t=TT)
        hrow_lo = h_lo.rearrange("p c n -> p (c n)").rearrange("p (t n) -> p t n", t=TT)
        gates_at = region(2 * KD * TOK)
        gates = v3(place("gates", 2 * KD * TOK, at=gates_at), 2 * KD)
        h = gates[:, 0:KD, :]
        conv_at = region(KC * (U_W + Z_W) + 8)
        u = v3(place("u", KC * U_W, at=conv_at), KC)
        z = v3(place("z", KC * Z_W, at=up32(conv_at + 4 * KC * U_W)), KC)
        cT_hi = v3(place("cT_hi", KC * TOK, F32R, at=conv_at), KC)
        att_at = region((KT * VD + TOK + KEYS + TT * QK + KT * QK) * H)
        v = v3(place("v", KT * H * VD, at=att_at), KT)
        qT_at = att_at + 4 * KT * H * VD
        qT = v3(place("qT", H * TOK, at=qT_at), H)
        kT_at = qT_at + 4 * H * TOK
        kT = v3(place("kT", H * KEYS, at=kT_at), H)
        q_at = kT_at + 4 * H * KEYS
        q = place("q", TT * H * QK, at=q_at).rearrange("p (t h d) -> p t h d", t=TT, h=H)
        k_at = q_at + 4 * TT * H * QK
        k = place("k", KT * H * QK, at=k_at).rearrange("p (t h d) -> p t h d", t=KT, h=H)
        o_at = k_at + 4 * (KT * H * QK - TT * DC)
        o = v3(place("o", TT * DC, at=o_at), TT)
        cT_lo = v3(place("cT_lo", KC * TOK, F32R, at=o_at), KC)
        assert att_at + 4 * 2 * UNIT * PRE_PLACES <= o_at
        w_hi = [place(f"w_hi{n}", UNIT, F32R, at=att_at + 4 * 2 * UNIT * n) for n in range(PRE_PLACES)]
        w_lo = [place(f"w_lo{n}", UNIT, F32R, at=att_at + 4 * (2 * n + 1) * UNIT) for n in range(PRE_PLACES)]
        w_hi.append(place("w_hi3", UNIT, F32R, at=gates_at + 4 * KD * TOK))
        w_lo.append(place("w_lo3", UNIT, F32R, at=conv_at))
        work_at = region(3 * TOK + 2 * TOK + KEYS + 1024)
        probs = v3(place("probs", 3 * TOK, at=work_at), 3)
        cq = v3(place("cq", TT * QL, at=work_at), TT)
        ckv = v3(place("ckv", TT * KVL, at=work_at + 4 * TT * QL), TT)
        probsT_at = work_at + 4 * 3 * TOK
        probsT = v3(place("probsT", 2 * TOK, at=probsT_at), 2)
        cqT = v3(place("cqT", 2 * TOK, at=probsT_at), 2)
        ckvT_at = probsT_at + 4 * 2 * TOK
        ckvT = place("ckvT", KEYS, at=ckvT_at)
        scratch_at = ckvT_at + 4 * KEYS
        scratch = v3(place("scratch", 1024, at=scratch_at), 2)
        sig = v3(place("sig", 2 * TOK, at=scratch_at), 2)
        oT_hi = v3(place("oT_hi", 4 * TOK, F32R, at=work_at), 4)
        oT_lo = v3(place("oT_lo", 4 * TOK, F32R, at=work_at + 4 * 4 * TOK), 4)
        hg_hi = v3(place("hg_hi", KD * P, F32R, at=gates_at), KD)
        hg_lo = v3(place("hg_lo", KD * P, F32R, at=gates_at + 4 * KD * P), KD)
        hs = v3(place("hs", 2 * FE, at=gates_at + 4 * (KD * TOK + UNIT)), 2)
        hm = v3(place("hm", 2 * FE, at=gates_at + 4 * (KD * TOK + UNIT + 2 * FE)), 2)
        y_hi = place("y_hi", D, F32R, at=work_at)
        y_lo = place("y_lo", D, F32R, at=work_at + 4 * D)
        hT_hi = place("hT_hi", 2 * FE, F32R, at=work_at + 4 * 2 * D).rearrange("p (s c n) -> p s c n", s=2, c=2)
        hT_lo = place("hT_lo", 2 * FE, F32R, at=work_at + 4 * (2 * D + 2 * FE)).rearrange("p (s c n) -> p s c n", s=2, c=2)
        pick = v3(place("pick", TT * P, F32R, at=work_at + 4 * (2 * D + 4 * FE)), TT)
        pickT = place("pickT", TOK, F32R, at=conv_at + 4 * UNIT)
        unused = v3(place("unused", 4 * 416, at=gates_at + 4 * KD * TOK), 4)
        assert where[0] <= nc.sbuf_usable_end

        at = [0]

        def sm(n):
            at[0] += n
            return small[:, at[0] - n:at[0]]

        lat_ss = sm(6)
        kr_ss = sm(KT)
        lat_r = sm(6)
        head_ss = sm(32)
        head_r = sm(32)
        row_max = sm(H * TT)
        row_sum = sm(H * TT)
        lg = v3(sm(TT * NR), TT)
        best = sm(TT)
        tie = v3(sm(TT * 4), TT)
        low = sm(TT)
        oh_g = v3(sm(TT * 4), TT)
        oh_1 = v3(sm(TT * 4), TT)
        oh_2 = v3(sm(TT * 4), TT)
        ex = v3(sm(TT * 5), TT)
        e_own = v3(sm(TT * 4), TT)
        e_rest = v3(sm(TT * 4), TT)
        m1 = sm(TT)
        m2 = sm(TT)
        gw = sm(TT)
        dn = sm(TT)
        v1 = sm(TT)
        v2 = sm(TT)
        cw = v3(sm(TT * 4), TT)
        cw2 = v3(sm(TT * 4), TT)
        pos = sm(TT)
        most = sm(4)
        cwg = sm(4)
        assert at[0] <= 384
        tmp16 = scratch[:, 0, 0:TT * 16]

        ps = ctx.enter_context(nc.psum_tensor("ps", [P, 8, 512], F32))

        ident = const[:, C_ID:C_ID + P]
        ones = const[:, C_ONE:C_ONE + P]
        tri = const[:, C_TRI:C_TRI + P]
        slot_no = const[:, C_SLOT:C_SLOT + P]
        sel = const[:, C_SEL:C_SEL + 2]
        rope = const[:, C_ROPE:C_ROPE + 64].rearrange("p (t s a f) -> p t s a f", t=2, s=2, a=2)
        order4 = const[:, C_ORD:C_ORD + 4]

        def pf(name):
            a, b = FIELD[name]
            return par[:, a:b]

        route_w = pf("route_w").rearrange("p (c n) -> p c n", c=KD)
        dw = pf("dw").rearrange("p (c n) -> p c n", c=KC)

        def slot(s, n=1):
            return ring[:, s * UNIT:(s + n) * UNIT]

        loaded = sem("loaded")
        x_loaded = sem("x_loaded")
        par_loaded = sem("par_loaded")
        w_landed = [sem(f"w_landed{s}") for s in range(SLOTS)]
        raw_used = sem("raw_used")
        set_up = sem("set_up")
        settled = sem("settled")
        cond_ready = sem("cond_ready")
        condp_ready = sem("condp_ready")
        ada_full = sem("ada_full")
        ada_taken = sem("ada_taken")
        adaT_full = sem("adaT_full")
        adaT_taken = sem("adaT_taken")
        split_hi = sem("split_hi")
        split_lo = sem("split_lo")
        split_used = sem("split_used")
        gain2_ready = sem("gain2_ready")
        h_raw = sem("h_raw")
        h_hi_done = sem("h_hi_done")
        oT_hi_done = sem("oT_hi_done")
        cT_hi_done = sem("cT_hi_done")
        sum_raw = sem("sum_raw")
        sum_hi_done = sem("sum_hi_done")
        hrow_hi_done = sem("hrow_hi_done")
        hT_hi_done = sem("hT_hi_done")
        hg_hi_done = sem("hg_hi_done")
        y_hi_done = sem("y_hi_done")
        layer_set = sem("layer_set")
        psum_full = sem("psum_full")
        taken = {"act": sem("psum_taken_by_act"), "dve": sem("psum_taken_by_dve")}
        sq_ready = sem("sq_ready")
        xn_ready = sem("xn_ready")
        h_ready = sem("h_ready")
        lat_rms = sem("lat_rms")
        squared = sem("squared")
        sq_summed = sem("sq_summed")
        head_summed = sem("head_summed")
        head_rooted = sem("head_rooted")
        qk_ready = sem("qk_ready")
        conv_done = sem("conv_done")
        z_squared = sem("z_squared")
        z_normed = sem("z_normed")
        conv_act = sem("conv_act")
        max_ready = sem("max_ready")
        pv_done = sem("pv_done")
        merged = sem("merged")
        ex_in = sem("ex_in")
        ex_out = sem("ex_out")
        onehot_ready = sem("onehot_ready")
        routed = sem("routed")
        ckv_ready = sem("ckv_ready")
        ckv_stored = sem("ckv_stored")
        pick_ready = sem("pick_ready")
        pickT_full = sem("pickT_full")
        pickT_taken = sem("pickT_taken")
        hg_full = sem("hg_full")
        hg_dve = sem("hg_dve")
        hid_full = sem("hid_full")
        silu_done = sem("silu_done")
        hm_ready = sem("hm_ready")
        hT_full = sem("hT_full")
        hT_taken = sem("hT_taken")
        w2_done = sem("w2_done")
        y_dve = sem("y_dve")
        back_full = sem("back_full")
        x_moe = sem("x_moe")
        x_stored = sem("x_stored")
        act_order = sem("act_order")
        dve_order = sem("dve_order")

        def pre_slot(n):
            return (ADA_FIRST + n) % SLOTS

        def landed16(eng, l, done):
            return eng.snap(l * (16 * (PRE_UNITS // SLOTS)) + done * (16 * (GROUP_UNITS // SLOTS)))

        def turns_in(n):
            return 16 * ((ADA_FIRST + n) // SLOTS + 1)

        def settle(eng):
            eng.sem_inc(settled, 1)

        def rounds_before(eng, l):
            settle(eng)
            return eng.value_load(before[0:1, bass.ts(l, 1)], min_val=0, max_val=3 * GROUPS * LAYERS)

        def passes(eng, l):
            settle(eng)
            return eng.value_load(rounds[0:1, bass.ts(l, 1)], min_val=1, max_val=3)

        def wait_full(eng, l, name, index=0):
            eng.wait_ge(psum_full, l * len(FULL_JOBS) + (FULL[(name, index)] + 1))

        def wait_taken(eng, l, name, index=0):
            who, n = TAKEN[(name, index)]
            eng.wait_ge(taken[who], l * N_TAKEN[who] + (n + 1))

        def ps_of(name, index=0):
            return ps[:, JOBS[JOB[(name, index)]][2], :]

        def splits_before(eng, l, done):
            return eng.snap(l * PRE_SPLITS + done * GROUP_UNITS)

        def wait_made(eng, base, n):
            eng.wait_ge(split_lo, base + (n + 2))

        def make_hi(eng, base, use16, n):
            at = PRE_AT[SPLIT[n]]
            eng.wait_ge(w_landed[pre_slot(at)], use16 + turns_in(at))
            if n >= PRE_PLACES and n < EARLY_SPLITS or n >= EARLY_SPLITS + PRE_PLACES:
                eng.wait_ge(split_used, base + (n - PRE_PLACES + 1))
            nc.scalar.activation(w_hi[n % PRE_PLACES], slot(pre_slot(at)), ACT.Copy).then_inc(split_hi, 1)

        def make_lo(eng, base, n):
            eng.wait_ge(split_hi, base + (n + 1))
            nc.vector.tensor_tensor(w_lo[n % PRE_PLACES], slot(pre_slot(PRE_AT[SPLIT[n]])),
                                    w_hi[n % PRE_PLACES].bitcast(F32), ALU.subtract).then_inc(split_lo, 1)

        def lower(out, whole, leading):
            return nc.vector.tensor_tensor(out, whole, leading.bitcast(F32), ALU.subtract)

        block = ctx.enter_context(nc.Block())

        @block.sync
        def _(sp):
            sp.dma_start(cond_sb[:, :, :], cond).then_inc(loaded, 16)
            sp.dma_start(const[:, :], const_in).then_inc(loaded, 16)
            for n in range(ADA_FIRST):
                if n >= SLOTS:
                    sp.wait_ge(raw_used, n - SLOTS + 1)
                sp.dma_start(slot(n % SLOTS), wfirst[n]).then_inc(w_landed[n % SLOTS], 16)
                if n == 3:
                    sp.dma_start(x[:, :, :], x0).then_inc(x_loaded, 16)
            sp.wait_ge(set_up, 1)
            n_raw = PRE_UNITS - PRE_SPLITS
            with sp.Fori(0, LAYERS) as l:
                done = rounds_before(sp, l)
                base = splits_before(sp, l, done)
                raw_base = sp.snap(l * n_raw)
                for n, e in enumerate(PRE):
                    if n < SLOTS:
                        sp.wait_ge(raw_used, raw_base + (ADA_FIRST - SLOTS + n + 1))
                        sp.wait_ge(split_lo, base + 1)
                    elif PRE[n - SLOTS] in SPLIT_AT:
                        sp.wait_ge(split_lo, base + (SPLIT_AT[PRE[n - SLOTS]] + 2))
                    else:
                        raw = sum(e not in SPLIT_AT for e in PRE[:n - SLOTS + 1])
                        sp.wait_ge(raw_used, raw_base + (ADA_FIRST + raw))
                    sp.dma_start(slot(pre_slot(n)), wpre[l, n]).then_inc(w_landed[pre_slot(n)], 16)

                def experts(i, g, layers_first=False):
                    split_base = splits_before(sp, l, i)
                    if layers_first:
                        sp.wait_ge(raw_used, raw_base + (ADA_FIRST + n_raw))
                        settle(sp)
                    for m in range(GROUP_UNITS):
                        back = 0 if layers_first and m < SLOTS else m - SLOTS + 1
                        sp.wait_ge(split_lo, split_base + (PRE_SPLITS + back + 1))
                        sp.dma_start(slot(pre_slot(m)), wmoe[l, g, m]).then_inc(w_landed[pre_slot(m)], 16)

                experts(done, 0, layers_first=True)
                with sp.Fori(1, GROUPS) as g:
                    experts(done + g, g)
                sp.wait_ge(routed, l + 1)
                n = passes(sp, l)
                with sp.If(n > 1):
                    with sp.Fori(1, n) as p:
                        with sp.Fori(0, GROUPS) as g:
                            experts(done + p * GROUPS + g, g)
                with sp.Else():
                    pass
            total = rounds_before(sp, LAYERS)
            sp.wait_ge(x_moe, total * KD + 1)
            sp.dma_start(x_out, x[:, :, :]).then_inc(x_stored, 16)
            sp.wait_ge(x_stored, 16)
            sp.wait_ge(ckv_stored, 32 * LAYERS)

        @block.gpsimd
        def _(pool):
            pool.dma_start(par, par_in[0]).then_inc(par_loaded, 16)
            with pool.Fori(0, LAYERS) as l:
                pool.wait_ge(ckv_ready, l + 1)
                pool.dma_start(ckv_out[l], ckvT[:, 0:CTX]).then_inc(ckv_stored, 16)
                pool.dma_start(kr_out[l], kr[:, 0, :]).then_inc(ckv_stored, 16)
                pool.wait_ge(routed, l + 1)
                pool.dma_start(par, par_in[l + 1]).then_inc(par_loaded, 16)
            pool.wait_ge(par_loaded, 16 * (LAYERS + 1))

        @block.tensor
        def _(pe):
            mm = nc.tensor.matmul
            held = []

            def first(ins):
                if held:
                    ins.then_inc(held.pop(0), 1)
                return ins

            def transposes(out, srcs):
                for n, src in enumerate(srcs):
                    m = nc.tensor.transpose(out[:, n * P:(n + 1) * P], src, ident)
                    if n == 0 and len(srcs) > 1:
                        first(m)
                return m

            def product(out, lhs, rhs):
                n = len(lhs)
                for i in range(n):
                    m = mm(out, lhs[i], rhs[i], start=(i == 0), stop=(i == n - 1))
                    if i == 0 and n > 1:
                        first(m)
                return m

            def split_product(out, lhs, rhs, start=True, stop=True):
                n = len(lhs)
                for i, ((lh, ll), (rh, rl)) in enumerate(zip(lhs, rhs)):
                    for j, (a, b) in enumerate(((lh, rh), (lh, rl), (ll, rh))):
                        m = mm(out, a, b, start=(start and i == 0 and j == 0), stop=(stop and i == n - 1 and j == 2))
                        if i == 0 and j == 0:
                            first(m)
                return m

            def ada_rows_of(w, out):
                w = v3(w, KD)
                for c in range(2):
                    for j in range(4):
                        m = mm(out[32 * j:32 * j + 32, 0:ADA_COLS], condp[:, 2 * j + c, :], w[:, 2 * j + c, :],
                               start=(c == 0), stop=(c == 1))
                        if c == 0 and j == 0:
                            first(m)
                return m

            def ada_columns(out, place):
                for c in range(2):
                    m = mm(out[:, 2 * c:2 * c + 2], ada_rows[:, place, c * P:(c + 1) * P], sel, start=True, stop=True)
                    if c == 0:
                        first(m)
                return m

            pe.wait_ge(loaded, 32)
            pe.wait_ge(condp_ready, 1)
            for n in range(ADA_FIRST + 1):
                if n < ADA_FIRST:
                    pe.wait_ge(w_landed[n % SLOTS], 16 * (n // SLOTS + 1))
                    if n >= 2:
                        pe.wait_ge(ada_taken, n - 1)
                    ada_rows_of(slot(n % SLOTS), ps[:, n % 2, :]).then_inc(ada_full, 1)
                if n:
                    pe.wait_ge(ada_taken, n)
                    if n > 2:
                        pe.wait_ge(adaT_taken, n - 2)
                    held.append(raw_used)
                    ada_columns(ps[:, 2 + n % 2, :], (n - 1) % 2).then_inc(adaT_full, 1)
            assert not held

            with pe.Fori(0, LAYERS) as l:
                done = rounds_before(pe, l)
                base = splits_before(pe, l, done)
                base16 = landed16(pe, l, done)
                ada_base = pe.snap(l * ADA_UNITS)
                stage = []

                def begin(name, index=0, source=None):
                    j = JOB[(name, index)]
                    bank = JOBS[j][2]
                    earlier = [(n, i) for n, i, b, _ in JOBS[:j] if b == bank][-1:] + ([source] if source else [])
                    last = {TAKEN[e][0]: e for e in sorted(earlier, key=lambda e: TAKEN[e][1])}
                    for e in last.values():
                        wait_taken(pe, l, *e)
                    return ps[:, bank, :]

                def raw_unit(kind, c):
                    at = PRE_AT[(kind, c)]
                    pe.wait_ge(w_landed[pre_slot(at)], base16 + turns_in(at))
                    return slot(pre_slot(at))

                def split_unit(kind, c, chunks, width=None):
                    n = SPLIT_AT[(kind, c)]
                    wait_made(pe, base, n)
                    used = chunks * width if width else UNIT
                    hi, lo = (v3(a[n % PRE_PLACES][:, 0:used], chunks) for a in (w_hi, w_lo))
                    return lambda a, b: [(hi[:, d, a:b], lo[:, d, a:b]) for d in range(chunks)]

                def pairs(hi, lo, chunks, a, b):
                    return [(hi[:, d, a:b], lo[:, d, a:b]) for d in range(chunks)]

                def ada(entry):
                    if stage:
                        last = stage.pop()
                        out = begin("adaT", last)
                        wait_taken(pe, l, "ada", last)
                        ada_columns(out, JOB_ADA[last] % 2).then_inc(psum_full, 1)
                    if entry is not None:
                        w = raw_unit(*entry)
                        out = begin("ada", entry)
                        ada_rows_of(w, out).then_inc(psum_full, 1)
                        held.append(raw_used)
                        stage.append(entry)

                def square_sum(which):
                    out = begin("ss", which)
                    for c in range(KD):
                        pe.wait_ge(sq_ready, l * 2 * KD + (which * KD + c + 1))
                        m = mm(out[:, 0:TOK], ones, h[:, c, :], start=(c == 0), stop=(c == KD - 1))
                        if c == 0:
                            first(m)
                    m.then_inc(psum_full, 1)

                square_sum(0)
                for e in adas_after("lat", 1):
                    ada(e)
                lat = split_unit("lat", 0, 4, LAT_W)(0, LAT_W) + split_unit("lat", 1, 4, LAT_W)(0, LAT_W)
                for t in range(TT):
                    out = begin("lat", t)
                    if t == 0:
                        pe.wait_ge(h_ready, l * KD + KD)
                    rows = pairs(h_hi, h_lo, KD, t * P, (t + 1) * P)
                    split_product(out[:, 0:LAT_W], rows, lat).then_inc(psum_full, 1)
                held.extend([split_used, split_used])
                tokens = pairs(h_hi, h_lo, KD, 0, TOK)
                for c in range(KC):
                    w = split_unit("glu", c, KD)
                    for half, name in enumerate(("glu_a", "glu_b")):
                        out = begin(name, c)
                        split_product(out[:, 0:TOK], w(half * P, (half + 1) * P), tokens).then_inc(psum_full, 1)
                    held.append(split_used)
                    for e in adas_after("glu", c):
                        ada(e)
                for c in range(3):
                    out = begin("latT", c, source=("lat", TT - 1))
                    transposes(out, [cq[:, t, c * P:(c + 1) * P] if c < 2 else ckv[:, t, :] for t in range(TT)]
                               ).then_inc(psum_full, 1)
                for c in range(KD):
                    w = split_unit("gate", c, KD)
                    for half in range(2):
                        out = begin("gate", 2 * c + half)
                        split_product(out[:, 0:TOK], w(half * P, (half + 1) * P), tokens).then_inc(psum_full, 1)
                    held.append(split_used)
                    for e in adas_after("gate", c):
                        ada(e)
                ada(None)
                w = raw_unit("uq", 0)
                for j in range(2 * TT):
                    t, half = divmod(j, 2)
                    out = begin("q", j, source=("latT", 1))
                    n = H * QK // 2
                    product(out[:, 0:n], [cqT[:, c, t * P:(t + 1) * P] for c in range(2)],
                            [w[:, c * H * QK + half * n:c * H * QK + (half + 1) * n] for c in range(2)]
                            ).then_inc(psum_full, 1)
                held.append(raw_used)
                w = raw_unit("ukv", 0)
                for t in range(KT):
                    for half, name in enumerate(("k", "v")):
                        out = begin(name, t, source=("latT", 2))
                        product(out[:, 0:512], [ckvT[:, t * P:(t + 1) * P]], [w[:, half * 512:(half + 1) * 512]]
                                ).then_inc(psum_full, 1)
                held.append(raw_used)
                out = begin("mean")
                pe.wait_ge(conv_done, l + 1)
                product(out[:, 0:Z_W], [ones] * KC, [z[:, c, :] for c in range(KC)]).then_inc(psum_full, 1)

                for n, (name, tiles) in enumerate((("qT", TT), ("kT", KT))):
                    pe.wait_ge(qk_ready, l * 2 + (n + 1))
                    for hd in range(H):
                        out = begin(name, hd)
                        transposes(out[0:QK, :], [q[:, t, hd, :] if n == 0 else k[:, t, hd, :] for t in range(tiles)]
                                   ).then_inc(psum_full, 1)

                def scores(i):
                    hd, t = divmod(i, TT)
                    out = begin("s", i, source=("kT", H - 1))
                    keys = kT[0:QK, hd, 0:CTX] if t == 0 else kT[0:QK, hd, CTX:KEYS]
                    n = CTX if t == 0 else LAT + PAST
                    product(out[:, 0:n], [qT[0:QK, hd, t * P:(t + 1) * P]], [keys]).then_inc(psum_full, 1)

                def weigh(i):
                    hd, t = divmod(i, TT)
                    n = 1 if t == 0 else KT - 1
                    out = begin("pT", i)
                    wait_taken(pe, l, "s", i)
                    for b in range(n):
                        m = nc.tensor.transpose(out[:, b * P:(b + 1) * P], probs[:, i % 3, b * P:(b + 1) * P], ident)
                    m.then_inc(psum_full, 1)
                    return hd, t, n

                def attend(i, hd, t, n):
                    wait_taken(pe, l, "pT", i)
                    k0 = 0 if t == 0 else 1
                    o_ps = ps[:, 5 + t, hd * VD:(hd + 1) * VD]
                    for b in range(n):
                        m = mm(o_ps, probsT[:, i % 2, b * P:(b + 1) * P], v[:, k0 + b, hd * VD:(hd + 1) * VD],
                               start=(b == 0), stop=(b == n - 1))
                    m.then_inc(pv_done, 1)

                for t in range(TT):
                    begin("o", t)
                last = None
                for i in range(H * TT + 2):
                    if i < H * TT:
                        scores(i)
                    if i >= 2:
                        turned = weigh(i - 2)
                        if last is not None:
                            attend(i - 3, *last)
                        last = turned
                    if i == 12:
                        out = begin("var")
                        pe.wait_ge(z_squared, l + 1)
                        product(out[:, 0:Z_W], [ones] * KC, [u[:, c, HALF:HALF + Z_W] for c in range(KC)]
                                ).then_inc(psum_full, 1)
                attend(H * TT - 1, *last)

                for c in range(4):
                    out = begin("oT", c, source=("o", TT - 1))
                    transposes(out, [o[:, t, c * P:(c + 1) * P] for t in range(TT)]).then_inc(psum_full, 1)

                def widen(name, units, rhs, wait):
                    per = KD // units
                    for n in range(units):
                        w = split_unit(name, n, len(rhs))
                        for c in range(per):
                            out = begin(name, n * per + c)
                            if n + c == 0:
                                wait()
                            split_product(out[:, 0:TOK], w(c * P, (c + 1) * P), rhs).then_inc(psum_full, 1)
                        held.append(split_used)
                        for e in adas_after(name, n):
                            ada(e)

                widen("wo", 2, pairs(oT_hi, oT_lo, 4, 0, TOK), lambda: wait_taken(pe, l, "oT", 3))
                widen("pw2", 2, pairs(cT_hi, cT_lo, KC, 0, TOK), lambda: pe.wait_ge(conv_act, l + 1))
                widen("wout", 4, pairs(h_hi, h_lo, KD, 0, TOK), lambda: pe.wait_ge(merged, l * KD + KD))
                ada(None)
                square_sum(1)
                out = begin("logit")
                for c in range(KD):
                    pe.wait_ge(h_raw, l * KD + (c + 1))
                    for t in range(TT):
                        m = mm(out[:, t * NR:(t + 1) * NR], h[:, c, t * P:(t + 1) * P], route_w[:, c, :],
                               start=(c + t == 0), stop=(c == KD - 1 and t == TT - 1))
                m.then_inc(psum_full, 1)
                for j in range(2 * TT):
                    t, half = divmod(j, 2)
                    out = begin("hrow", j)
                    transposes(out, [h[:, half * 4 + b, t * P:(t + 1) * P] for b in range(4)]).then_inc(psum_full, 1)
                    if j == RANK_AFTER:
                        out = begin("rank")
                        pe.wait_ge(onehot_ready, l + 1)
                        for t in range(TT + 1):
                            n = min(t + 1, TT)
                            m = product(out[:, t * 4:t * 4 + 4], [tri if j == t else ones for j in range(n)],
                                        [oh_g[:, j, :] for j in range(n)])
                        m.then_inc(psum_full, 1)
                assert not held

                pe.wait_ge(routed, l + 1)
                n = passes(pe, l)
                wait_taken(pe, l, "hrow", 2 * TT - 1)
                settle(pe)

                def gather(i, half):
                    if half == 0:
                        pe.wait_ge(pick_ready, i + 1)
                    for c in range(4):
                        out = ps[:, 4 + half, c * P:(c + 1) * P]
                        f = 4 * half + c
                        for t in range(TT):
                            for part, src in enumerate((hrow_hi, hrow_lo)):
                                m = mm(out, src[:, t, f * P:(f + 1) * P], pick[:, t, :],
                                       start=(t + part == 0), stop=(t == TT - 1 and part == 1))
                                if c + t + part == 0:
                                    first(m)
                    m.then_inc(hg_full, 1)
                    if half == 1:
                        product(ps[:, 7, FE:FE + EPG], [pick[:, t, :].bitcast(F32) for t in range(TT)],
                                [cw[:, t, :] for t in range(TT)]).then_inc(hg_full, 1)

                def group_round(i, last):
                    mbase = pe.snap(splits_before(pe, l, i) + PRE_SPLITS)
                    nxt = pe.snap(i + 1)

                    def up(e, half):
                        m = GROUP_AT[("up", e, half)]
                        wait_made(pe, mbase, m)
                        if e == 0:
                            pe.wait_ge(hg_dve, i * 3 + (half + 1))
                        if e >= 2 and half == 0:
                            pe.wait_ge(hm_ready, i * EPG + (e - 1))
                        hi, lo = v3(w_hi[m % MOE_PLACES], 4), v3(w_lo[m % MOE_PLACES], 4)
                        m = split_product(
                            ps[:, 2 + e % 2, :], [(hg_hi[:, 4 * half + d, :], hg_lo[:, 4 * half + d, :]) for d in range(4)],
                            [(hi[:, d, :], lo[:, d, :]) for d in range(4)], start=(half == 0), stop=(half == 1))
                        if half == 1:
                            m.then_inc(hid_full, 1)
                        held.append(split_used)

                    def turn(e):
                        pe.wait_ge(hm_ready, i * EPG + (e + 1))
                        if e < 2:
                            pe.wait_ge(pickT_taken, i + 1)
                        else:
                            pe.wait_ge(hT_taken, i * EPG + (e - 1))
                        transposes(ps[:, 6 + e % 2, :], [hm[:, e % 2, b * P:(b + 1) * P] for b in range(2)]
                                   ).then_inc(hT_full, 1)

                    def down(e):
                        m = GROUP_AT[("down", e, 0)]
                        wait_made(pe, mbase, m)
                        pe.wait_ge(hT_taken, i * EPG + (e + 1))
                        hi, lo = v3(w_hi[m % MOE_PLACES], 2), v3(w_lo[m % MOE_PLACES], 2)
                        for half in range(2):
                            a, b = half * 512, (half + 1) * 512
                            m = split_product(
                                ps[:, half, :], [(hT_hi[:, e % 2, c, :], hT_lo[:, e % 2, c, :]) for c in range(2)],
                                [(hi[:, c, a:b], lo[:, c, a:b]) for c in range(2)], start=(e == 0), stop=(e == EPG - 1))
                        m.then_inc(w2_done, 1)
                        held.append(split_used)

                    up(0, 0)
                    up(0, 1)
                    pe.wait_ge(x_moe, i * KD + 1)
                    transposes(ps[:, 6, :], [pick[:, t, :].bitcast(F32) for t in range(TT)]).then_inc(pickT_full, 1)
                    for e in range(EPG - 1):
                        up(e + 1, 0)
                        turn(e)
                        up(e + 1, 1)
                        down(e)
                    turn(EPG - 1)
                    if not last:
                        gather(nxt, 0)
                    down(EPG - 1)
                    if not last:
                        gather(nxt, 1)
                    for c, bank in enumerate(BACK_BANKS):
                        if c == 0:
                            pe.wait_ge(y_dve, i * 2 + 1)
                        if c == 2:
                            pe.wait_ge(y_dve, i * 2 + 2)
                        if not last and c in (1, 4):
                            pe.wait_ge(hg_dve, nxt * 3 + (1 if c == 1 else 3))
                        if c >= 6:
                            pe.wait_ge(x_moe, i * KD + (c - 4))
                        first(mm(ps[:, bank, 0:TOK], y_hi[:, c * P:(c + 1) * P], pickT, start=True, stop=False))
                        mm(ps[:, bank, 0:TOK], y_lo[:, c * P:(c + 1) * P], pickT, start=False, stop=True
                           ).then_inc(back_full, 1)
                    assert not held

                with pe.Fori(0, n) as p:
                    i0 = pe.snap(done + p * GROUPS)
                    pe.wait_ge(x_moe, i0 * KD + 1)
                    gather(i0, 0)
                    gather(i0, 1)
                    with pe.Fori(0, GROUPS - 1) as g:
                        group_round(pe.snap(i0 + g), last=False)
                    group_round(pe.snap(i0 + (GROUPS - 1)), last=True)

        @block.scalar
        def _(act):
            af = nc.scalar.activation
            count = [0]

            def chain(ins):
                count[0] += 1
                ins.then_inc(act_order, 1)
                act.wait_ge(act_order, count[0])

            def rewind():
                if count[0]:
                    act.sem_clear(act_order)
                    count[0] = 0

            act.wait_ge(loaded, 32)
            af(cond_sb[:, :, :], cond_sb[:, :, :], ACT.Silu).then_inc(cond_ready, 1)
            act.wait_ge(set_up, 1)

            with act.Fori(0, LAYERS) as l:
                done = rounds_before(act, l)
                base = splits_before(act, l, done)
                base16 = landed16(act, l, done)
                act.wait_ge(x_loaded, 16)
                act.wait_ge(x_moe, done * KD + 1)

                def hi(n):
                    make_hi(act, base, base16, n)

                def norm(which):
                    for c in range(KD):
                        if which == 1:
                            wait_taken(act, l, "wout", c)
                        af(h[:, c, :], x[:, c, :], ACT.Square).then_inc(sq_ready, 1)
                    if which == 0:
                        hi(0)
                        hi(1)
                    wait_full(act, l, "ss", which)
                    af(rs[:, 0:TOK], ps_of("ss", which)[:, 0:TOK], ACT.Sqrt, bias=eps[:, 0:1],
                       scale=1.0 / D).then_inc(taken["act"], 1)
                    act.wait_ge(gain2_ready if which else layer_set, l + 1)
                    for c in range(KD):
                        act.wait_ge(xn_ready, l * 2 * KD + (which * KD + c + 1))
                        out, done_sem = (h, h_raw) if which else (h_hi, h_hi_done)
                        for st, (a, b) in enumerate(((0, CTX), (CTX, TOK))):
                            m = af(out[:, c, a:b], h[:, c, a:b], ACT.Identity, bias=mod[:, 24 * which + c, st:st + 1])
                        m.then_inc(done_sem, 1)

                norm(0)
                hi(2)
                for t in range(TT):
                    wait_full(act, l, "lat", t)
                    src = ps_of("lat", t)
                    for n, (a, b) in enumerate(((0, QL), (QL, QL + KVL), (QL + KVL, QL + KVL + ROPE))):
                        dst = lat_ss[:, n * 3 + t:n * 3 + t + 1] if n < 2 else kr_ss[:, t:t + 1]
                        af(unused[:, t, a:b], src[:, a:b], ACT.Square, accum_out=dst)
                chain(af(unused[:, TT, 0:ROPE], pf("cache_kr"), ACT.Square, accum_out=kr_ss[:, TT:TT + 1]))
                af(lat_r[:, 0:3], lat_ss[:, 0:3], ACT.Sqrt, bias=eps[:, 0:1], scale=1.0 / QL)
                af(lat_r[:, 3:6], lat_ss[:, 3:6], ACT.Sqrt, bias=eps[:, 0:1], scale=1.0 / KVL).then_inc(lat_rms, 1)
                hi(3)
                hi(4)
                for c in range(KC):
                    wait_full(act, l, "glu_b", c)
                    if c >= 2:
                        wait_taken(act, l, "glu_a", c - 2)
                    af(sig[:, c % 2, :], ps_of("glu_b", c)[:, 0:TOK], ACT.Sigmoid).then_inc(taken["act"], 1)
                    hi(5 + c)
                for c in range(2 * KD):
                    wait_full(act, l, "gate", c)
                    af(gates[:, c, :], ps_of("gate", c)[:, 0:TOK], ACT.Sigmoid).then_inc(taken["act"], 1)
                    if c % 2 and 9 + c // 2 < EARLY_SPLITS:
                        hi(9 + c // 2)
                n_sq = 0
                for j in range(2 * TT):
                    t, half = divmod(j, 2)
                    wait_full(act, l, "q", j)
                    if n_sq >= 2:
                        act.wait_ge(sq_summed, l * 10 + (n_sq - 1))
                    src = ps_of("q", j)[:, 0:H * QK // 2]
                    af(scratch[:, n_sq % 2, 0:H * QK // 2], src, ACT.Square).then_inc(squared, 1)
                    af(q[:, t, half * 4:half * 4 + 4, :], src.rearrange("p (h d) -> p h d", h=4), ACT.Copy
                       ).then_inc(taken["act"], 1)
                    n_sq += 1
                act.wait_ge(head_summed, l * 2 + 1)
                af(head_r[:, 0:24], head_ss[:, 0:24], ACT.Sqrt, bias=eps[:, 1:2], scale=1.0).then_inc(head_rooted, 1)
                for t in range(KT):
                    wait_full(act, l, "k", t)
                    act.wait_ge(sq_summed, l * 10 + (n_sq - 1))
                    src = ps_of("k", t)
                    af(scratch[:, n_sq % 2, :], src, ACT.Square).then_inc(squared, 1)
                    af(k[:, t, :, 0:NOPE], src.rearrange("p (h d) -> p h d", h=H), ACT.Copy).then_inc(taken["act"], 1)
                    n_sq += 1
                    wait_full(act, l, "v", t)
                    af(v[:, t, :], ps_of("v", t), ACT.Copy).then_inc(taken["act"], 1)
                act.wait_ge(head_summed, l * 2 + 2)
                af(head_r[:, 0:32], head_ss[:, 0:32], ACT.Sqrt, bias=eps[:, 0:1], scale=1.0 / QK).then_inc(head_rooted, 1)
                for hd in range(H):
                    wait_full(act, l, "qT", hd)
                    af(qT[0:QK, hd, :], ps_of("qT", hd)[0:QK, 0:TOK], ACT.Copy).then_inc(taken["act"], 1)
                for hd in range(H):
                    wait_full(act, l, "kT", hd)
                    af(kT[0:QK, hd, :], ps_of("kT", hd)[0:QK, :], ACT.Copy).then_inc(taken["act"], 1)

                wait_taken(act, l, "mean")
                af(u[:, :, HALF:HALF + Z_W], z[:, :, :], ACT.Square).then_inc(z_squared, 1)

                def soft(i):
                    hd, t = divmod(i, TT)
                    n = CTX if t == 0 else LAT + PAST
                    if i >= 3:
                        wait_full(act, l, "pT", i - 3)
                    act.wait_ge(max_ready, l * H * TT + (i + 1))
                    af(probs[:, i % 3, 0:n], ps_of("s", i)[:, 0:n], ACT.Exp, bias=row_max[:, i:i + 1],
                       accum_out=row_sum[:, t * H + hd:t * H + hd + 1]).then_inc(taken["act"], 1)

                def copy_pT(i):
                    n = CTX if i % TT == 0 else LAT + PAST
                    wait_full(act, l, "pT", i)
                    act.wait_ge(pv_done, l * H * TT + (i - 1))
                    af(probsT[:, i % 2, 0:n], ps_of("pT", i)[:, 0:n], ACT.Copy).then_inc(taken["act"], 1)

                for i in range(H * TT + 2):
                    if i < H * TT:
                        soft(i)
                    if i >= 2 and i % 2:
                        copy_pT(i - 2)
                    if i == 12:
                        wait_full(act, l, "var")
                        af(rs[:, :], ps_of("var")[:, 0:Z_W], ACT.Sqrt, bias=eps[:, 0:1], scale=1.0 / DC
                           ).then_inc(taken["act"], 1)
                act.wait_ge(pv_done, l * H * TT + H * TT)
                hi(EARLY_SPLITS)
                for c in range(4):
                    wait_full(act, l, "oT", c)
                    af(oT_hi[:, c, :], ps_of("oT", c)[:, 0:TOK], ACT.Copy).then_inc(oT_hi_done, 1)
                hi(EARLY_SPLITS + 1)
                hi(EARLY_SPLITS + 2)
                act.wait_ge(z_normed, l + 1)
                for c in range(KC):
                    m = af(z[:, c, :], z[:, c, :], ACT.Silu, scale=pf("ln_g")[:, c:c + 1], bias=pf("ln_b")[:, c:c + 1])
                chain(m)
                for c in range(KC):
                    af(cT_hi[:, c, 0:CTX], z[:, c, 0:CTX], ACT.Copy)
                    af(cT_hi[:, c, CTX:TOK], z[:, c, Z_LAT:Z_W], ACT.Copy).then_inc(cT_hi_done, 1)
                hi(EARLY_SPLITS + 3)
                hi(EARLY_SPLITS + 4)
                for c in range(KD):
                    act.wait_ge(sum_raw, l * KD + (c + 1))
                    af(h_hi[:, c, :], gates[:, c, :], ACT.Copy).then_inc(sum_hi_done, 1)
                    if c == KD // 2 - 1:
                        hi(EARLY_SPLITS + 5)
                for n in range(EARLY_SPLITS + 6, PRE_SPLITS):
                    hi(n)
                norm(1)
                for j in range(2 * TT):
                    t, half = divmod(j, 2)
                    if j == 3:
                        act.wait_ge(ex_in, l + 1)
                        af(ex, ex, ACT.Exp).then_inc(ex_out, 1)
                    wait_full(act, l, "hrow", j)
                    af(hrow_hi[:, t, half * 512:(half + 1) * 512], ps_of("hrow", j), ACT.Copy).then_inc(hrow_hi_done, 1)

                act.wait_ge(routed, l + 1)
                n = passes(act, l)
                rewind()
                wait_taken(act, l, "hrow", 2 * TT - 1)
                settle(act)

                def gathered(i, half):
                    act.wait_ge(hg_full, i * 3 + (half + 1))
                    af(hg_hi[:, 4 * half:4 * half + 4, :], v3(ps[:, 4 + half, :], 4), ACT.Copy).then_inc(hg_hi_done, 1)

                def make_hi_of(i):
                    mbase = act.snap(splits_before(act, l, i) + PRE_SPLITS)
                    m16 = act.snap(landed16(act, l, i) + 16 * (PRE_UNITS // SLOTS))

                    def hi(m):
                        act.wait_ge(w_landed[pre_slot(m)], m16 + turns_in(m))
                        act.wait_ge(split_used, mbase + (m - MOE_PLACES + 1))
                        af(w_hi[m % MOE_PLACES], slot(pre_slot(m)), ACT.Copy).then_inc(split_hi, 1)

                    return hi

                def group_round(i, last):
                    hi = make_hi_of(i)
                    nxt = act.snap(i + 1)

                    def places(_):
                        act.wait_ge(pickT_full, i + 1)
                        af(pickT, ps[:, 6, 0:TOK], ACT.Copy).then_inc(pickT_taken, 1)

                    def silu(e):
                        act.wait_ge(hid_full, i * EPG + (e + 1))
                        if e >= 2:
                            act.wait_ge(hm_ready, i * EPG + (e - 1))
                        af(hs[:, e % 2, :], ps[:, 2 + e % 2, 0:FE], ACT.Silu).then_inc(silu_done, 1)

                    def hT(e):
                        act.wait_ge(hT_full, i * EPG + (e + 1))
                        if e >= 2:
                            act.wait_ge(w2_done, i * EPG + (e - 1))
                        af(hT_hi[:, e % 2, :, :], v3(ps[:, 6 + e % 2, 0:FE], 2), ACT.Copy).then_inc(hT_hi_done, 1)

                    def total(half):
                        act.wait_ge(w2_done, i * EPG + EPG)
                        af(y_hi[:, half * 512:(half + 1) * 512], ps[:, half, :], ACT.Copy).then_inc(y_hi_done, 1)

                    for kind, n in group_steps(last):
                        if kind == "gather":
                            gathered(nxt, n)
                        else:
                            {"split": hi, "places": places, "gate": silu, "turn": hT, "sum": total}[kind](n)

                with act.Fori(0, n) as p:
                    i0 = act.snap(done + p * GROUPS)
                    hi = make_hi_of(i0)
                    hi(0)
                    hi(1)
                    gathered(i0, 0)
                    gathered(i0, 1)
                    hi(2)
                    with act.Fori(0, GROUPS - 1) as g:
                        group_round(act.snap(i0 + g), last=False)
                    group_round(act.snap(i0 + (GROUPS - 1)), last=True)

        @block.vector
        def _(dve):
            vt = nc.vector.tensor_tensor
            vs = nc.vector.tensor_scalar
            stt = nc.vector.scalar_tensor_tensor
            copy = nc.vector.tensor_copy
            count = [0]

            def mark(ins):
                count[0] += 1
                ins.then_inc(dve_order, 1)
                return count[0]

            def chain(ins):
                mark(ins)
                dve.wait_ge(dve_order, count[0])

            def rewind():
                dve.wait_ge(dve_order, count[0])
                dve.sem_clear(dve_order)
                count[0] = 0

            mark(nc.vector.memset(eps[:, 0:1], EPS))
            mark(nc.vector.memset(eps[:, 1:2], EPS * QK))
            chain(nc.vector.memset(condp[:, :, :], 0.0))
            nc.vector.memset(before, 0).then_inc(set_up, 1)
            dve.wait_ge(loaded, 32)
            dve.wait_ge(cond_ready, 1)
            copy(condp[:, :, 0:2], cond_sb[:, :, :]).then_inc(condp_ready, 1)
            rewind()

            def add_bias(out, src, bias):
                return vt(out, v3(src, 2), bias.unsqueeze(2).broadcast_to([P, 2, 2]), ALU.add)

            for n in range(ADA_FIRST + 1):
                if n < ADA_FIRST:
                    dve.wait_ge(ada_full, n + 1)
                    if n >= 2:
                        dve.wait_ge(adaT_full, n - 1)
                    copy(ada_rows[:, n % 2, :], ps[:, n % 2, 0:ADA_COLS]).then_inc(ada_taken, 1)
                if n:
                    dve.wait_ge(adaT_full, n)
                    add_bias(mod_next[:, 2 * n - 2:2 * n, :], ps[:, 2 + n % 2, 0:4],
                             const[:, C_ADA + 2 * n - 2:C_ADA + 2 * n]).then_inc(adaT_taken, 1)
            dve.sem_inc(split_lo, 1)
            nc.vector.memset(best, 0.0).then_inc(x_moe, 1)
            dve.wait_ge(adaT_taken, ADA_FIRST)

            with dve.Fori(0, LAYERS) as l:
                done = rounds_before(dve, l)
                base = splits_before(dve, l, done)
                dve.wait_ge(par_loaded, l * 16 + 16)
                chain(copy(mod[:, 0:16, :], mod_next[:, :, :]))

                def gain(which, name):
                    return stt(amp[:, which, :, :], mod[:, 24 * which + 8:24 * which + 16, :], 1.0,
                               pf(name).unsqueeze(2).broadcast_to([P, KD, 2]), ALU.add, ALU.mult)

                gain(0, "norm1").then_inc(layer_set, 1)

                def lo(n):
                    make_lo(dve, base, n)

                stage = []

                def ada(entry):
                    if stage:
                        kind, n = last = stage.pop()
                        wait_full(dve, l, "adaT", last)
                        c = 2 * n
                        out = mod[:, c:c + 2, :] if kind == "ada" else mod_next[:, c:c + 2, :]
                        b0 = c - 16 if kind == "ada" else 32 + c
                        add_bias(out, ps_of("adaT", last)[:, 0:4], pf("b_ada")[:, b0:b0 + 2]).then_inc(taken["dve"], 1)
                    if entry is not None:
                        wait_full(dve, l, "ada", entry)
                        order = JOB_ADA[entry]
                        if order >= 2:
                            wait_full(dve, l, "adaT", ADA_ORDER[order - 2])
                        copy(ada_rows[:, order % 2, :], ps_of("ada", entry)[:, 0:ADA_COLS]).then_inc(taken["dve"], 1)
                        stage.append(entry)

                def norm(which):
                    wait_taken(dve, l, "ss", which)
                    chain(nc.vector.reciprocal(rs[:, 0:TOK], rs[:, 0:TOK]))
                    for c in range(KD):
                        for st, (a, b) in enumerate(((0, CTX), (CTX, TOK))):
                            m = stt(h[:, c, a:b], x[:, c, a:b], amp[:, which, c, st:st + 1], rs[:, a:b],
                                    ALU.mult, ALU.mult)
                        m.then_inc(xn_ready, 1)

                lo(0)
                lo(1)
                dve.wait_ge(layer_set, l + 1)
                norm(0)
                for c in range(KD):
                    dve.wait_ge(h_hi_done, l * KD + (c + 1))
                    for st, (a, b) in enumerate(((0, CTX), (CTX, TOK))):
                        m = stt(h_lo[:, c, a:b], h[:, c, a:b], mod[:, c, st:st + 1],
                                h_hi[:, c, a:b].bitcast(F32), ALU.add, ALU.subtract)
                    m.then_inc(h_ready, 1)
                    if c % 2:
                        ada(adas_after("lat", 1)[c // 2])
                chain(nc.vector.memset(u[:, :, :], 0.0))
                lo(2)
                dve.wait_ge(lat_rms, l + 1)
                chain(nc.vector.reciprocal(lat_r, lat_r))
                for t in range(TT):
                    src = ps_of("lat", t)
                    vs(cq[:, t, :], src[:, 0:QL], lat_r[:, t:t + 1], None, ALU.mult)
                    vs(ckv[:, t, :], src[:, QL:QL + KVL], lat_r[:, 3 + t:4 + t], None, ALU.mult)
                    copy(kr[:, t, :], src[:, QL + KVL:QL + KVL + ROPE]).then_inc(taken["dve"], 1)
                mark(copy(kr[:, TT, :], pf("cache_kr")))
                lo(3)
                lo(4)

                taps_done = [0] * KC
                last_tap = [0] * KC

                def conv_taps(chunks, n):
                    for _ in range(n):
                        c = min(range(chunks), key=lambda c: taps_done[c])
                        tap = taps_done[c]
                        if tap == TAPS:
                            return
                        src = u[:, c, tap:tap + Z_W]
                        if tap == 0:
                            wait_taken(dve, l, "glu_a", c)
                            m = vs(z[:, c, :], src, dw[:, c, 0:1], pf("dw_b")[:, c:c + 1], ALU.mult, ALU.add)
                        else:
                            dve.wait_ge(dve_order, last_tap[c])
                            m = stt(z[:, c, :], src, dw[:, c, tap:tap + 1], z[:, c, :], ALU.mult, ALU.add)
                        taps_done[c] += 1
                        if sum(taps_done) == KC * TAPS:
                            m.then_inc(conv_done, 1)
                        else:
                            last_tap[c] = mark(m)

                for c in range(KC):
                    wait_full(dve, l, "glu_a", c)
                    wait_taken(dve, l, "glu_b", c)
                    src = ps_of("glu_a", c)
                    vt(u[:, c, U_CTX:U_CTX + CTX], src[:, 0:CTX], sig[:, c % 2, 0:CTX], ALU.mult)
                    vt(u[:, c, U_LAT:U_LAT + LAT], src[:, CTX:TOK], sig[:, c % 2, CTX:TOK], ALU.mult
                       ).then_inc(taken["dve"], 1)
                    lo(5 + c)
                    for e in adas_after("glu", c):
                        ada(e)
                    conv_taps(c + 1, CONV_GLU[c])
                copy(ckvT[:, TOK:KEYS], pf("cache_ckv"))
                for c in range(3):
                    wait_full(dve, l, "latT", c)
                    part = pf("q_lora")[:, c:c + 1] if c < 2 else pf("kv_lora")
                    dst = cqT[:, c, :] if c < 2 else ckvT[:, 0:TOK]
                    vs(dst, ps_of("latT", c)[:, 0:TOK], part, None, ALU.mult).then_inc(taken["dve"], 1)
                wait_taken(dve, l, "latT", 2)
                nc.vector.memset(most, 0.0).then_inc(ckv_ready, 1)

                for c in range(KD):
                    if 9 + c < EARLY_SPLITS:
                        lo(9 + c)
                    for e in adas_after("gate", c):
                        ada(e)
                    conv_taps(KC, (KC * TAPS - CONV_EARLY + KD - 1) // KD)
                ada(None)

                def bc_head(a, n):
                    return a.unsqueeze(2).broadcast_to([P, a.shape[1], n])

                def bc_row(a, heads):
                    return a.unsqueeze(1).broadcast_to([P, heads, a.shape[1]])

                def rotate(rows, tile):
                    part = rows[:, :, NOPE:QK].rearrange("p h (a s f) -> p h a s f", a=2, s=2)
                    x1, x2 = part[:, :, :, 0, :], part[:, :, :, 1, :]
                    tmp = [scratch[:, 0, n * 128:(n + 1) * 128].rearrange("p (h a f) -> p h a f", h=H, a=2)
                           for n in range(4)]
                    cos, sin = (rope[:, tile, s, :, :].unsqueeze(1).broadcast_to([P, H, 2, NF]) for s in range(2))
                    vt(tmp[0], x1, cos, ALU.mult)
                    vt(tmp[1], x2, sin, ALU.mult)
                    vt(tmp[2], x2, cos, ALU.mult)
                    chain(vt(tmp[3], x1, sin, ALU.mult))
                    chain(vt(x1, tmp[0], tmp[1], ALU.subtract))
                    return vt(x2, tmp[2], tmp[3], ALU.add)

                for j in range(2 * TT):
                    dve.wait_ge(squared, l * 10 + (j + 1))
                    m = nc.vector.tensor_reduce(head_ss[:, j * 4:j * 4 + 4],
                                                scratch[:, j % 2, 0:H * QK // 2].rearrange("p (h d) -> p h d", h=4),
                                                AX_X, ALU.add)
                    m.then_inc(sq_summed, 1)
                mark(nc.vector.memset(low, 0.0))
                dve.wait_ge(sq_summed, l * 10 + 6)
                nc.vector.memset(most, 0.0).then_inc(head_summed, 1)
                dve.wait_ge(head_rooted, l * 2 + 1)
                chain(nc.vector.reciprocal(head_r[:, 0:24], head_r[:, 0:24]))
                wait_taken(dve, l, "q", 2 * TT - 1)
                for t in range(TT):
                    mark(vt(q[:, t, :, :], q[:, t, :, :], bc_head(head_r[:, t * 8:t * 8 + 8], QK), ALU.mult))
                last = count[0]
                for t in range(KT):
                    n = 2 * TT + t
                    dve.wait_ge(squared, l * 10 + (n + 1))
                    m = nc.vector.tensor_reduce(head_ss[:, t * 8:t * 8 + 8],
                                                scratch[:, n % 2, :].rearrange("p (h d) -> p h d", h=H), AX_X, ALU.add)
                    m.then_inc(sq_summed, 1)
                dve.wait_ge(sq_summed, l * 10 + 10)
                hs4 = head_ss.rearrange("p (t h) -> p t h", t=KT)
                vt(hs4, hs4, kr_ss.unsqueeze(2).broadcast_to([P, KT, H]), ALU.add).then_inc(head_summed, 1)
                dve.wait_ge(dve_order, last)
                for t in range(TT):
                    mark(vt(q[:, t, :, :], q[:, t, :, :], bc_row(pf("q_norm"), H), ALU.mult))
                dve.wait_ge(dve_order, count[0])
                dve.wait_ge(head_rooted, l * 2 + 2)
                chain(rotate(q[:, 1, :, :], 0))
                rotate(q[:, 2, :, :], 1).then_inc(qk_ready, 1)
                chain(nc.vector.reciprocal(head_r, head_r))
                wait_taken(dve, l, "k", KT - 1)
                for t in range(KT):
                    r8 = head_r[:, t * 8:t * 8 + 8]
                    mark(vt(k[:, t, :, 0:NOPE], k[:, t, :, 0:NOPE], bc_head(r8, NOPE), ALU.mult))
                    mark(vt(k[:, t, :, NOPE:QK], bc_row(kr[:, t, :], H), bc_head(r8, ROPE), ALU.mult))
                dve.wait_ge(dve_order, count[0])
                for t in range(KT):
                    mark(vt(k[:, t, :, :], k[:, t, :, :], bc_row(pf("k_norm"), H), ALU.mult))
                dve.wait_ge(dve_order, count[0])
                chain(rotate(k[:, 1, :, :], 0))
                rotate(k[:, 2, :, :], 1).then_inc(qk_ready, 1)

                wait_full(dve, l, "mean")
                for c in range(KC):
                    m = stt(z[:, c, :], ps_of("mean")[:, 0:Z_W], -1.0 / DC, z[:, c, :], ALU.mult, ALU.add)
                m.then_inc(taken["dve"], 1)

                def peak(i):
                    n = CTX if i % TT == 0 else LAT + PAST
                    wait_full(dve, l, "s", i)
                    nc.vector.tensor_reduce(row_max[:, i:i + 1], ps_of("s", i)[:, 0:n], AX_X, ALU.max, negate=True
                                            ).then_inc(max_ready, 1)

                def copy_pT(i):
                    n = CTX if i % TT == 0 else LAT + PAST
                    wait_full(dve, l, "pT", i)
                    if i >= 2:
                        dve.wait_ge(pv_done, l * H * TT + (i - 1))
                    copy(probsT[:, i % 2, 0:n], ps_of("pT", i)[:, 0:n]).then_inc(taken["dve"], 1)

                for i in range(H * TT + 2):
                    if i < H * TT:
                        peak(i)
                    if i >= 2 and i % 2 == 0:
                        copy_pT(i - 2)
                    if i == 14:
                        wait_taken(dve, l, "var")
                        chain(nc.vector.reciprocal(rs[:, :], rs[:, :]))
                        for c in range(KC):
                            m = vt(z[:, c, :], z[:, c, :], rs[:, :], ALU.mult)
                        m.then_inc(z_normed, 1)
                dve.wait_ge(pv_done, l * H * TT + H * TT)
                chain(nc.vector.reciprocal(row_sum, row_sum))
                for t in range(TT):
                    vt(o[:, t, :].rearrange("p (h d) -> p h d", h=H), ps[:, 5 + t, :].rearrange("p (h d) -> p h d", h=H),
                       bc_head(row_sum[:, t * H:(t + 1) * H], VD), ALU.mult).then_inc(taken["dve"], 1)
                lo(EARLY_SPLITS)
                dve.wait_ge(ckv_stored, l * 32 + 32)
                for c in range(4):
                    dve.wait_ge(oT_hi_done, l * 4 + (c + 1))
                    lower(oT_lo[:, c, :], ps_of("oT", c)[:, 0:TOK], oT_hi[:, c, :]).then_inc(taken["dve"], 1)
                lo(EARLY_SPLITS + 1)
                lo(EARLY_SPLITS + 2)
                for c in range(KC):
                    dve.wait_ge(cT_hi_done, l * KC + (c + 1))
                    lower(cT_lo[:, c, 0:CTX], z[:, c, 0:CTX], cT_hi[:, c, 0:CTX])
                    m = lower(cT_lo[:, c, CTX:TOK], z[:, c, Z_LAT:Z_W], cT_hi[:, c, CTX:TOK])
                m.then_inc(conv_act, 1)
                splits = iter(range(EARLY_SPLITS + 3, PRE_SPLITS))
                for c in range(KD):
                    wait_full(dve, l, "wo", c)
                    vt(gates[:, KD + c, :], gates[:, KD + c, :], ps_of("wo", c)[:, 0:TOK], ALU.mult
                       ).then_inc(taken["dve"], 1)
                    if c % 4 == 3:
                        lo(next(splits))
                        for e in adas_after("wo", c // 4):
                            ada(e)

                def finish_sum(c):
                    dve.wait_ge(sum_hi_done, l * KD + (c + 1))
                    lower(h_lo[:, c, :], gates[:, c, :], h_hi[:, c, :]).then_inc(merged, 1)

                for c in range(KD):
                    wait_full(dve, l, "pw2", c)
                    vt(gates[:, c, :], gates[:, c, :], ps_of("pw2", c)[:, 0:TOK], ALU.mult).then_inc(taken["dve"], 1)
                    wait_taken(dve, l, "pw2", c)
                    vt(gates[:, c, :], gates[:, c, :], gates[:, KD + c, :], ALU.add).then_inc(sum_raw, 1)
                    if c:
                        finish_sum(c - 1)
                    if c % 4 == 3:
                        if c == KD - 1:
                            finish_sum(c)
                        lo(next(splits))
                        for e in adas_after("pw2", c // 4):
                            ada(e)
                for c in range(KD):
                    wait_full(dve, l, "wout", c)
                    for st, (a, b) in enumerate(((0, CTX), (CTX, TOK))):
                        m = stt(x[:, c, a:b], ps_of("wout", c)[:, a:b], mod[:, 16 + c, st:st + 1], x[:, c, a:b],
                                ALU.mult, ALU.add)
                    m.then_inc(taken["dve"], 1)
                    if c % 2:
                        for n in splits:
                            lo(n)
                            break
                        for e in adas_after("wout", c // 2):
                            ada(e)
                gain(1, "norm2").then_inc(gain2_ready, 1)
                dve.wait_ge(gain2_ready, l + 1)
                ada(None)
                norm(1)

                def b4(a):
                    return a.unsqueeze(2).broadcast_to([P, TT, 4])

                def one_hot(dst, src, m):
                    chain(vt(tie, src, b4(m), ALU.is_ge))
                    chain(stt(tie, tie, -8.0, order4.unsqueeze(1).broadcast_to([P, TT, 4]), ALU.mult, ALU.add))
                    chain(nc.vector.tensor_reduce(low, tie, AX_X, ALU.min))
                    return vt(dst, tie, b4(low), ALU.is_equal)

                wait_full(dve, l, "logit")
                vt(lg, ps_of("logit")[:, 0:TT * NR].rearrange("p (t n) -> p t n", t=TT),
                   pf("route_b").unsqueeze(1).broadcast_to([P, TT, NR]), ALU.add).then_inc(taken["dve"], 1)
                wait_taken(dve, l, "logit")
                g_lg = lg[:, :, 0:GROUPS]
                chain(nc.vector.tensor_reduce(best, g_lg, AX_X, ALU.max))
                one_hot(oh_g, g_lg, best).then_inc(onehot_ready, 1)
                vt(ex[:, :, 0:4], g_lg, b4(best), ALU.subtract)
                dve.wait_ge(onehot_ready, l + 1)
                for t in range(TT):
                    own = tmp16[:, t * 16:(t + 1) * 16].rearrange("p (e g) -> p e g", e=EPG)
                    mark(vt(own, lg[:, t, GROUPS:NR].rearrange("p (g e) -> p e g", g=GROUPS),
                            oh_g[:, t, :].unsqueeze(1).broadcast_to([P, EPG, GROUPS]), ALU.mult))
                dve.wait_ge(dve_order, count[0])
                chain(nc.vector.tensor_reduce(e_own.rearrange("p t e -> p (t e)"),
                                              tmp16.rearrange("p (n g) -> p n g", g=GROUPS), AX_X, ALU.add))
                chain(nc.vector.tensor_reduce(m1, e_own, AX_X, ALU.max))
                chain(one_hot(oh_1, e_own, m1))
                chain(stt(e_rest, oh_1, -3.0e38, e_own, ALU.mult, ALU.add))
                chain(nc.vector.tensor_reduce(m2, e_rest, AX_X, ALU.max))
                vt(ex[:, :, 4], m2, m1, ALU.subtract).then_inc(ex_in, 1)
                chain(one_hot(oh_2, e_rest, m2))
                def rows_lo(js):
                    for j in js:
                        t, half = divmod(j, 2)
                        dve.wait_ge(hrow_hi_done, l * 2 * TT + (j + 1))
                        a, b = half * 512, (half + 1) * 512
                        lower(hrow_lo[:, t, a:b], ps_of("hrow", j), hrow_hi[:, t, a:b]).then_inc(taken["dve"], 1)

                rows_lo(range(RANK_AFTER + 1))
                wait_full(dve, l, "rank")
                rank = ps_of("rank")[:, 0:(TT + 1) * 4].rearrange("p (t n) -> p t n", n=4)
                chain(vt(tie, rank[:, 0:TT, :], oh_g, ALU.mult))
                chain(nc.vector.tensor_reduce(pos, tie, AX_X, ALU.add))
                nc.vector.tensor_reduce(most[:, 0:1], rank[:, TT, :], AX_X, ALU.max).then_inc(taken["dve"], 1)
                wait_taken(dve, l, "rank")
                chain(vs(most[:, 1:2], most[:, 0:1], float(P), 1.0, ALU.is_gt, ALU.add))
                chain(vs(most[:, 2:3], most[:, 0:1], float(2 * P), None, ALU.is_gt))
                chain(vt(most[:, 1:2], most[:, 1:2], most[:, 2:3], ALU.add))
                mark(copy(rounds[0:1, bass.ts(l, 1)], most[0:1, 1:2]))
                chain(copy(low[0:1, 0:1], before[0:1, bass.ts(l, 1)]))
                chain(stt(low[0:1, 1:2], most[0:1, 1:2], float(GROUPS), low[0:1, 0:1], ALU.mult, ALU.add))
                copy(before[0:1, bass.ds(l + 1, 1)], low[0:1, 1:2]).then_inc(routed, 1)

                rows_lo(range(RANK_AFTER + 1, 2 * TT))
                dve.wait_ge(ex_out, l + 1)
                mark(nc.vector.tensor_reduce(gw, ex[:, :, 0:4], AX_X, ALU.add))
                chain(vs(dn, ex[:, :, 4], 1.0, None, ALU.add))
                chain(vt(dn, dn, gw, ALU.mult))
                chain(nc.vector.reciprocal(v1, dn))
                chain(vt(v2, v1, ex[:, :, 4], ALU.mult))
                mark(vt(cw, oh_1, b4(v1), ALU.mult))
                chain(vt(cw2, oh_2, b4(v2), ALU.mult))
                chain(vt(cw, cw, cw2, ALU.add))
                dve.wait_ge(routed, l + 1)
                n = passes(dve, l)
                rewind()

                def make_pick(g):
                    for t in range(TT):
                        m = vs(pick[:, t, :], slot_no, pos[:, t:t + 1], oh_g[:, t, bass.ts(g, 1)],
                               ALU.is_equal, ALU.mult)
                    m.then_inc(pick_ready, 1)

                def gathered(i, half):
                    dve.wait_ge(hg_hi_done, i * 2 + (half + 1))
                    lower(hg_lo[:, 4 * half:4 * half + 4, :], v3(ps[:, 4 + half, :], 4),
                          hg_hi[:, 4 * half:4 * half + 4, :]).then_inc(hg_dve, 1)
                    if half == 1:
                        dve.wait_ge(hg_full, i * 3 + 3)
                        copy(cwg, ps[:, 7, FE:FE + EPG]).then_inc(hg_dve, 1)

                def make_lo_of(i):
                    mbase = dve.snap(splits_before(dve, l, i) + PRE_SPLITS)

                    def lo(m):
                        dve.wait_ge(split_hi, mbase + (m + 1))
                        lower(w_lo[m % MOE_PLACES], slot(pre_slot(m)), w_hi[m % MOE_PLACES]).then_inc(split_lo, 1)

                    return lo

                def group_round(i, g, last):
                    lo = make_lo_of(i)
                    nxt = dve.snap(i + 1)

                    def gated(e):
                        dve.wait_ge(silu_done, i * EPG + (e + 1))
                        if e == 0:
                            dve.wait_ge(hg_dve, i * 3 + 3)
                        if e >= 2:
                            dve.wait_ge(hT_full, i * EPG + (e - 1))
                        stt(hm[:, e % 2, :], hs[:, e % 2, :], cwg[:, e:e + 1], ps[:, 2 + e % 2, FE:2 * FE],
                            ALU.mult, ALU.mult).then_inc(hm_ready, 1)

                    def hT(e):
                        dve.wait_ge(hT_hi_done, i * EPG + (e + 1))
                        lower(hT_lo[:, e % 2, :, :], v3(ps[:, 6 + e % 2, 0:FE], 2), hT_hi[:, e % 2, :, :]
                              ).then_inc(hT_taken, 1)

                    def places(_):
                        if not last:
                            dve.wait_ge(pickT_full, i + 1)
                            make_pick(g_next)

                    def total(half):
                        dve.wait_ge(y_hi_done, i * 2 + (half + 1))
                        a, b = half * 512, (half + 1) * 512
                        lower(y_lo[:, a:b], ps[:, half, :], y_hi[:, a:b]).then_inc(y_dve, 1)

                    if not last:
                        g_next = dve.snap(g + 1)
                    for kind, n in group_steps(last):
                        if kind == "gather":
                            gathered(nxt, n)
                        else:
                            {"split": lo, "places": places, "gate": gated, "turn": hT, "sum": total}[kind](n)
                    for c, bank in enumerate(BACK_BANKS):
                        dve.wait_ge(back_full, i * KD + (c + 1))
                        for st, (a, b) in enumerate(((0, CTX), (CTX, TOK))):
                            m = stt(x[:, c, a:b], ps[:, bank, a:b], mod[:, 40 + c, st:st + 1], x[:, c, a:b],
                                    ALU.mult, ALU.add)
                        m.then_inc(x_moe, 1)
                    dve.wait_ge(x_moe, i * KD + (KD + 1))

                with dve.Fori(0, n) as p:
                    i0 = dve.snap(done + p * GROUPS)
                    make_pick(0)
                    lo = make_lo_of(i0)
                    lo(0)
                    lo(1)
                    gathered(i0, 0)
                    gathered(i0, 1)
                    lo(2)
                    with dve.Fori(0, GROUPS - 1) as g:
                        group_round(dve.snap(i0 + g), g, last=False)
                    group_round(dve.snap(i0 + (GROUPS - 1)), None, last=True)
                    chain(vs(pos, pos, -float(P), None, ALU.add))
                    rewind()


def _fold(w, cols):
    kk, n = w.shape
    return w.reshape(kk // P, P, n // cols, cols).transpose(2, 1, 0, 3).reshape(n // cols, P, kk // P * cols)


def _unit(a):
    out = np.zeros((P, UNIT), np.float32)
    out[:, :a.shape[1]] = a
    return out[None]


def _pre_units(w, l):
    w_in = w["w_in"][l]
    i0, i3 = 2 * DC, 2 * DC + LAT_W
    glu = w_in[:, :i0].reshape(D, 2, KC, P).transpose(0, 2, 1, 3).reshape(D, i0)
    latent = _fold(w_in[:, i0:i3], LAT_W).reshape(P, 2, 4 * LAT_W)
    ukv = w["w_ukv"][l].reshape(KVL, H, NOPE + VD)
    ukv = np.concatenate([ukv[:, :, :NOPE].reshape(KVL, -1), ukv[:, :, NOPE:].reshape(KVL, -1)], axis=1)
    by = {"lat": np.concatenate([_unit(latent[:, n]) for n in range(2)]), "glu": _fold(glu, 256),
          "gate": _fold(w_in[:, i3:], 256), "uq": _unit(_fold(w["w_uq"][l], H * QK)[0]), "ukv": _unit(ukv),
          "pw2": _fold(w["w_pw2"][l], 512), "wo": _fold(w["w_o"][l], 512), "wout": _fold(w["w_out"][l], 256),
          "ada": _fold(w["w_ada"][l], ADA_COLS), "next": _fold(w["w_ada"][(l + 1) % LAYERS], ADA_COLS)}
    return np.stack([by[kind][n] for kind, n in PRE])


def _moe_units(w, l):
    w13 = np.concatenate([w["w1"][l], w["w3"][l]], axis=2)
    up = w13.reshape(EXPERTS, 2, 4, P, 2 * FE).transpose(0, 1, 3, 2, 4).reshape(EXPERTS, 2, P, UNIT)
    down = w["w2"][l].reshape(EXPERTS, 2, P, D).transpose(0, 2, 1, 3).reshape(EXPERTS, P, UNIT)
    return np.stack([np.stack([up[g * EPG + e, half] if kind == "up" else down[g * EPG + e] for kind, e, half in GROUP])
                     for g in range(GROUPS)])


def _columns(a):
    return a.reshape(-1, P).T


def _params(w, l):
    row = lambda a: np.broadcast_to(a.reshape(1, -1), (P, a.size))
    route = np.concatenate([w["w_group"][l], w["w_expert"][l]], axis=1)
    parts = {
        "b_ada": np.concatenate([_columns(w["b_ada"][l])[:, 16:], _columns(w["b_ada"][(l + 1) % LAYERS])[:, :16]], axis=1),
        "norm1": _columns(w["norm1"][l]), "norm2": _columns(w["norm2"][l]),
        "dw": w["conv_dw"][l].reshape(TAPS, KC, P).transpose(2, 1, 0).reshape(P, -1),
        "dw_b": _columns(w["conv_dw_b"][l]), "ln_g": _columns(w["conv_ln_g"][l]), "ln_b": _columns(w["conv_ln_b"][l]),
        "q_lora": _columns(w["q_lora_norm"][l]), "kv_lora": _columns(w["kv_lora_norm"][l]),
        "q_norm": row(w["q_norm"][l]), "k_norm": row(w["k_norm"][l]),
        "route_b": row(np.concatenate([w["b_group"][l], w["b_expert"][l]])),
        "route_w": route.reshape(KD, P, NR).transpose(1, 0, 2).reshape(P, -1),
        "cache_ckv": w["cache_ckv"][0, l].T, "cache_kr": w["cache_krope"][0, l],
    }
    return np.concatenate([parts[n] for n, _ in _FIELDS], axis=1)


def _constants():
    c = np.zeros((P, C_ADA), np.float32)
    c[:, C_ID:C_ID + P] = np.eye(P)
    c[:, C_ONE:C_ONE + P] = 1.0
    c[:, C_TRI:C_TRI + P] = np.triu(np.ones((P, P)), 1)
    c[:, C_SLOT:C_SLOT + P] = np.arange(P)
    for s in range(2):
        c[s::32, C_SEL + s] = 1.0
    freqs = (np.float32(10000.0) ** (-np.arange(NF, dtype=np.float32) / np.float32(NF))).astype(np.float32)
    n = np.arange(LAT)
    ang = np.stack([(n // GRID_W).astype(np.float32)[:, None] * freqs, (n % GRID_W).astype(np.float32)[:, None] * freqs], 1)
    table = np.stack([np.cos(ang), np.sin(ang)], 1).reshape(2, P, 2 * 2 * NF)
    c[:, C_ROPE:C_ROPE + 64] = table.transpose(1, 0, 2).reshape(P, 64)
    c[:, C_ORD:C_ORD + 4] = np.arange(4)
    return c


def kernel(**inputs):
    import concourse.bacc as bacc
    from concourse.bass_utils import run_bass_kernel_spmd

    w = {n: np.asarray(a) for n, a in inputs.items()}
    tokens = np.concatenate([w["x_prompt"][0], w["x_sample"][0]], axis=0)
    arrays = {
        "wfirst": np.ascontiguousarray(_fold(w["w_ada"][0], ADA_COLS)[:ADA_FIRST]),
        "wpre": np.stack([_pre_units(w, l) for l in range(LAYERS)]),
        "wmoe": np.stack([_moe_units(w, l) for l in range(LAYERS)]),
        "x0": np.ascontiguousarray(tokens.reshape(TOK, KD, P).transpose(2, 1, 0)),
        "cond": np.ascontiguousarray(np.stack([_columns(w["c_ctx"]), _columns(w["c"][0])], axis=2)),
        "par_in": np.stack([_params(w, l % LAYERS) for l in range(LAYERS + 1)]),
        "const_in": np.concatenate([_constants(), _columns(w["b_ada"][0])[:, :16]], axis=1),
    }
    nc = bacc.Bacc("TRN2", target_bir_lowering=False, num_devices=1)
    args = [nc.dram_tensor(n, a.shape, F32, kind="ExternalInput").ap() for n, a in arrays.items()]
    outs = [("x_out", (P, KD, TOK)), ("ckv_out", (LAYERS, P, CTX)), ("kr_out", (LAYERS, CTX, ROPE))]
    args += [nc.dram_tensor(n, s, F32, kind="ExternalOutput").ap() for n, s in outs]
    build(nc, *args)
    r = run_bass_kernel_spmd(nc, [arrays], core_ids=[0]).results[0]
    y = r["x_out"].transpose(2, 1, 0).reshape(TOK, D)
    return (y[None, :CTX], y[None, CTX:], r["ckv_out"].transpose(0, 2, 1)[None], r["kr_out"][None])
```

```python
from contextlib import ExitStack

import numpy as np

import concourse.bass as bass
from concourse import mybir

F32 = mybir.dt.float32
I32 = mybir.dt.int32
F32R = mybir.dt.float32r
ALU = mybir.AluOpType
ACT = mybir.ActivationFunctionType
AX_X = mybir.AxisListType.X

P = 128
LAYERS = 2
D = 1024
KD = D // P
CTX, LAT, PAST = 128, 256, 128
TOK = CTX + LAT
TT = TOK // P
KEYS = TOK + PAST
KT = KEYS // P
GRID_W = 64
DC = 512
KC = DC // P
TAPS = 31
HALF = TAPS // 2
H, NOPE, ROPE, VD = 8, 64, 32, 64
QK = NOPE + ROPE
NF = ROPE // 4
QL, KVL = 256, 128
LAT_W = QL + KVL + ROPE
SMALL = 328
GROUPS, EPG = 4, 4
EXPERTS = GROUPS * EPG
FE = 256
EPS = 1e-6

U_CTX = HALF
U_LAT = HALF + CTX + HALF
U_W = U_LAT + LAT + HALF
Z_W = U_W - 2 * HALF
Z_LAT = CTX + HALF

UNIT = 2048
SLOTS = 6
ADA_UNITS = 6 * D * KD // UNIT
ADA_FIRST = 2 * D * KD // UNIT
ADA_COLS = UNIT // KD
ADA_HEAD = 4
LAT_ADA = (1, 3, 5)
NEXT_LAST = 2


def pre_stream():
    ada = iter(range(ADA_FIRST, ADA_UNITS))
    out = [("lat", 0), ("lat", 1)] + [("ada", next(ada)) for _ in range(ADA_HEAD)]
    for c in range(KC):
        out += [("glu", c), ("ada", next(ada))]
    out += [("uq", 0), ("ukv", 0)]
    for c in range(KD):
        out += [("gate", c), ("ada", next(ada))]
    nxt = iter(range(ADA_FIRST))
    for name in ("wo", "pw2"):
        for c in range(2):
            out += [(name, c), ("next", next(nxt))]
    for c in range(4):
        out.append(("wout", c))
        if c < 4 - NEXT_LAST:
            out.append(("next", next(nxt)))
    return out + [("next", n) for n in nxt]


PRE = pre_stream()
PRE_AT = {e: n for n, e in enumerate(PRE)}
PRE_UNITS = len(PRE)
GROUP_UNITS = 3 * EPG
SPLIT = [e for e in PRE if e[0] in ("lat", "glu", "gate", "wo", "pw2", "wout")]
SPLIT_AT = {e: n for n, e in enumerate(SPLIT)}
PRE_SPLITS = len(SPLIT)
EARLY_SPLITS = SPLIT_AT[("wo", 0)]
MOE_PLACES = 4


def place_of(n):
    if SPLIT_AT[("gate", 0)] <= n < EARLY_SPLITS:
        return (n - SPLIT_AT[("gate", 0)]) % 2
    return (n - EARLY_SPLITS) % 3 if n >= EARLY_SPLITS else n % 3


GROUP = [("up", 0, 0), ("up", 0, 1), ("up", 1, 0), ("up", 1, 1), ("down", 0, 0), ("up", 2, 0), ("up", 2, 1),
         ("down", 1, 0), ("up", 3, 0), ("up", 3, 1), ("down", 2, 0), ("down", 3, 0)]
GROUP_AT = {e: n for n, e in enumerate(GROUP)}

_FIELDS = [("b_ada", 48), ("norm1", KD), ("norm2", KD), ("dw", KC * TAPS), ("dw_b", KC), ("ln_g", KC),
           ("ln_b", KC), ("q_lora", QL // P), ("kv_lora", 1), ("q_norm", QK), ("k_norm", QK),
           ("route_b", GROUPS + EXPERTS), ("route_w", KD * (GROUPS + EXPERTS)),
           ("cache_ckv", PAST), ("cache_kr", ROPE)]
FIELD = {}
NPAR = 0
for _n, _w in _FIELDS:
    FIELD[_n] = (NPAR, NPAR + _w)
    NPAR += _w
NR = GROUPS + EXPERTS

C_ID, C_ONE, C_TRI, C_SLOT, C_SEL, C_ROPE, C_ORD, C_ADA = 0, 128, 256, 384, 512, 514, 514 + 64, 514 + 68
NCONST = C_ADA + 16

CONV_TMP = 2 * KD - 3
CONV_GLU = [0, 8, 8, 10]
CONV_GATES = [12, 6, 6, 6, 6, 6, 6, 9]
EXPERT_STEPS = [("split", 3), ("split", 4), ("places", 0), ("gate", 0), ("split", 5), ("turn", 0), ("split", 6),
                ("gate", 1), ("split", 7), ("split", 8), ("turn", 1), ("split", 9), ("gate", 2), ("split", 10),
                ("turn", 2), ("split", 11), ("gate", 3), ("split", 12), ("turn", 3), ("split", 13), ("gather", 0),
                ("split", 14), ("sum", 0), ("sum", 1), ("gather", 1)]
BACK_BANKS = (6, 4, 0, 1, 7, 5, 6, 4)


def group_steps(last):
    return [(kind, n) for kind, n in EXPERT_STEPS
            if not (last and (kind == "gather" or kind == "split" and n >= GROUP_UNITS))]


def adas_after(kind, c):
    n = PRE_AT[(kind, c)] + 1
    out = []
    while n < PRE_UNITS and PRE[n][0] in ("ada", "next"):
        out.append(PRE[n])
        n += 1
    return out


LATT_AFTER = 2


def pre_jobs():
    jobs = []

    def add(name, index, taker, bank=None):
        if bank is None:
            bank = add.next
            add.next = (add.next + 1) % add.banks
        jobs.append((name, index, bank, taker))

    turning = []

    def add_ada(entry):
        if turning:
            add("adaT", turning.pop(), "dve")
        if entry is not None:
            add("ada", entry, "dve")
            turning.append(entry)

    add.next, add.banks = 0, 5
    add("ss", 0, "act")
    for e in adas_after("lat", 1):
        add_ada(e)
    for t in range(TT):
        add("lat", t, "dve", 5 + t)
    add.next, add.banks = 0, 8
    for c in range(KC):
        add("glu_a", c, "dve")
        add("glu_b", c, "act")
        for e in adas_after("glu", c):
            add_ada(e)
        if c == LATT_AFTER:
            for n in range(3):
                add("latT", n, "dve")
    for j in range(2 * TT):
        add("q", j, "act")
    for t in range(KT):
        add("k", t, "act")
        add("v", t, "act")
    for c in range(KD):
        add("gate", 2 * c, "act")
        add("gate", 2 * c + 1, "act")
        for e in adas_after("gate", c):
            add_ada(e)
    add_ada(None)
    add("mean", 0, "dve")
    for h in range(H):
        add("qT", h, "act")
    add("var", 0, "act")
    for h in range(H):
        add("kT", h, "act")
    add.next, add.banks = 0, 5
    for i in range(H * TT + 2):
        if i < H * TT:
            add("s", i, "act")
        if i >= 2:
            add("pT", i - 2, "dve" if i % 2 == 0 else "act")
    for t in range(TT):
        add("o", t, "dve", 5 + t)
    add.next, add.banks = 0, 8
    for c in range(4):
        add("oT", c, "dve")
    for name, units, per in (("wo", 2, 4), ("pw2", 2, 4), ("wout", 4, 2)):
        for n in range(units):
            for c in range(per):
                add(name, n * per + c, "dve")
            if (name, n) != ("wout", 3):
                for e in adas_after(name, n):
                    add_ada(e)
    add_ada(None)
    add("ss", 1, "act")
    for e in adas_after("wout", 3):
        add_ada(e)
    add_ada(None)
    add("logit", 0, "dve")
    add("rank", 0, "dve")
    for j in range(2 * TT):
        add("hrow", j, "dve")
    return jobs


JOBS = pre_jobs()
JOB = {(n, i): k for k, (n, i, _, _) in enumerate(JOBS)}
FULL_JOBS = [j for j in JOBS if j[0] != "o"]
FULL = {(n, i): k for k, (n, i, _, _) in enumerate(FULL_JOBS)}
TAKEN = {}
for _who in ("act", "dve"):
    for _k, (_n, _i, _, _) in enumerate([j for j in JOBS if j[3] == _who]):
        TAKEN[(_n, _i)] = (_who, _k)
JOB_ADA = {e: n for n, e in enumerate(i for name, i, _, _ in JOBS if name == "ada")}
ADA_ORDER = list(JOB_ADA)
N_TAKEN = {who: sum(j[3] == who for j in JOBS) for who in ("act", "dve")}


def build(nc, wfirst, wpre, wmoe, x0, cond, par_in, const_in, x_out, ckv_out, kr_out):
    ctx = ExitStack()
    with ctx:
        def sem(name):
            return ctx.enter_context(nc.semaphore(name))

        def up32(n):
            return (n + 31) // 32 * 32

        where = [up32(nc.sbuf_base)]
        names = set()

        def place(name, n, dt=F32, at=None):
            assert name not in names
            names.add(name)
            if at is None:
                at = region(n)
            return nc.alloc_sbuf_tensor_at(name, [P, n], dt, offset=at)[:, :]

        def region(n):
            at = where[0]
            where[0] = up32(at + 4 * n)
            return at

        def v3(a, c):
            return a.rearrange("p (c n) -> p c n", c=c)

        ring = place("ring", SLOTS * UNIT)
        x = v3(place("x", KD * TOK), KD)
        par = place("par", NPAR)
        const = place("const", NCONST)
        cond_sb = v3(place("cond_sb", KD * 2), KD)
        condp = v3(place("condp", KD * 32), KD)
        ada_rows = v3(place("ada_rows", 2 * ADA_COLS), 2)
        mod_next = v3(place("mod_next", 16 * 2), 16)
        mod = v3(place("mod", 48 * 2), 48)
        amp = place("amp", 2 * KD * 2).rearrange("p (w c s) -> p w c s", w=2, c=KD)
        rs = place("rs", Z_W)
        kr = v3(place("kr", KT * ROPE), KT)
        small = place("small", SMALL)
        eps = place("eps", 2)
        counts = place("counts", 2 * LAYERS + 1, I32)
        rounds, before = counts[0:1, 0:LAYERS], counts[0:1, LAYERS:2 * LAYERS + 1]

        h_hi = v3(place("h_hi", KD * TOK, F32R), KD)
        h_lo = v3(place("h_lo", KD * TOK, F32R), KD)
        hrow_hi = h_hi.rearrange("p c n -> p (c n)").rearrange("p (t n) -> p t n", t=TT)
        hrow_lo = h_lo.rearrange("p c n -> p (c n)").rearrange("p (t n) -> p t n", t=TT)
        gates_at = region(2 * KD * TOK)
        gates = v3(place("gates", 2 * KD * TOK, at=gates_at), 2 * KD)
        h = gates[:, 0:KD, :]
        conv_tmp = v3(place("conv_tmp", 2 * Z_W, at=gates_at + 4 * CONV_TMP * TOK), 2)
        conv_at = region(KC * (U_W + Z_W) + 8)
        u = v3(place("u", KC * U_W, at=conv_at), KC)
        z = v3(place("z", KC * Z_W, at=up32(conv_at + 4 * KC * U_W)), KC)
        cT_hi = v3(place("cT_hi", KC * TOK, F32R, at=conv_at), KC)
        v_at = region(KT * H * VD)
        v = v3(place("v", KT * H * VD, at=v_at), KT)
        q_at = region(TT * H * QK)
        q = place("q", TT * H * QK, at=q_at).rearrange("p (t h d) -> p t h d", t=TT, h=H)
        k_at = region(KT * H * QK)
        k = place("k", KT * H * QK, at=k_at).rearrange("p (t h d) -> p t h d", t=KT, h=H)
        o_at = q_at + 4 * UNIT
        o = v3(place("o", TT * DC, at=o_at), TT)
        cT_lo = v3(place("cT_lo", KC * TOK, F32R, at=o_at + 4 * TT * DC), KC)
        assert o_at + 4 * (TT * DC + KC * TOK) <= k_at + 4 * KT * H * QK
        places_at = region(4 * UNIT)
        qT = v3(place("qT", H * TOK, at=places_at), H)
        kT = v3(place("kT", H * KEYS, at=places_at + 4 * H * TOK), H)
        w_hi = [place(f"w_hi{n}", UNIT, F32R, at=places_at + 4 * 2 * UNIT * n) for n in range(2)]
        w_lo = [place(f"w_lo{n}", UNIT, F32R, at=places_at + 4 * (2 * n + 1) * UNIT) for n in range(2)]
        w_hi.append(place("w_hi2", UNIT, F32R, at=v_at))
        w_lo.append(place("w_lo2", UNIT, F32R, at=q_at))
        w_hi.append(place("w_hi3", UNIT, F32R, at=o_at))
        w_lo.append(place("w_lo3", UNIT, F32R, at=conv_at))
        work_at = region(3 * TOK + 2 * TOK + KEYS + 1024)
        probs = v3(place("probs", 3 * TOK, at=work_at), 3)
        cq = v3(place("cq", TT * QL, at=work_at), TT)
        ckv = v3(place("ckv", TT * KVL, at=work_at + 4 * TT * QL), TT)
        probsT_at = work_at + 4 * 3 * TOK
        probsT = v3(place("probsT", 2 * TOK, at=probsT_at), 2)
        cqT = v3(place("cqT", 2 * TOK, at=probsT_at), 2)
        ckvT_at = probsT_at + 4 * 2 * TOK
        ckvT = place("ckvT", KEYS, at=ckvT_at)
        scratch_at = ckvT_at + 4 * KEYS
        scratch = v3(place("scratch", 1024, at=scratch_at), 2)
        sig = v3(place("sig", 2 * TOK, at=scratch_at), 2)
        oT_hi = v3(place("oT_hi", 4 * TOK, F32R, at=work_at), 4)
        oT_lo = v3(place("oT_lo", 4 * TOK, F32R, at=work_at + 4 * 4 * TOK), 4)
        hg_hi = v3(place("hg_hi", KD * P, F32R, at=gates_at), KD)
        hg_lo = v3(place("hg_lo", KD * P, F32R, at=gates_at + 4 * KD * P), KD)
        hs = v3(place("hs", 2 * FE, at=gates_at + 4 * (KD * TOK + UNIT)), 2)
        hm = v3(place("hm", 2 * FE, at=gates_at + 4 * (KD * TOK + UNIT + 2 * FE)), 2)
        y_hi = place("y_hi", D, F32R, at=work_at)
        y_lo = place("y_lo", D, F32R, at=work_at + 4 * D)
        hT_hi = place("hT_hi", 2 * FE, F32R, at=work_at + 4 * 2 * D).rearrange("p (s c n) -> p s c n", s=2, c=2)
        hT_lo = place("hT_lo", 2 * FE, F32R, at=work_at + 4 * (2 * D + 2 * FE)).rearrange("p (s c n) -> p s c n", s=2, c=2)
        pick = v3(place("pick", TT * P, F32R, at=work_at + 4 * (2 * D + 4 * FE)), TT)
        pickT = place("pickT", TOK, F32R, at=conv_at + 4 * UNIT)
        unused = v3(place("unused", 4 * LAT_W, at=k_at), 4)
        assert where[0] <= nc.sbuf_usable_end

        at = [0]

        def sm(n):
            at[0] += n
            return small[:, at[0] - n:at[0]]

        lat_ss = sm(6)
        kr_ss = sm(KT)
        lat_r = sm(6)
        head_r = sm(56)
        row_max = head_r[:, 0:H * TT]
        row_sum = head_r[:, H * TT:2 * H * TT]
        head_ss = sm(TT * NR)
        lg = v3(head_ss, TT)
        best = sm(TT)
        tie = v3(sm(TT * 4), TT)
        low = sm(TT)
        oh_g = v3(sm(TT * 4), TT)
        oh_sum = v3(sm(TT * 4), TT)
        oh_1 = v3(sm(TT * 4), TT)
        oh_2 = v3(sm(TT * 4), TT)
        ex = v3(sm(TT * 5), TT)
        e_own = v3(sm(TT * 4), TT)
        e_rest = v3(sm(TT * 4), TT)
        m1 = sm(TT)
        m2 = sm(TT)
        gw = sm(TT)
        dn = sm(TT)
        v1 = sm(TT)
        v2 = sm(TT)
        cw = v3(sm(TT * 4), TT)
        cw2 = v3(sm(TT * 4), TT)
        pos = sm(TT)
        most = sm(4)
        cwg = sm(4)
        assert at[0] <= SMALL
        tmp16 = scratch[:, 0, 0:TT * 16]

        ps = ctx.enter_context(nc.psum_tensor("ps", [P, 8, 512], F32))

        ident = const[:, C_ID:C_ID + P]
        ones = const[:, C_ONE:C_ONE + P]
        tri = const[:, C_TRI:C_TRI + P]
        slot_no = const[:, C_SLOT:C_SLOT + P]
        sel = const[:, C_SEL:C_SEL + 2]
        rope = const[:, C_ROPE:C_ROPE + 64].rearrange("p (t s a f) -> p t s a f", t=2, s=2, a=2)
        order4 = const[:, C_ORD:C_ORD + 4]

        def pf(name):
            a, b = FIELD[name]
            return par[:, a:b]

        route_w = pf("route_w").rearrange("p (c n) -> p c n", c=KD)
        dw = pf("dw").rearrange("p (c n) -> p c n", c=KC)

        def slot(s, n=1):
            return ring[:, s * UNIT:(s + n) * UNIT]

        loaded = sem("loaded")
        x_loaded = sem("x_loaded")
        u_cleared = sem("u_cleared")
        par_loaded = sem("par_loaded")
        w_landed = [sem(f"w_landed{s}") for s in range(SLOTS)]
        raw_used = sem("raw_used")
        set_up = sem("set_up")
        settled = sem("settled")
        cond_ready = sem("cond_ready")
        condp_ready = sem("condp_ready")
        ada_full = sem("ada_full")
        ada_taken = sem("ada_taken")
        adaT_full = sem("adaT_full")
        adaT_taken = sem("adaT_taken")
        split_hi = sem("split_hi")
        split_lo = sem("split_lo")
        split_used = sem("split_used")
        gain2_ready = sem("gain2_ready")
        h_raw = sem("h_raw")
        h_hi_done = sem("h_hi_done")
        oT_hi_done = sem("oT_hi_done")
        cT_hi_done = sem("cT_hi_done")
        sum_raw = sem("sum_raw")
        sum_hi_done = sem("sum_hi_done")
        hrow_hi_done = sem("hrow_hi_done")
        hT_hi_done = sem("hT_hi_done")
        hg_hi_done = sem("hg_hi_done")
        y_hi_done = sem("y_hi_done")
        layer_set = sem("layer_set")
        psum_full = sem("psum_full")
        taken = {"act": sem("psum_taken_by_act"), "dve": sem("psum_taken_by_dve")}
        sq_ready = sem("sq_ready")
        squares_added = sem("squares_added")
        xn_ready = sem("xn_ready")
        h_ready = sem("h_ready")
        lat_rms = sem("lat_rms")
        squared = sem("squared")
        sq_summed = sem("sq_summed")
        head_summed = sem("head_summed")
        head_rooted = sem("head_rooted")
        qk_ready = sem("qk_ready")
        conv_done = sem("conv_done")
        conv_pool_done = sem("conv_pool_done")
        pool_order = sem("pool_order")
        z_squared = sem("z_squared")
        z_normed = sem("z_normed")
        conv_act = sem("conv_act")
        max_ready = sem("max_ready")
        pv_done = sem("pv_done")
        merged = sem("merged")
        ex_in = sem("ex_in")
        ex_out = sem("ex_out")
        onehot_ready = sem("onehot_ready")
        routed = sem("routed")
        ckv_stored = sem("ckv_stored")
        pick_ready = sem("pick_ready")
        pickT_full = sem("pickT_full")
        pickT_taken = sem("pickT_taken")
        hg_full = sem("hg_full")
        hg_dve = sem("hg_dve")
        hid_full = sem("hid_full")
        silu_done = sem("silu_done")
        hm_ready = sem("hm_ready")
        hT_full = sem("hT_full")
        hT_taken = sem("hT_taken")
        w2_done = sem("w2_done")
        y_dve = sem("y_dve")
        back_full = sem("back_full")
        x_moe = sem("x_moe")
        x_stored = sem("x_stored")
        act_order = sem("act_order")
        dve_order = sem("dve_order")

        def pre_slot(n):
            return (ADA_FIRST + n) % SLOTS

        def landed16(eng, l, done):
            return eng.snap(l * (16 * (PRE_UNITS // SLOTS)) + done * (16 * (GROUP_UNITS // SLOTS)))

        def turns_in(n):
            return 16 * ((ADA_FIRST + n) // SLOTS + 1)

        def settle(eng):
            eng.sem_inc(settled, 1)

        def rounds_before(eng, l):
            settle(eng)
            return eng.value_load(before[0:1, bass.ts(l, 1)], min_val=0, max_val=3 * GROUPS * LAYERS)

        def passes(eng, l):
            settle(eng)
            return eng.value_load(rounds[0:1, bass.ts(l, 1)], min_val=1, max_val=3)

        def wait_full(eng, l, name, index=0):
            eng.wait_ge(psum_full, l * len(FULL_JOBS) + (FULL[(name, index)] + 1))

        def wait_taken(eng, l, name, index=0):
            who, n = TAKEN[(name, index)]
            eng.wait_ge(taken[who], l * N_TAKEN[who] + (n + 1))

        def ps_of(name, index=0):
            return ps[:, JOBS[JOB[(name, index)]][2], :]

        def splits_before(eng, l, done):
            return eng.snap(l * PRE_SPLITS + done * GROUP_UNITS)

        def wait_made(eng, base, n):
            eng.wait_ge(split_lo, base + (n + 2))

        def make_hi(eng, base, use16, n):
            at = PRE_AT[SPLIT[n]]
            eng.wait_ge(w_landed[pre_slot(at)], use16 + turns_in(at))
            earlier = [m for m in range(EARLY_SPLITS if n >= EARLY_SPLITS else 0, n) if place_of(m) == place_of(n)]
            if earlier:
                eng.wait_ge(split_used, base + (earlier[-1] + 1))
            nc.scalar.activation(w_hi[place_of(n)], slot(pre_slot(at)), ACT.Copy).then_inc(split_hi, 1)

        def make_lo(eng, base, n):
            eng.wait_ge(split_hi, base + (n + 1))
            nc.vector.tensor_tensor(w_lo[place_of(n)], slot(pre_slot(PRE_AT[SPLIT[n]])),
                                    w_hi[place_of(n)].bitcast(F32), ALU.subtract).then_inc(split_lo, 1)

        def lower(out, whole, leading):
            return nc.vector.tensor_tensor(out, whole, leading.bitcast(F32), ALU.subtract)

        block = ctx.enter_context(nc.Block())

        @block.sync
        def _(sp):
            sp.dma_start(cond_sb[:, :, :], cond).then_inc(loaded, 16)
            sp.dma_start(const[:, :], const_in).then_inc(loaded, 16)
            for n in range(ADA_FIRST):
                if n >= SLOTS:
                    sp.wait_ge(raw_used, n - SLOTS + 1)
                sp.dma_start(slot(n % SLOTS), wfirst[n]).then_inc(w_landed[n % SLOTS], 16)
                if n == 3:
                    sp.dma_start(x[:, :, :], x0).then_inc(x_loaded, 16)
            sp.wait_ge(set_up, 1)
            n_raw = PRE_UNITS - PRE_SPLITS
            with sp.Fori(0, LAYERS) as l:
                done = rounds_before(sp, l)
                base = splits_before(sp, l, done)
                raw_base = sp.snap(l * n_raw)
                for n, e in enumerate(PRE):
                    if n < SLOTS:
                        sp.wait_ge(raw_used, raw_base + (ADA_FIRST - SLOTS + n + 1))
                        sp.wait_ge(split_lo, base + 1)
                    elif PRE[n - SLOTS] in SPLIT_AT:
                        sp.wait_ge(split_lo, base + (SPLIT_AT[PRE[n - SLOTS]] + 2))
                    else:
                        raw = sum(e not in SPLIT_AT for e in PRE[:n - SLOTS + 1])
                        sp.wait_ge(raw_used, raw_base + (ADA_FIRST + raw))
                    sp.dma_start(slot(pre_slot(n)), wpre[l, n]).then_inc(w_landed[pre_slot(n)], 16)

                def experts(i, g, layers_first=False):
                    split_base = splits_before(sp, l, i)
                    if layers_first:
                        sp.wait_ge(raw_used, raw_base + (ADA_FIRST + n_raw))
                        settle(sp)
                    for m in range(GROUP_UNITS):
                        back = 0 if layers_first and m < SLOTS else m - SLOTS + 1
                        sp.wait_ge(split_lo, split_base + (PRE_SPLITS + back + 1))
                        sp.dma_start(slot(pre_slot(m)), wmoe[l, g, m]).then_inc(w_landed[pre_slot(m)], 16)

                experts(done, 0, layers_first=True)
                with sp.Fori(1, GROUPS) as g:
                    experts(done + g, g)
                sp.wait_ge(routed, l + 1)
                n = passes(sp, l)
                with sp.If(n > 1):
                    with sp.Fori(1, n) as p:
                        with sp.Fori(0, GROUPS) as g:
                            experts(done + p * GROUPS + g, g)
                with sp.Else():
                    pass
            total = rounds_before(sp, LAYERS)
            for c in range(0, KD, 2):
                sp.wait_ge(x_moe, total * KD + (c + 2))
                sp.dma_start(x_out[:, c:c + 2, :], x[:, c:c + 2, :]).then_inc(x_stored, 16)
            sp.wait_ge(x_stored, 16 * KD // 2)
            sp.wait_ge(ckv_stored, 32 * LAYERS)

        @block.gpsimd
        def _(pool):
            pool.dma_start(par, par_in[0]).then_inc(par_loaded, 16)
            with pool.Fori(0, LAYERS) as l:
                pool.wait_ge(squares_added, l * 2 + 1)
                settle(pool)
                nc.gpsimd.memset(u[:, :, :], 0.0).then_inc(u_cleared, 1)
                wait_taken(pool, l, "glu_a", 0)
                settle(pool)
                nc.gpsimd.tensor_scalar(z[:, 0, :], u[:, 0, 0:Z_W], dw[:, 0, 0:1], pf("dw_b")[:, 0:1], ALU.mult, ALU.add
                                        ).then_inc(pool_order, 1)
                for tap in range(1, TAPS):
                    if tap > 2:
                        pool.wait_ge(pool_order, 2 * tap - 3)
                    nc.gpsimd.tensor_scalar(conv_tmp[:, tap % 2, :], u[:, 0, tap:tap + Z_W], dw[:, 0, tap:tap + 1], None,
                                            ALU.mult).then_inc(pool_order, 1)
                    pool.wait_ge(pool_order, 2 * tap)
                    nc.gpsimd.tensor_tensor(z[:, 0, :], z[:, 0, :], conv_tmp[:, tap % 2, :], ALU.add
                                            ).then_inc(pool_order if tap < TAPS - 1 else conv_pool_done, 1)
                pool.wait_ge(pool_order, 2 * TAPS - 2)
                pool.sem_clear(pool_order)
                wait_taken(pool, l, "latT", 2)
                pool.dma_start(ckv_out[l], ckvT[:, 0:CTX]).then_inc(ckv_stored, 16)
                pool.dma_start(kr_out[l], kr[:, 0, :]).then_inc(ckv_stored, 16)
                pool.wait_ge(routed, l + 1)
                pool.dma_start(par, par_in[l + 1]).then_inc(par_loaded, 16)
            pool.wait_ge(par_loaded, 16 * (LAYERS + 1))

        @block.tensor
        def _(pe):
            mm = nc.tensor.matmul
            held = []

            def first(ins):
                if held:
                    ins.then_inc(held.pop(0), 1)
                return ins

            def transposes(out, srcs):
                for n, src in enumerate(srcs):
                    m = nc.tensor.transpose(out[:, n * P:(n + 1) * P], src, ident)
                    if n == 0 and len(srcs) > 1:
                        first(m)
                return m

            def product(out, lhs, rhs):
                n = len(lhs)
                for i in range(n):
                    m = mm(out, lhs[i], rhs[i], start=(i == 0), stop=(i == n - 1))
                    if i == 0 and n > 1:
                        first(m)
                return m

            def split_product(out, lhs, rhs, start=True, stop=True, await_chunk=None):
                n = len(lhs)
                for i, ((lh, ll), (rh, rl)) in enumerate(zip(lhs, rhs)):
                    if await_chunk is not None:
                        await_chunk(i)
                    for j, (a, b) in enumerate(((lh, rh), (lh, rl), (ll, rh))):
                        m = mm(out, a, b, start=(start and i == 0 and j == 0), stop=(stop and i == n - 1 and j == 2))
                        if i == 0 and j == 0:
                            first(m)
                return m

            def ada_rows_of(w, out):
                w = v3(w, KD)
                for c in range(2):
                    for j in range(4):
                        m = mm(out[32 * j:32 * j + 32, 0:ADA_COLS], condp[:, 2 * j + c, :], w[:, 2 * j + c, :],
                               start=(c == 0), stop=(c == 1))
                        if c == 0 and j == 0:
                            first(m)
                return m

            def ada_columns(out, place):
                for c in range(2):
                    m = mm(out[:, 2 * c:2 * c + 2], ada_rows[:, place, c * P:(c + 1) * P], sel, start=True, stop=True)
                    if c == 0:
                        first(m)
                return m

            pe.wait_ge(loaded, 32)
            pe.wait_ge(condp_ready, 1)
            for n in range(ADA_FIRST + 1):
                if n < ADA_FIRST:
                    pe.wait_ge(w_landed[n % SLOTS], 16 * (n // SLOTS + 1))
                    if n >= 2:
                        pe.wait_ge(ada_taken, n - 1)
                    ada_rows_of(slot(n % SLOTS), ps[:, n % 2, :]).then_inc(ada_full, 1)
                if n:
                    pe.wait_ge(ada_taken, n)
                    if n > 2:
                        pe.wait_ge(adaT_taken, n - 2)
                    held.append(raw_used)
                    ada_columns(ps[:, 2 + n % 2, :], (n - 1) % 2).then_inc(adaT_full, 1)
            assert not held

            with pe.Fori(0, LAYERS) as l:
                done = rounds_before(pe, l)
                base = splits_before(pe, l, done)
                base16 = landed16(pe, l, done)
                ada_base = pe.snap(l * ADA_UNITS)
                stage = []

                def begin(name, index=0, source=None):
                    j = JOB[(name, index)]
                    bank = JOBS[j][2]
                    earlier = [(n, i) for n, i, b, _ in JOBS[:j] if b == bank][-1:] + ([source] if source else [])
                    last = {TAKEN[e][0]: e for e in sorted(earlier, key=lambda e: TAKEN[e][1])}
                    for e in last.values():
                        wait_taken(pe, l, *e)
                    return ps[:, bank, :]

                def raw_unit(kind, c):
                    at = PRE_AT[(kind, c)]
                    pe.wait_ge(w_landed[pre_slot(at)], base16 + turns_in(at))
                    return slot(pre_slot(at))

                def split_unit(kind, c, chunks, width=None):
                    n = SPLIT_AT[(kind, c)]
                    wait_made(pe, base, n)
                    used = chunks * width if width else UNIT
                    hi, lo = (v3(a[place_of(n)][:, 0:used], chunks) for a in (w_hi, w_lo))
                    return lambda a, b: [(hi[:, d, a:b], lo[:, d, a:b]) for d in range(chunks)]

                def pairs(hi, lo, chunks, a, b):
                    return [(hi[:, d, a:b], lo[:, d, a:b]) for d in range(chunks)]

                def ada(entry):
                    if stage:
                        last = stage.pop()
                        out = begin("adaT", last)
                        wait_taken(pe, l, "ada", last)
                        ada_columns(out, JOB_ADA[last] % 2).then_inc(psum_full, 1)
                    if entry is not None:
                        w = raw_unit(*entry)
                        out = begin("ada", entry)
                        ada_rows_of(w, out).then_inc(psum_full, 1)
                        held.append(raw_used)
                        stage.append(entry)

                def square_sum(which):
                    out = begin("ss", which)
                    pe.wait_ge(squares_added, l * 2 + (which + 1))
                    mm(out[:, 0:TOK], ones, rs[:, 0:TOK], start=True, stop=True).then_inc(psum_full, 1)

                square_sum(0)
                units = adas_after("lat", 1)
                ada(units[0])
                outs = [begin("lat", t) for t in range(TT)]
                for c in range(KD):
                    if c % 4 == 0:
                        w = split_unit("lat", c // 4, 4, LAT_W)(0, LAT_W)
                    pe.wait_ge(h_ready, l * KD + (c + 1))
                    for t in range(TT):
                        m = split_product(outs[t][:, 0:LAT_W], pairs(h_hi, h_lo, KD, t * P, (t + 1) * P)[c:c + 1],
                                          w[c % 4:c % 4 + 1], start=(c == 0), stop=(c == KD - 1))
                        if c == KD - 1:
                            m.then_inc(psum_full, 1)
                    if c % 4 == 3:
                        held.append(split_used)
                    if c in LAT_ADA:
                        ada(units[LAT_ADA.index(c) + 1])
                tokens = pairs(h_hi, h_lo, KD, 0, TOK)
                for c in range(KC):
                    w = split_unit("glu", c, KD)
                    for half, name in enumerate(("glu_a", "glu_b")):
                        out = begin(name, c)
                        split_product(out[:, 0:TOK], w(half * P, (half + 1) * P), tokens).then_inc(psum_full, 1)
                    held.append(split_used)
                    for e in adas_after("glu", c):
                        ada(e)
                    if c == LATT_AFTER:
                        for n in range(3):
                            out = begin("latT", n, source=("lat", TT - 1))
                            transposes(out, [cq[:, t, n * P:(n + 1) * P] if n < 2 else ckv[:, t, :] for t in range(TT)]
                                       ).then_inc(psum_full, 1)
                w = raw_unit("uq", 0)
                for j in range(2 * TT):
                    t, half = divmod(j, 2)
                    out = begin("q", j, source=("latT", 1))
                    n = H * QK // 2
                    product(out[:, 0:n], [cqT[:, c, t * P:(t + 1) * P] for c in range(2)],
                            [w[:, c * H * QK + half * n:c * H * QK + (half + 1) * n] for c in range(2)]
                            ).then_inc(psum_full, 1)
                held.append(raw_used)
                w = raw_unit("ukv", 0)
                for t in range(KT):
                    for half, name in enumerate(("k", "v")):
                        out = begin(name, t, source=("latT", 2))
                        product(out[:, 0:512], [ckvT[:, t * P:(t + 1) * P]], [w[:, half * 512:(half + 1) * 512]]
                                ).then_inc(psum_full, 1)
                held.append(raw_used)
                for c in range(KD):
                    w = split_unit("gate", c, KD)
                    for half in range(2):
                        out = begin("gate", 2 * c + half)
                        split_product(out[:, 0:TOK], w(half * P, (half + 1) * P), tokens).then_inc(psum_full, 1)
                    held.append(split_used)
                    for e in adas_after("gate", c):
                        ada(e)
                ada(None)
                out = begin("mean")
                pe.wait_ge(conv_done, l + 1)
                pe.wait_ge(conv_pool_done, l + 1)
                product(out[:, 0:Z_W], [ones] * KC, [z[:, c, :] for c in range(KC)]).then_inc(psum_full, 1)

                for n, (name, tiles) in enumerate((("qT", TT), ("kT", KT))):
                    pe.wait_ge(qk_ready, l * 2 + (n + 1))
                    for hd in range(H):
                        out = begin(name, hd)
                        transposes(out[0:QK, :], [q[:, t, hd, :] if n == 0 else k[:, t, hd, :] for t in range(tiles)]
                                   ).then_inc(psum_full, 1)
                    if n == 0:
                        out = begin("var")
                        pe.wait_ge(z_squared, l + 1)
                        product(out[:, 0:Z_W], [ones] * KC, [u[:, c, HALF:HALF + Z_W] for c in range(KC)]
                                ).then_inc(psum_full, 1)

                def scores(i):
                    hd, t = divmod(i, TT)
                    out = begin("s", i, source=("kT", H - 1))
                    keys = kT[0:QK, hd, 0:CTX] if t == 0 else kT[0:QK, hd, CTX:KEYS]
                    n = CTX if t == 0 else LAT + PAST
                    product(out[:, 0:n], [qT[0:QK, hd, t * P:(t + 1) * P]], [keys]).then_inc(psum_full, 1)

                def weigh(i):
                    hd, t = divmod(i, TT)
                    n = 1 if t == 0 else KT - 1
                    out = begin("pT", i)
                    wait_taken(pe, l, "s", i)
                    for b in range(n):
                        m = nc.tensor.transpose(out[:, b * P:(b + 1) * P], probs[:, i % 3, b * P:(b + 1) * P], ident)
                    m.then_inc(psum_full, 1)
                    return hd, t, n

                def attend(i, hd, t, n):
                    wait_taken(pe, l, "pT", i)
                    k0 = 0 if t == 0 else 1
                    o_ps = ps[:, 5 + t, hd * VD:(hd + 1) * VD]
                    for b in range(n):
                        m = mm(o_ps, probsT[:, i % 2, b * P:(b + 1) * P], v[:, k0 + b, hd * VD:(hd + 1) * VD],
                               start=(b == 0), stop=(b == n - 1))
                    m.then_inc(pv_done, 1)

                for t in range(TT):
                    begin("o", t)
                last = None
                for i in range(H * TT + 2):
                    if i < H * TT:
                        scores(i)
                    if i >= 2:
                        turned = weigh(i - 2)
                        if last is not None:
                            attend(i - 3, *last)
                        last = turned
                attend(H * TT - 1, *last)

                for c in range(4):
                    out = begin("oT", c, source=("o", TT - 1))
                    transposes(out, [o[:, t, c * P:(c + 1) * P] for t in range(TT)]).then_inc(psum_full, 1)

                def widen(name, units, rhs, await_chunk):
                    per = KD // units
                    for n in range(units):
                        w = split_unit(name, n, len(rhs))
                        for c in range(per):
                            out = begin(name, n * per + c)
                            split_product(out[:, 0:TOK], w(c * P, (c + 1) * P), rhs,
                                          await_chunk=await_chunk if n + c == 0 else None).then_inc(psum_full, 1)
                        held.append(split_used)
                        if (name, n) != ("wout", 3):
                            for e in adas_after(name, n):
                                ada(e)

                widen("wo", 2, pairs(oT_hi, oT_lo, 4, 0, TOK), lambda i: wait_taken(pe, l, "oT", 3) if i == 0 else None)
                widen("pw2", 2, pairs(cT_hi, cT_lo, KC, 0, TOK), lambda i: pe.wait_ge(conv_act, l + 1) if i == 0 else None)
                widen("wout", 4, pairs(h_hi, h_lo, KD, 0, TOK), lambda i: pe.wait_ge(merged, l * KD + (i + 1)))
                ada(None)
                square_sum(1)
                for e in adas_after("wout", 3):
                    ada(e)
                ada(None)
                out = begin("logit")
                for c in range(KD):
                    pe.wait_ge(h_raw, l * KD + (c + 1))
                    for t in range(TT):
                        m = mm(out[:, t * NR:(t + 1) * NR], h[:, c, t * P:(t + 1) * P], route_w[:, c, :],
                               start=(c + t == 0), stop=(c == KD - 1 and t == TT - 1))
                m.then_inc(psum_full, 1)
                out = begin("rank")
                pe.wait_ge(onehot_ready, l + 1)
                n = TT * GROUPS
                mm(out[:, 0:n], tri, oh_g.rearrange("p t g -> p (t g)"), start=True, stop=False)
                mm(out[:, GROUPS:n], ones, oh_sum[:, 0:TT - 1, :].rearrange("p t g -> p (t g)"), start=False, stop=True)
                mm(out[:, n:n + GROUPS], ones, oh_sum[:, TT - 1, :], start=True, stop=True).then_inc(psum_full, 1)
                for j in range(2 * TT):
                    t, half = divmod(j, 2)
                    out = begin("hrow", j)
                    transposes(out, [h[:, half * 4 + b, t * P:(t + 1) * P] for b in range(4)]).then_inc(psum_full, 1)
                assert not held

                pe.wait_ge(routed, l + 1)
                n = passes(pe, l)
                wait_taken(pe, l, "hrow", 2 * TT - 1)
                settle(pe)

                def gather(i, half):
                    if half == 0:
                        pe.wait_ge(pick_ready, i + 1)
                    for c in range(4):
                        out = ps[:, 4 + half, c * P:(c + 1) * P]
                        f = 4 * half + c
                        for t in range(TT):
                            for part, src in enumerate((hrow_hi, hrow_lo)):
                                m = mm(out, src[:, t, f * P:(f + 1) * P], pick[:, t, :],
                                       start=(t + part == 0), stop=(t == TT - 1 and part == 1))
                                if c + t + part == 0:
                                    first(m)
                    m.then_inc(hg_full, 1)
                    if half == 1:
                        product(ps[:, 7, FE:FE + EPG], [pick[:, t, :].bitcast(F32) for t in range(TT)],
                                [cw[:, t, :] for t in range(TT)]).then_inc(hg_full, 1)

                def group_round(i, last):
                    mbase = pe.snap(splits_before(pe, l, i) + PRE_SPLITS)
                    nxt = pe.snap(i + 1)

                    def up(e, half):
                        m = GROUP_AT[("up", e, half)]
                        wait_made(pe, mbase, m)
                        if e == 0:
                            pe.wait_ge(hg_dve, i * 3 + (half + 1))
                        if e >= 2 and half == 0:
                            pe.wait_ge(hm_ready, i * EPG + (e - 1))
                        hi, lo = v3(w_hi[m % MOE_PLACES], 4), v3(w_lo[m % MOE_PLACES], 4)
                        m = split_product(
                            ps[:, 2 + e % 2, :], [(hg_hi[:, 4 * half + d, :], hg_lo[:, 4 * half + d, :]) for d in range(4)],
                            [(hi[:, d, :], lo[:, d, :]) for d in range(4)], start=(half == 0), stop=(half == 1))
                        if half == 1:
                            m.then_inc(hid_full, 1)
                        held.append(split_used)

                    def turn(e):
                        pe.wait_ge(hm_ready, i * EPG + (e + 1))
                        if e < 2:
                            pe.wait_ge(pickT_taken, i + 1)
                        else:
                            pe.wait_ge(hT_taken, i * EPG + (e - 1))
                        transposes(ps[:, 6 + e % 2, :], [hm[:, e % 2, b * P:(b + 1) * P] for b in range(2)]
                                   ).then_inc(hT_full, 1)

                    def down(e):
                        m = GROUP_AT[("down", e, 0)]
                        wait_made(pe, mbase, m)
                        pe.wait_ge(hT_taken, i * EPG + (e + 1))
                        hi, lo = v3(w_hi[m % MOE_PLACES], 2), v3(w_lo[m % MOE_PLACES], 2)
                        for half in range(2):
                            a, b = half * 512, (half + 1) * 512
                            m = split_product(
                                ps[:, half, :], [(hT_hi[:, e % 2, c, :], hT_lo[:, e % 2, c, :]) for c in range(2)],
                                [(hi[:, c, a:b], lo[:, c, a:b]) for c in range(2)], start=(e == 0), stop=(e == EPG - 1))
                        m.then_inc(w2_done, 1)
                        held.append(split_used)

                    up(0, 0)
                    up(0, 1)
                    pe.wait_ge(x_moe, i * KD + KD)
                    transposes(ps[:, 6, :], [pick[:, t, :].bitcast(F32) for t in range(TT)]).then_inc(pickT_full, 1)
                    for e in range(EPG - 1):
                        up(e + 1, 0)
                        turn(e)
                        up(e + 1, 1)
                        down(e)
                    turn(EPG - 1)
                    if not last:
                        gather(nxt, 0)
                    down(EPG - 1)
                    if not last:
                        gather(nxt, 1)
                    for c, bank in enumerate(BACK_BANKS):
                        if c == 0:
                            pe.wait_ge(y_dve, i * 2 + 1)
                        if c == 2:
                            pe.wait_ge(y_dve, i * 2 + 2)
                        if not last and c in (1, 4):
                            pe.wait_ge(hg_dve, nxt * 3 + (1 if c == 1 else 3))
                        if c >= 6:
                            pe.wait_ge(x_moe, i * KD + (KD + c - 5))
                        first(mm(ps[:, bank, 0:TOK], y_hi[:, c * P:(c + 1) * P], pickT, start=True, stop=False))
                        mm(ps[:, bank, 0:TOK], y_lo[:, c * P:(c + 1) * P], pickT, start=False, stop=True
                           ).then_inc(back_full, 1)
                    assert not held

                with pe.Fori(0, n) as p:
                    i0 = pe.snap(done + p * GROUPS)
                    pe.wait_ge(x_moe, i0 * KD + KD)
                    gather(i0, 0)
                    gather(i0, 1)
                    with pe.Fori(0, GROUPS - 1) as g:
                        group_round(pe.snap(i0 + g), last=False)
                    group_round(pe.snap(i0 + (GROUPS - 1)), last=True)

        @block.scalar
        def _(act):
            af = nc.scalar.activation
            count = [0]

            def chain(ins):
                count[0] += 1
                ins.then_inc(act_order, 1)
                act.wait_ge(act_order, count[0])

            def rewind():
                if count[0]:
                    act.sem_clear(act_order)
                    count[0] = 0

            act.wait_ge(loaded, 32)
            af(cond_sb[:, :, :], cond_sb[:, :, :], ACT.Silu).then_inc(cond_ready, 1)
            act.wait_ge(set_up, 1)

            with act.Fori(0, LAYERS) as l:
                done = rounds_before(act, l)
                base = splits_before(act, l, done)
                base16 = landed16(act, l, done)
                act.wait_ge(x_loaded, 16)

                def hi(n):
                    make_hi(act, base, base16, n)

                def norm(which):
                    for c in range(KD):
                        if which == 0:
                            act.wait_ge(x_moe, done * KD + (c + 1))
                        else:
                            wait_taken(act, l, "wout", c)
                        af(h[:, c, :], x[:, c, :], ACT.Square).then_inc(sq_ready, 1)
                    if which == 0:
                        hi(0)
                    wait_full(act, l, "ss", which)
                    af(rs[:, 0:TOK], ps_of("ss", which)[:, 0:TOK], ACT.Sqrt, bias=eps[:, 0:1],
                       scale=1.0 / D).then_inc(taken["act"], 1)
                    if which == 0:
                        hi(1)
                    act.wait_ge(gain2_ready if which else layer_set, l + 1)
                    for c in range(KD):
                        act.wait_ge(xn_ready, l * 2 * KD + (which * KD + c + 1))
                        out, done_sem = (h, h_raw) if which else (h_hi, h_hi_done)
                        for st, (a, b) in enumerate(((0, CTX), (CTX, TOK))):
                            m = af(out[:, c, a:b], h[:, c, a:b], ACT.Identity, bias=mod[:, 24 * which + c, st:st + 1],
                                   scale=amp[:, 1, c, st:st + 1] if which else 1.0)
                        m.then_inc(done_sem, 1)

                norm(0)
                hi(2)
                for t in range(TT):
                    wait_full(act, l, "lat", t)
                    src = ps_of("lat", t)
                    for n, (a, b) in enumerate(((0, QL), (QL, QL + KVL), (QL + KVL, QL + KVL + ROPE))):
                        dst = lat_ss[:, n * 3 + t:n * 3 + t + 1] if n < 2 else kr_ss[:, t:t + 1]
                        af(unused[:, t, a:b], src[:, a:b], ACT.Square, accum_out=dst)
                chain(af(unused[:, TT, 0:ROPE], pf("cache_kr"), ACT.Square, accum_out=kr_ss[:, TT:TT + 1]))
                af(lat_r[:, 0:3], lat_ss[:, 0:3], ACT.Sqrt, bias=eps[:, 0:1], scale=1.0 / QL)
                af(lat_r[:, 3:6], lat_ss[:, 3:6], ACT.Sqrt, bias=eps[:, 0:1], scale=1.0 / KVL).then_inc(lat_rms, 1)
                hi(3)
                hi(4)
                for c in range(KC):
                    wait_full(act, l, "glu_b", c)
                    if c >= 2:
                        wait_taken(act, l, "glu_a", c - 2)
                    af(sig[:, c % 2, :], ps_of("glu_b", c)[:, 0:TOK], ACT.Sigmoid).then_inc(taken["act"], 1)
                    if c < KC - 1:
                        hi(5 + c)
                n_sq = 0
                for j in range(2 * TT):
                    t, half = divmod(j, 2)
                    wait_full(act, l, "q", j)
                    if n_sq >= 2:
                        act.wait_ge(sq_summed, l * 10 + (n_sq - 1))
                    elif n_sq == 0:
                        wait_taken(act, l, "glu_a", KC - 1)
                    src = ps_of("q", j)[:, 0:H * QK // 2]
                    af(scratch[:, n_sq % 2, 0:H * QK // 2], src, ACT.Square).then_inc(squared, 1)
                    af(q[:, t, half * 4:half * 4 + 4, :], src.rearrange("p (h d) -> p h d", h=4), ACT.Copy
                       ).then_inc(taken["act"], 1)
                    n_sq += 1
                for t in range(KT):
                    wait_full(act, l, "k", t)
                    act.wait_ge(sq_summed, l * 10 + (n_sq - 1))
                    src = ps_of("k", t)
                    af(scratch[:, n_sq % 2, :], src, ACT.Square).then_inc(squared, 1)
                    af(k[:, t, :, 0:NOPE], src.rearrange("p (h d) -> p h d", h=H), ACT.Copy).then_inc(taken["act"], 1)
                    n_sq += 1
                    wait_full(act, l, "v", t)
                    af(v[:, t, :], ps_of("v", t), ACT.Copy).then_inc(taken["act"], 1)
                act.wait_ge(head_summed, l + 1)
                af(head_r[:, 0:24], head_ss[:, 0:24], ACT.Sqrt, bias=eps[:, 1:2], scale=1.0)
                af(head_r[:, 24:56], head_ss[:, 24:56], ACT.Sqrt, bias=eps[:, 0:1], scale=1.0 / QK).then_inc(head_rooted, 1)
                for c in range(2 * KD):
                    wait_full(act, l, "gate", c)
                    if c == CONV_TMP:
                        act.wait_ge(conv_pool_done, l + 1)
                    af(gates[:, c, :], ps_of("gate", c)[:, 0:TOK], ACT.Sigmoid).then_inc(taken["act"], 1)
                    if c % 2 and 8 + c // 2 < EARLY_SPLITS:
                        hi(8 + c // 2)
                for hd in range(H):
                    wait_full(act, l, "qT", hd)
                    af(qT[0:QK, hd, :], ps_of("qT", hd)[0:QK, 0:TOK], ACT.Copy).then_inc(taken["act"], 1)
                    if hd == 3:
                        wait_taken(act, l, "mean")
                        af(u[:, :, HALF:HALF + Z_W], z[:, :, :], ACT.Square).then_inc(z_squared, 1)
                wait_full(act, l, "var")
                af(rs[:, :], ps_of("var")[:, 0:Z_W], ACT.Sqrt, bias=eps[:, 0:1], scale=1.0 / DC).then_inc(taken["act"], 1)
                for hd in range(H):
                    wait_full(act, l, "kT", hd)
                    af(kT[0:QK, hd, :], ps_of("kT", hd)[0:QK, :], ACT.Copy).then_inc(taken["act"], 1)

                def soft(i):
                    hd, t = divmod(i, TT)
                    n = CTX if t == 0 else LAT + PAST
                    if i >= 3:
                        wait_full(act, l, "pT", i - 3)
                    act.wait_ge(max_ready, l * H * TT + (i + 1))
                    af(probs[:, i % 3, 0:n], ps_of("s", i)[:, 0:n], ACT.Exp, bias=row_max[:, i:i + 1],
                       accum_out=row_sum[:, t * H + hd:t * H + hd + 1]).then_inc(taken["act"], 1)

                def copy_pT(i):
                    n = CTX if i % TT == 0 else LAT + PAST
                    wait_full(act, l, "pT", i)
                    act.wait_ge(pv_done, l * H * TT + (i - 1))
                    af(probsT[:, i % 2, 0:n], ps_of("pT", i)[:, 0:n], ACT.Copy).then_inc(taken["act"], 1)

                for i in range(H * TT + 2):
                    if i < H * TT:
                        soft(i)
                    if i >= 2 and i % 2:
                        copy_pT(i - 2)
                act.wait_ge(pv_done, l * H * TT + H * TT)
                hi(EARLY_SPLITS)
                for c in range(4):
                    wait_full(act, l, "oT", c)
                    af(oT_hi[:, c, :], ps_of("oT", c)[:, 0:TOK], ACT.Copy).then_inc(oT_hi_done, 1)
                hi(EARLY_SPLITS + 1)
                hi(EARLY_SPLITS + 2)
                act.wait_ge(z_normed, l + 1)
                for c in range(KC):
                    m = af(z[:, c, :], z[:, c, :], ACT.Silu, scale=pf("ln_g")[:, c:c + 1], bias=pf("ln_b")[:, c:c + 1])
                chain(m)
                for c in range(KC):
                    af(cT_hi[:, c, 0:CTX], z[:, c, 0:CTX], ACT.Copy)
                    af(cT_hi[:, c, CTX:TOK], z[:, c, Z_LAT:Z_W], ACT.Copy).then_inc(cT_hi_done, 1)
                hi(EARLY_SPLITS + 3)
                hi(EARLY_SPLITS + 4)
                for c in range(KD):
                    act.wait_ge(sum_raw, l * KD + (c + 1))
                    af(h_hi[:, c, :], gates[:, c, :], ACT.Copy).then_inc(sum_hi_done, 1)
                    if c == KD // 2 - 1:
                        hi(EARLY_SPLITS + 5)
                for n in range(EARLY_SPLITS + 6, PRE_SPLITS):
                    hi(n)
                norm(1)
                for j in range(2 * TT):
                    t, half = divmod(j, 2)
                    if j == 0:
                        act.wait_ge(ex_in, l + 1)
                        af(ex, ex, ACT.Exp).then_inc(ex_out, 1)
                    wait_full(act, l, "hrow", j)
                    af(hrow_hi[:, t, half * 512:(half + 1) * 512], ps_of("hrow", j), ACT.Copy).then_inc(hrow_hi_done, 1)

                act.wait_ge(routed, l + 1)
                n = passes(act, l)
                rewind()
                wait_taken(act, l, "hrow", 2 * TT - 1)
                settle(act)

                def gathered(i, half):
                    act.wait_ge(hg_full, i * 3 + (half + 1))
                    af(hg_hi[:, 4 * half:4 * half + 4, :], v3(ps[:, 4 + half, :], 4), ACT.Copy).then_inc(hg_hi_done, 1)

                def make_hi_of(i):
                    mbase = act.snap(splits_before(act, l, i) + PRE_SPLITS)
                    m16 = act.snap(landed16(act, l, i) + 16 * (PRE_UNITS // SLOTS))

                    def hi(m):
                        act.wait_ge(w_landed[pre_slot(m)], m16 + turns_in(m))
                        act.wait_ge(split_used, mbase + (m - MOE_PLACES + 1))
                        af(w_hi[m % MOE_PLACES], slot(pre_slot(m)), ACT.Copy).then_inc(split_hi, 1)

                    return hi

                def group_round(i, last):
                    hi = make_hi_of(i)
                    nxt = act.snap(i + 1)

                    def places(_):
                        act.wait_ge(pickT_full, i + 1)
                        af(pickT, ps[:, 6, 0:TOK], ACT.Copy).then_inc(pickT_taken, 1)

                    def silu(e):
                        act.wait_ge(hid_full, i * EPG + (e + 1))
                        if e >= 2:
                            act.wait_ge(hm_ready, i * EPG + (e - 1))
                        af(hs[:, e % 2, :], ps[:, 2 + e % 2, 0:FE], ACT.Silu).then_inc(silu_done, 1)

                    def hT(e):
                        act.wait_ge(hT_full, i * EPG + (e + 1))
                        if e >= 2:
                            act.wait_ge(w2_done, i * EPG + (e - 1))
                        af(hT_hi[:, e % 2, :, :], v3(ps[:, 6 + e % 2, 0:FE], 2), ACT.Copy).then_inc(hT_hi_done, 1)

                    def total(half):
                        act.wait_ge(w2_done, i * EPG + EPG)
                        af(y_hi[:, half * 512:(half + 1) * 512], ps[:, half, :], ACT.Copy).then_inc(y_hi_done, 1)

                    for kind, n in group_steps(last):
                        if kind == "gather":
                            gathered(nxt, n)
                        else:
                            {"split": hi, "places": places, "gate": silu, "turn": hT, "sum": total}[kind](n)

                with act.Fori(0, n) as p:
                    i0 = act.snap(done + p * GROUPS)
                    hi = make_hi_of(i0)
                    hi(0)
                    hi(1)
                    gathered(i0, 0)
                    gathered(i0, 1)
                    hi(2)
                    with act.Fori(0, GROUPS - 1) as g:
                        group_round(act.snap(i0 + g), last=False)
                    group_round(act.snap(i0 + (GROUPS - 1)), last=True)

        @block.vector
        def _(dve):
            vt = nc.vector.tensor_tensor
            vs = nc.vector.tensor_scalar
            stt = nc.vector.scalar_tensor_tensor
            copy = nc.vector.tensor_copy
            count = [0]

            def mark(ins):
                count[0] += 1
                ins.then_inc(dve_order, 1)
                return count[0]

            def chain(ins):
                mark(ins)
                dve.wait_ge(dve_order, count[0])

            def rewind():
                dve.wait_ge(dve_order, count[0])
                dve.sem_clear(dve_order)
                count[0] = 0

            mark(nc.vector.memset(eps[:, 0:1], EPS))
            mark(nc.vector.memset(eps[:, 1:2], EPS * QK))
            chain(nc.vector.memset(condp[:, :, :], 0.0))
            nc.vector.memset(before, 0).then_inc(set_up, 1)
            dve.wait_ge(loaded, 32)
            dve.wait_ge(cond_ready, 1)
            copy(condp[:, :, 0:2], cond_sb[:, :, :]).then_inc(condp_ready, 1)
            rewind()

            def add_bias(out, src, bias):
                return vt(out, v3(src, 2), bias.unsqueeze(2).broadcast_to([P, 2, 2]), ALU.add)

            for n in range(ADA_FIRST + 1):
                if n < ADA_FIRST:
                    dve.wait_ge(ada_full, n + 1)
                    if n >= 2:
                        dve.wait_ge(adaT_full, n - 1)
                    copy(ada_rows[:, n % 2, :], ps[:, n % 2, 0:ADA_COLS]).then_inc(ada_taken, 1)
                if n:
                    dve.wait_ge(adaT_full, n)
                    add_bias(mod_next[:, 2 * n - 2:2 * n, :], ps[:, 2 + n % 2, 0:4],
                             const[:, C_ADA + 2 * n - 2:C_ADA + 2 * n]).then_inc(adaT_taken, 1)
            dve.sem_inc(split_lo, 1)
            dve.sem_inc(x_moe, KD)
            dve.wait_ge(adaT_taken, ADA_FIRST)

            with dve.Fori(0, LAYERS) as l:
                done = rounds_before(dve, l)
                base = splits_before(dve, l, done)
                def add_squares(which, c):
                    dve.wait_ge(sq_ready, l * 2 * KD + (which * KD + c + 1))
                    m = vt(rs[:, 0:TOK], h[:, 0, :] if c == 1 else rs[:, 0:TOK], h[:, c, :], ALU.add)
                    if c < KD - 1:
                        chain(m)
                    else:
                        m.then_inc(squares_added, 1)

                for c in range(1, KD):
                    add_squares(0, c)
                dve.wait_ge(par_loaded, l * 16 + 16)
                chain(copy(mod[:, 0:16, :], mod_next[:, :, :]))

                def gain(which, name):
                    return stt(amp[:, which, :, :], mod[:, 24 * which + 8:24 * which + 16, :], 1.0,
                               pf(name).unsqueeze(2).broadcast_to([P, KD, 2]), ALU.add, ALU.mult)

                gain(0, "norm1").then_inc(layer_set, 1)

                def lo(n):
                    make_lo(dve, base, n)

                stage = []

                def ada(entry):
                    if stage:
                        kind, n = last = stage.pop()
                        wait_full(dve, l, "adaT", last)
                        c = 2 * n
                        out = mod[:, c:c + 2, :] if kind == "ada" else mod_next[:, c:c + 2, :]
                        b0 = c - 16 if kind == "ada" else 32 + c
                        add_bias(out, ps_of("adaT", last)[:, 0:4], pf("b_ada")[:, b0:b0 + 2]).then_inc(taken["dve"], 1)
                    if entry is not None:
                        wait_full(dve, l, "ada", entry)
                        order = JOB_ADA[entry]
                        if order >= 2:
                            wait_full(dve, l, "adaT", ADA_ORDER[order - 2])
                        copy(ada_rows[:, order % 2, :], ps_of("ada", entry)[:, 0:ADA_COLS]).then_inc(taken["dve"], 1)
                        stage.append(entry)

                def norm(which, units, below=None):
                    wait_taken(dve, l, "ss", which)
                    chain(nc.vector.reciprocal(rs[:, 0:TOK], rs[:, 0:TOK]))
                    for c in range(KD):
                        if which == 0:
                            for st, (a, b) in enumerate(((0, CTX), (CTX, TOK))):
                                m = stt(h[:, c, a:b], x[:, c, a:b], amp[:, 0, c, st:st + 1], rs[:, a:b],
                                        ALU.mult, ALU.mult)
                        else:
                            m = vt(h[:, c, :], x[:, c, :], rs[:, 0:TOK], ALU.mult)
                        m.then_inc(xn_ready, 1)
                        if below is not None and c > 1:
                            below(c - 2)
                        if which == 0 and c == 2:
                            lo(1)
                        if c in units:
                            ada(units[c])

                lo(0)
                dve.wait_ge(layer_set, l + 1)
                units = adas_after("lat", 1)

                def below(c):
                    dve.wait_ge(h_hi_done, l * KD + (c + 1))
                    for st, (a, b) in enumerate(((0, CTX), (CTX, TOK))):
                        m = stt(h_lo[:, c, a:b], h[:, c, a:b], mod[:, c, st:st + 1],
                                h_hi[:, c, a:b].bitcast(F32), ALU.add, ALU.subtract)
                    m.then_inc(h_ready, 1)

                norm(0, {1: units[0], 5: units[1], 7: units[2]}, below)
                below(KD - 2)
                below(KD - 1)
                ada(units[3])
                lo(2)
                dve.wait_ge(lat_rms, l + 1)
                chain(nc.vector.reciprocal(lat_r, lat_r))
                for t in range(TT):
                    src = ps_of("lat", t)
                    vs(cq[:, t, :], src[:, 0:QL], lat_r[:, t:t + 1], None, ALU.mult)
                    vs(ckv[:, t, :], src[:, QL:QL + KVL], lat_r[:, 3 + t:4 + t], None, ALU.mult)
                    copy(kr[:, t, :], src[:, QL + KVL:QL + KVL + ROPE]).then_inc(taken["dve"], 1)
                mark(copy(kr[:, TT, :], pf("cache_kr")))
                lo(3)
                lo(4)

                taps_done = [TAPS] + [0] * (KC - 1)
                last_tap = [0] * KC

                def conv_taps(chunks, n):
                    for _ in range(n):
                        c = min(range(1, chunks), key=lambda c: taps_done[c])
                        tap = taps_done[c]
                        if tap == TAPS:
                            return
                        src = u[:, c, tap:tap + Z_W]
                        if tap == 0:
                            wait_taken(dve, l, "glu_a", c)
                            m = vs(z[:, c, :], src, dw[:, c, 0:1], pf("dw_b")[:, c:c + 1], ALU.mult, ALU.add)
                        else:
                            dve.wait_ge(dve_order, last_tap[c])
                            m = stt(z[:, c, :], src, dw[:, c, tap:tap + 1], z[:, c, :], ALU.mult, ALU.add)
                        taps_done[c] += 1
                        if sum(taps_done) == KC * TAPS:
                            m.then_inc(conv_done, 1)
                        else:
                            last_tap[c] = mark(m)

                dve.wait_ge(u_cleared, l + 1)
                for c in range(KC):
                    wait_full(dve, l, "glu_a", c)
                    wait_taken(dve, l, "glu_b", c)
                    src = ps_of("glu_a", c)
                    vt(u[:, c, U_CTX:U_CTX + CTX], src[:, 0:CTX], sig[:, c % 2, 0:CTX], ALU.mult)
                    vt(u[:, c, U_LAT:U_LAT + LAT], src[:, CTX:TOK], sig[:, c % 2, CTX:TOK], ALU.mult
                       ).then_inc(taken["dve"], 1)
                    for e in adas_after("glu", c):
                        ada(e)
                    if c == LATT_AFTER:
                        mark(copy(ckvT[:, TOK:KEYS], pf("cache_ckv")))
                        for n in range(3):
                            wait_full(dve, l, "latT", n)
                            part = pf("q_lora")[:, n:n + 1] if n < 2 else pf("kv_lora")
                            dst = cqT[:, n, :] if n < 2 else ckvT[:, 0:TOK]
                            vs(dst, ps_of("latT", n)[:, 0:TOK], part, None, ALU.mult).then_inc(taken["dve"], 1)
                    if c:
                        conv_taps(c + 1, CONV_GLU[c])
                    if c < KC - 1:
                        lo(5 + c)

                def bc_head(a, n):
                    return a.unsqueeze(2).broadcast_to([P, a.shape[1], n])

                def bc_row(a, heads):
                    return a.unsqueeze(1).broadcast_to([P, heads, a.shape[1]])

                def rotate(rows, tile):
                    part = rows[:, :, NOPE:QK].rearrange("p h (a s f) -> p h a s f", a=2, s=2)
                    x1, x2 = part[:, :, :, 0, :], part[:, :, :, 1, :]
                    tmp = [scratch[:, 0, n * 128:(n + 1) * 128].rearrange("p (h a f) -> p h a f", h=H, a=2)
                           for n in range(4)]
                    cos, sin = (rope[:, tile, s, :, :].unsqueeze(1).broadcast_to([P, H, 2, NF]) for s in range(2))
                    vt(tmp[0], x1, cos, ALU.mult)
                    vt(tmp[1], x2, sin, ALU.mult)
                    vt(tmp[2], x2, cos, ALU.mult)
                    chain(vt(tmp[3], x1, sin, ALU.mult))
                    chain(vt(x1, tmp[0], tmp[1], ALU.subtract))
                    return vt(x2, tmp[2], tmp[3], ALU.add)

                for j in range(2 * TT):
                    dve.wait_ge(squared, l * 10 + (j + 1))
                    nc.vector.tensor_reduce(head_ss[:, j * 4:j * 4 + 4],
                                            scratch[:, j % 2, 0:H * QK // 2].rearrange("p (h d) -> p h d", h=4),
                                            AX_X, ALU.add).then_inc(sq_summed, 1)
                    conv_taps(KC, 1)
                for t in range(KT):
                    n = 2 * TT + t
                    dve.wait_ge(squared, l * 10 + (n + 1))
                    nc.vector.tensor_reduce(head_ss[:, 24 + t * 8:32 + t * 8],
                                            scratch[:, n % 2, :].rearrange("p (h d) -> p h d", h=H), AX_X, ALU.add
                                            ).then_inc(sq_summed, 1)
                    conv_taps(KC, 1)
                dve.wait_ge(sq_summed, l * 10 + 10)
                hs4 = head_ss[:, 24:56].rearrange("p (t h) -> p t h", t=KT)
                vt(hs4, hs4, kr_ss.unsqueeze(2).broadcast_to([P, KT, H]), ALU.add).then_inc(head_summed, 1)

                def divide_queries():
                    dve.wait_ge(head_rooted, l + 1)
                    chain(nc.vector.reciprocal(head_r, head_r))
                    for t in range(TT):
                        mark(vt(q[:, t, :, :], q[:, t, :, :], bc_head(head_r[:, t * 8:t * 8 + 8], QK), ALU.mult))

                def gain_queries():
                    dve.wait_ge(dve_order, count[0])
                    for t in range(TT):
                        mark(vt(q[:, t, :, :], q[:, t, :, :], bc_row(pf("q_norm"), H), ALU.mult))

                def rotate_rows(rows):
                    dve.wait_ge(dve_order, count[0])
                    chain(rotate(rows[:, 1, :, :], 0))
                    rotate(rows[:, 2, :, :], 1).then_inc(qk_ready, 1)

                def divide_keys():
                    dve.wait_ge(qk_ready, l * 2 + 1)
                    for t in range(KT):
                        r8 = head_r[:, 24 + t * 8:32 + t * 8]
                        mark(vt(k[:, t, :, 0:NOPE], k[:, t, :, 0:NOPE], bc_head(r8, NOPE), ALU.mult))
                        mark(vt(k[:, t, :, NOPE:QK], bc_row(kr[:, t, :], H), bc_head(r8, ROPE), ALU.mult))

                def gain_keys():
                    dve.wait_ge(dve_order, count[0])
                    for t in range(KT):
                        mark(vt(k[:, t, :, :], k[:, t, :, :], bc_row(pf("k_norm"), H), ALU.mult))

                steps = [None, divide_queries, gain_queries, lambda: rotate_rows(q), divide_keys, gain_keys,
                         lambda: rotate_rows(k), None]
                for c in range(KD):
                    if steps[c] is not None:
                        steps[c]()
                    conv_taps(KC, CONV_GATES[c])
                    if 8 + c < EARLY_SPLITS:
                        lo(8 + c)
                    for e in adas_after("gate", c):
                        ada(e)
                ada(None)
                assert sum(taps_done) == KC * TAPS

                wait_full(dve, l, "mean")
                for c in range(KC):
                    m = stt(z[:, c, :], ps_of("mean")[:, 0:Z_W], -1.0 / DC, z[:, c, :], ALU.mult, ALU.add)
                m.then_inc(taken["dve"], 1)
                wait_taken(dve, l, "var")
                chain(nc.vector.reciprocal(rs[:, :], rs[:, :]))
                wait_taken(dve, l, "mean")
                for c in range(KC):
                    m = vt(z[:, c, :], z[:, c, :], rs[:, :], ALU.mult)
                m.then_inc(z_normed, 1)

                def peak(i):
                    n = CTX if i % TT == 0 else LAT + PAST
                    wait_full(dve, l, "s", i)
                    nc.vector.tensor_reduce(row_max[:, i:i + 1], ps_of("s", i)[:, 0:n], AX_X, ALU.max, negate=True
                                            ).then_inc(max_ready, 1)

                def copy_pT(i):
                    n = CTX if i % TT == 0 else LAT + PAST
                    wait_full(dve, l, "pT", i)
                    if i >= 2:
                        dve.wait_ge(pv_done, l * H * TT + (i - 1))
                    copy(probsT[:, i % 2, 0:n], ps_of("pT", i)[:, 0:n]).then_inc(taken["dve"], 1)

                for i in range(H * TT + 2):
                    if i < H * TT:
                        peak(i)
                    if i >= 2 and i % 2 == 0:
                        copy_pT(i - 2)
                dve.wait_ge(pv_done, l * H * TT + H * TT)
                chain(nc.vector.reciprocal(row_sum, row_sum))
                for t in range(TT):
                    vt(o[:, t, :].rearrange("p (h d) -> p h d", h=H), ps[:, 5 + t, :].rearrange("p (h d) -> p h d", h=H),
                       bc_head(row_sum[:, t * H:(t + 1) * H], VD), ALU.mult).then_inc(taken["dve"], 1)
                lo(EARLY_SPLITS)
                dve.wait_ge(ckv_stored, l * 32 + 32)
                for c in range(4):
                    dve.wait_ge(oT_hi_done, l * 4 + (c + 1))
                    lower(oT_lo[:, c, :], ps_of("oT", c)[:, 0:TOK], oT_hi[:, c, :]).then_inc(taken["dve"], 1)
                lo(EARLY_SPLITS + 1)
                lo(EARLY_SPLITS + 2)
                for c in range(KC):
                    dve.wait_ge(cT_hi_done, l * KC + (c + 1))
                    lower(cT_lo[:, c, 0:CTX], z[:, c, 0:CTX], cT_hi[:, c, 0:CTX])
                    m = lower(cT_lo[:, c, CTX:TOK], z[:, c, Z_LAT:Z_W], cT_hi[:, c, CTX:TOK])
                m.then_inc(conv_act, 1)
                splits = iter(range(EARLY_SPLITS + 3, PRE_SPLITS))
                for c in range(KD):
                    wait_full(dve, l, "wo", c)
                    vt(gates[:, KD + c, :], gates[:, KD + c, :], ps_of("wo", c)[:, 0:TOK], ALU.mult
                       ).then_inc(taken["dve"], 1)
                    if c % 4 == 3:
                        lo(next(splits))
                        for e in adas_after("wo", c // 4):
                            ada(e)

                def finish_sum(c):
                    dve.wait_ge(sum_hi_done, l * KD + (c + 1))
                    lower(h_lo[:, c, :], gates[:, c, :], h_hi[:, c, :]).then_inc(merged, 1)

                for c in range(KD):
                    wait_full(dve, l, "pw2", c)
                    vt(gates[:, c, :], gates[:, c, :], ps_of("pw2", c)[:, 0:TOK], ALU.mult).then_inc(taken["dve"], 1)
                    wait_taken(dve, l, "pw2", c)
                    vt(gates[:, c, :], gates[:, c, :], gates[:, KD + c, :], ALU.add).then_inc(sum_raw, 1)
                    if c:
                        finish_sum(c - 1)
                    if c % 4 == 3:
                        if c == KD - 1:
                            finish_sum(c)
                        lo(next(splits))
                        for e in adas_after("pw2", c // 4):
                            ada(e)
                for c in range(KD):
                    wait_full(dve, l, "wout", c)
                    for st, (a, b) in enumerate(((0, CTX), (CTX, TOK))):
                        m = stt(x[:, c, a:b], ps_of("wout", c)[:, a:b], mod[:, 16 + c, st:st + 1], x[:, c, a:b],
                                ALU.mult, ALU.add)
                    m.then_inc(taken["dve"], 1)
                    if c > 1:
                        add_squares(1, c - 1)
                    if c % 2:
                        for n in splits:
                            lo(n)
                            break
                        if c < KD - 1:
                            for e in adas_after("wout", c // 2):
                                ada(e)
                add_squares(1, KD - 1)
                gain(1, "norm2").then_inc(gain2_ready, 1)
                dve.wait_ge(gain2_ready, l + 1)
                ada(None)
                units = adas_after("wout", 3)
                ada(units[0])
                norm(1, {2: units[1], 6: None})

                def b4(a):
                    return a.unsqueeze(2).broadcast_to([P, TT, 4])

                def one_hot(dst, src, m):
                    chain(vt(tie, src, b4(m), ALU.is_ge))
                    chain(stt(tie, tie, -8.0, order4.unsqueeze(1).broadcast_to([P, TT, 4]), ALU.mult, ALU.add))
                    chain(nc.vector.tensor_reduce(low, tie, AX_X, ALU.min))
                    return vt(dst, tie, b4(low), ALU.is_equal)

                wait_full(dve, l, "logit")
                vt(lg, ps_of("logit")[:, 0:TT * NR].rearrange("p (t n) -> p t n", t=TT),
                   pf("route_b").unsqueeze(1).broadcast_to([P, TT, NR]), ALU.add).then_inc(taken["dve"], 1)
                wait_taken(dve, l, "logit")
                g_lg = lg[:, :, 0:GROUPS]
                chain(nc.vector.tensor_reduce(best, g_lg, AX_X, ALU.max))
                chain(one_hot(oh_g, g_lg, best))
                chain(copy(oh_sum[:, 0, :], oh_g[:, 0, :]))
                chain(vt(oh_sum[:, 1, :], oh_sum[:, 0, :], oh_g[:, 1, :], ALU.add))
                vt(oh_sum[:, 2, :], oh_sum[:, 1, :], oh_g[:, 2, :], ALU.add).then_inc(onehot_ready, 1)
                vt(ex[:, :, 0:4], g_lg, b4(best), ALU.subtract)
                for t in range(TT):
                    own = tmp16[:, t * 16:(t + 1) * 16].rearrange("p (e g) -> p e g", e=EPG)
                    mark(vt(own, lg[:, t, GROUPS:NR].rearrange("p (g e) -> p e g", g=GROUPS),
                            oh_g[:, t, :].unsqueeze(1).broadcast_to([P, EPG, GROUPS]), ALU.mult))
                dve.wait_ge(dve_order, count[0])
                chain(nc.vector.tensor_reduce(e_own.rearrange("p t e -> p (t e)"),
                                              tmp16.rearrange("p (n g) -> p n g", g=GROUPS), AX_X, ALU.add))
                chain(nc.vector.tensor_reduce(m1, e_own, AX_X, ALU.max))
                chain(one_hot(oh_1, e_own, m1))
                chain(stt(e_rest, oh_1, -3.0e38, e_own, ALU.mult, ALU.add))
                chain(nc.vector.tensor_reduce(m2, e_rest, AX_X, ALU.max))
                vt(ex[:, :, 4], m2, m1, ALU.subtract).then_inc(ex_in, 1)
                chain(one_hot(oh_2, e_rest, m2))
                wait_full(dve, l, "rank")
                rank = ps_of("rank")[:, 0:(TT + 1) * 4].rearrange("p (t n) -> p t n", n=4)
                chain(vt(tie, rank[:, 0:TT, :], oh_g, ALU.mult))
                chain(nc.vector.tensor_reduce(pos, tie, AX_X, ALU.add))
                nc.vector.tensor_reduce(most[:, 0:1], rank[:, TT, :], AX_X, ALU.max).then_inc(taken["dve"], 1)
                wait_taken(dve, l, "rank")
                chain(vs(most[:, 1:2], most[:, 0:1], float(P), 1.0, ALU.is_gt, ALU.add))
                chain(vs(most[:, 2:3], most[:, 0:1], float(2 * P), None, ALU.is_gt))
                chain(vt(most[:, 1:2], most[:, 1:2], most[:, 2:3], ALU.add))
                mark(copy(rounds[0:1, bass.ts(l, 1)], most[0:1, 1:2]))
                chain(copy(low[0:1, 0:1], before[0:1, bass.ts(l, 1)]))
                chain(stt(low[0:1, 1:2], most[0:1, 1:2], float(GROUPS), low[0:1, 0:1], ALU.mult, ALU.add))
                copy(before[0:1, bass.ds(l + 1, 1)], low[0:1, 1:2]).then_inc(routed, 1)

                dve.wait_ge(ex_out, l + 1)
                mark(nc.vector.tensor_reduce(gw, ex[:, :, 0:4], AX_X, ALU.add))
                chain(vs(dn, ex[:, :, 4], 1.0, None, ALU.add))
                chain(vt(dn, dn, gw, ALU.mult))
                chain(nc.vector.reciprocal(v1, dn))
                chain(vt(v2, v1, ex[:, :, 4], ALU.mult))
                mark(vt(cw, oh_1, b4(v1), ALU.mult))
                chain(vt(cw2, oh_2, b4(v2), ALU.mult))
                chain(vt(cw, cw, cw2, ALU.add))
                for j in range(2 * TT):
                    t, half = divmod(j, 2)
                    dve.wait_ge(hrow_hi_done, l * 2 * TT + (j + 1))
                    a, b = half * 512, (half + 1) * 512
                    lower(hrow_lo[:, t, a:b], ps_of("hrow", j), hrow_hi[:, t, a:b]).then_inc(taken["dve"], 1)

                dve.wait_ge(routed, l + 1)
                n = passes(dve, l)
                rewind()

                def make_pick(g):
                    for t in range(TT):
                        m = vs(pick[:, t, :], slot_no, pos[:, t:t + 1], oh_g[:, t, bass.ts(g, 1)],
                               ALU.is_equal, ALU.mult)
                    m.then_inc(pick_ready, 1)

                def gathered(i, half):
                    dve.wait_ge(hg_hi_done, i * 2 + (half + 1))
                    lower(hg_lo[:, 4 * half:4 * half + 4, :], v3(ps[:, 4 + half, :], 4),
                          hg_hi[:, 4 * half:4 * half + 4, :]).then_inc(hg_dve, 1)
                    if half == 1:
                        dve.wait_ge(hg_full, i * 3 + 3)
                        copy(cwg, ps[:, 7, FE:FE + EPG]).then_inc(hg_dve, 1)

                def make_lo_of(i):
                    mbase = dve.snap(splits_before(dve, l, i) + PRE_SPLITS)

                    def lo(m):
                        dve.wait_ge(split_hi, mbase + (m + 1))
                        lower(w_lo[m % MOE_PLACES], slot(pre_slot(m)), w_hi[m % MOE_PLACES]).then_inc(split_lo, 1)

                    return lo

                def group_round(i, g, last):
                    lo = make_lo_of(i)
                    nxt = dve.snap(i + 1)

                    def gated(e):
                        dve.wait_ge(silu_done, i * EPG + (e + 1))
                        if e == 0:
                            dve.wait_ge(hg_dve, i * 3 + 3)
                        if e >= 2:
                            dve.wait_ge(hT_full, i * EPG + (e - 1))
                        stt(hm[:, e % 2, :], hs[:, e % 2, :], cwg[:, e:e + 1], ps[:, 2 + e % 2, FE:2 * FE],
                            ALU.mult, ALU.mult).then_inc(hm_ready, 1)

                    def hT(e):
                        dve.wait_ge(hT_hi_done, i * EPG + (e + 1))
                        lower(hT_lo[:, e % 2, :, :], v3(ps[:, 6 + e % 2, 0:FE], 2), hT_hi[:, e % 2, :, :]
                              ).then_inc(hT_taken, 1)

                    def places(_):
                        if not last:
                            dve.wait_ge(pickT_full, i + 1)
                            make_pick(g_next)

                    def total(half):
                        dve.wait_ge(y_hi_done, i * 2 + (half + 1))
                        a, b = half * 512, (half + 1) * 512
                        lower(y_lo[:, a:b], ps[:, half, :], y_hi[:, a:b]).then_inc(y_dve, 1)

                    if not last:
                        g_next = dve.snap(g + 1)
                    for kind, n in group_steps(last):
                        if kind == "gather":
                            gathered(nxt, n)
                        else:
                            {"split": lo, "places": places, "gate": gated, "turn": hT, "sum": total}[kind](n)
                    for c, bank in enumerate(BACK_BANKS):
                        dve.wait_ge(back_full, i * KD + (c + 1))
                        for st, (a, b) in enumerate(((0, CTX), (CTX, TOK))):
                            m = stt(x[:, c, a:b], ps[:, bank, a:b], mod[:, 40 + c, st:st + 1], x[:, c, a:b],
                                    ALU.mult, ALU.add)
                        m.then_inc(x_moe, 1)
                    dve.wait_ge(x_moe, i * KD + 2 * KD)

                with dve.Fori(0, n) as p:
                    i0 = dve.snap(done + p * GROUPS)
                    make_pick(0)
                    lo = make_lo_of(i0)
                    lo(0)
                    lo(1)
                    gathered(i0, 0)
                    gathered(i0, 1)
                    lo(2)
                    with dve.Fori(0, GROUPS - 1) as g:
                        group_round(dve.snap(i0 + g), g, last=False)
                    group_round(dve.snap(i0 + (GROUPS - 1)), None, last=True)
                    chain(vs(pos, pos, -float(P), None, ALU.add))
                    rewind()


def _fold(w, cols):
    kk, n = w.shape
    return w.reshape(kk // P, P, n // cols, cols).transpose(2, 1, 0, 3).reshape(n // cols, P, kk // P * cols)


def _unit(a):
    out = np.zeros((P, UNIT), np.float32)
    out[:, :a.shape[1]] = a
    return out[None]


def _pre_units(w, l):
    w_in = w["w_in"][l]
    i0, i3 = 2 * DC, 2 * DC + LAT_W
    glu = w_in[:, :i0].reshape(D, 2, KC, P).transpose(0, 2, 1, 3).reshape(D, i0)
    latent = _fold(w_in[:, i0:i3], LAT_W).reshape(P, 2, 4 * LAT_W)
    ukv = w["w_ukv"][l].reshape(KVL, H, NOPE + VD)
    ukv = np.concatenate([ukv[:, :, :NOPE].reshape(KVL, -1), ukv[:, :, NOPE:].reshape(KVL, -1)], axis=1)
    by = {"lat": np.concatenate([_unit(latent[:, n]) for n in range(2)]), "glu": _fold(glu, 256),
          "gate": _fold(w_in[:, i3:], 256), "uq": _unit(_fold(w["w_uq"][l], H * QK)[0]), "ukv": _unit(ukv),
          "pw2": _fold(w["w_pw2"][l], 512), "wo": _fold(w["w_o"][l], 512), "wout": _fold(w["w_out"][l], 256),
          "ada": _fold(w["w_ada"][l], ADA_COLS), "next": _fold(w["w_ada"][(l + 1) % LAYERS], ADA_COLS)}
    return np.stack([by[kind][n] for kind, n in PRE])


def _moe_units(w, l):
    w13 = np.concatenate([w["w1"][l], w["w3"][l]], axis=2)
    up = w13.reshape(EXPERTS, 2, 4, P, 2 * FE).transpose(0, 1, 3, 2, 4).reshape(EXPERTS, 2, P, UNIT)
    down = w["w2"][l].reshape(EXPERTS, 2, P, D).transpose(0, 2, 1, 3).reshape(EXPERTS, P, UNIT)
    return np.stack([np.stack([up[g * EPG + e, half] if kind == "up" else down[g * EPG + e] for kind, e, half in GROUP])
                     for g in range(GROUPS)])


def _columns(a):
    return a.reshape(-1, P).T


def _params(w, l):
    row = lambda a: np.broadcast_to(a.reshape(1, -1), (P, a.size))
    route = np.concatenate([w["w_group"][l], w["w_expert"][l]], axis=1)
    parts = {
        "b_ada": np.concatenate([_columns(w["b_ada"][l])[:, 16:], _columns(w["b_ada"][(l + 1) % LAYERS])[:, :16]], axis=1),
        "norm1": _columns(w["norm1"][l]), "norm2": _columns(w["norm2"][l]),
        "dw": w["conv_dw"][l].reshape(TAPS, KC, P).transpose(2, 1, 0).reshape(P, -1),
        "dw_b": _columns(w["conv_dw_b"][l]), "ln_g": _columns(w["conv_ln_g"][l]), "ln_b": _columns(w["conv_ln_b"][l]),
        "q_lora": _columns(w["q_lora_norm"][l]), "kv_lora": _columns(w["kv_lora_norm"][l]),
        "q_norm": row(w["q_norm"][l]), "k_norm": row(w["k_norm"][l]),
        "route_b": row(np.concatenate([w["b_group"][l], w["b_expert"][l]])),
        "route_w": route.reshape(KD, P, NR).transpose(1, 0, 2).reshape(P, -1),
        "cache_ckv": w["cache_ckv"][0, l].T, "cache_kr": w["cache_krope"][0, l],
    }
    return np.concatenate([parts[n] for n, _ in _FIELDS], axis=1)


def _constants():
    c = np.zeros((P, C_ADA), np.float32)
    c[:, C_ID:C_ID + P] = np.eye(P)
    c[:, C_ONE:C_ONE + P] = 1.0
    c[:, C_TRI:C_TRI + P] = np.triu(np.ones((P, P)), 1)
    c[:, C_SLOT:C_SLOT + P] = np.arange(P)
    for s in range(2):
        c[s::32, C_SEL + s] = 1.0
    freqs = (np.float32(10000.0) ** (-np.arange(NF, dtype=np.float32) / np.float32(NF))).astype(np.float32)
    n = np.arange(LAT)
    ang = np.stack([(n // GRID_W).astype(np.float32)[:, None] * freqs, (n % GRID_W).astype(np.float32)[:, None] * freqs], 1)
    table = np.stack([np.cos(ang), np.sin(ang)], 1).reshape(2, P, 2 * 2 * NF)
    c[:, C_ROPE:C_ROPE + 64] = table.transpose(1, 0, 2).reshape(P, 64)
    c[:, C_ORD:C_ORD + 4] = np.arange(4)
    return c


def kernel(**inputs):
    import concourse.bacc as bacc
    from concourse.bass_utils import run_bass_kernel_spmd

    w = {n: np.asarray(a) for n, a in inputs.items()}
    tokens = np.concatenate([w["x_prompt"][0], w["x_sample"][0]], axis=0)
    arrays = {
        "wfirst": np.ascontiguousarray(_fold(w["w_ada"][0], ADA_COLS)[:ADA_FIRST]),
        "wpre": np.stack([_pre_units(w, l) for l in range(LAYERS)]),
        "wmoe": np.stack([_moe_units(w, l) for l in range(LAYERS)]),
        "x0": np.ascontiguousarray(tokens.reshape(TOK, KD, P).transpose(2, 1, 0)),
        "cond": np.ascontiguousarray(np.stack([_columns(w["c_ctx"]), _columns(w["c"][0])], axis=2)),
        "par_in": np.stack([_params(w, l % LAYERS) for l in range(LAYERS + 1)]),
        "const_in": np.concatenate([_constants(), _columns(w["b_ada"][0])[:, :16]], axis=1),
    }
    nc = bacc.Bacc("TRN2", target_bir_lowering=False, num_devices=1)
    args = [nc.dram_tensor(n, a.shape, F32, kind="ExternalInput").ap() for n, a in arrays.items()]
    outs = [("x_out", (P, KD, TOK)), ("ckv_out", (LAYERS, P, CTX)), ("kr_out", (LAYERS, CTX, ROPE))]
    args += [nc.dram_tensor(n, s, F32, kind="ExternalOutput").ap() for n, s in outs]
    build(nc, *args)
    r = run_bass_kernel_spmd(nc, [arrays], core_ids=[0]).results[0]
    y = r["x_out"].transpose(2, 1, 0).reshape(TOK, D)
    return (y[None, :CTX], y[None, CTX:], r["ckv_out"].transpose(0, 2, 1)[None], r["kr_out"][None])
```
